# Optimizing a Trainium2 kernel written in Bass

```python
import jax
import jax.numpy as jnp
from jax import lax
import numpy as np
import math
import jax, jax.numpy as jnp

D_MODEL = 1024
BATCH = 1
SEQ = 512
DEPTH = 1

GRID_W = 64
HEAD_DIM = 64
NA_HEADS = 8
NA_WIN_H = 8
NA_WIN_W = 16
GQA_HEADS = 8
GQA_KV_HEADS = 2
Q_BLOCK = 128
ROPE_THETA = 10000.0
PEER_HEADS = 8
PEER_NKEYS = 128
PEER_EXPERTS = PEER_NKEYS * PEER_NKEYS
PEER_QDIM = 256
PEER_HALF = PEER_QDIM // 2
PEER_TOPK = 16
PEER_CHUNK = 128
EPS = 1e-6

NA_WIDTH = NA_HEADS * HEAD_DIM
GQA_Q_WIDTH = GQA_HEADS * HEAD_DIM
GQA_KV_WIDTH = GQA_KV_HEADS * HEAD_DIM
IN_SPLITS = (NA_WIDTH, NA_WIDTH, NA_WIDTH, GQA_Q_WIDTH, GQA_KV_WIDTH, GQA_KV_WIDTH, D_MODEL, D_MODEL)
IN_WIDTH = sum(IN_SPLITS)
IN_SPLIT_POINTS = tuple(int(p) for p in np.cumsum(IN_SPLITS)[:-1])


def rmsnorm(x, g):
    xf = x.astype(jnp.float32)
    y = xf * lax.rsqrt(jnp.mean(xf * xf, axis=-1, keepdims=True) + EPS)
    return (y * g.astype(jnp.float32)).astype(x.dtype)

def neighbourhood_attention(q, k, v, rpb):
    b, s, h, dh = q.shape
    rows = s // GRID_W
    kh = min(NA_WIN_H, rows)
    q = q.reshape(b, rows, GRID_W, h, dh)
    k = k.reshape(b, rows, GRID_W, h, dh)
    v = v.reshape(b, rows, GRID_W, h, dh)
    r = jnp.arange(rows)
    row_start = jnp.clip(r - kh // 2, 0, rows - kh)
    key_rows = row_start[:, None] + jnp.arange(kh)[None, :]
    k_g = k[:, key_rows]
    v_g = v[:, key_rows]
    c = jnp.arange(GRID_W)
    col_start = jnp.clip(c - NA_WIN_W // 2, 0, GRID_W - NA_WIN_W)
    in_win = (c[None, :] >= col_start[:, None]) & (c[None, :] < col_start[:, None] + NA_WIN_W)
    dr = key_rows - r[:, None] + (NA_WIN_H - 1)
    dc = jnp.clip(c[None, :] - c[:, None], -(NA_WIN_W - 1), NA_WIN_W - 1) + (NA_WIN_W - 1)
    bias = rpb[:, dr[:, None, :, None], dc[None, :, None, :]].astype(jnp.float32)
    scores = jnp.einsum("brqhd,brkwhd->bhrqkw", q, k_g).astype(jnp.float32) * (dh ** -0.5) + bias[None]
    scores = jnp.where(in_win[:, None, :], scores, -jnp.inf)
    probs = jax.nn.softmax(scores.reshape(b, h, rows, GRID_W, kh * GRID_W), axis=-1)
    probs = probs.reshape(b, h, rows, GRID_W, kh, GRID_W).astype(v.dtype)
    out = jnp.einsum("bhrqkw,brkwhd->brqhd", probs, v_g)
    return out.reshape(b, s, h * dh)

def _rotate(x, ang):
    half = x.shape[-1] // 2
    x1, x2 = x[..., :half], x[..., half:]
    cos = jnp.cos(ang)[None, :, None, :]
    sin = jnp.sin(ang)[None, :, None, :]
    return jnp.concatenate([x1 * cos - x2 * sin, x2 * cos + x1 * sin], axis=-1)

def axial_rope(x):
    b, s, h, dh = x.shape
    sec = dh // 2
    nf = sec // 2
    t = jnp.arange(s)
    inv = ROPE_THETA ** (-jnp.arange(nf, dtype=jnp.float32) / nf)
    ang_r = (t // GRID_W).astype(jnp.float32)[:, None] * inv[None, :]
    ang_c = (t % GRID_W).astype(jnp.float32)[:, None] * inv[None, :]
    xf = x.astype(jnp.float32)
    out = jnp.concatenate([_rotate(xf[..., :sec], ang_r), _rotate(xf[..., sec:], ang_c)], axis=-1)
    return out.astype(x.dtype)

def gqa_attention(q, k, v):
    b, s, h, dh = q.shape
    hkv = k.shape[2]
    grp = h // hkv
    nblk = s // Q_BLOCK
    qb = q.reshape(b, nblk, Q_BLOCK, hkv, grp, dh).transpose(1, 0, 2, 3, 4, 5)
    scale = dh ** -0.5

    def block(qblk):
        sc = jnp.einsum("bqngd,bknd->bngqk", qblk, k).astype(jnp.float32) * scale
        p = jax.nn.softmax(sc, axis=-1).astype(v.dtype)
        return jnp.einsum("bngqk,bknd->bqngd", p, v)

    out = lax.map(block, qb)
    return out.transpose(1, 0, 2, 3, 4, 5).reshape(b, s, h * dh)

def peer(xn, w_q, sub_keys, u, v):
    b, s, d = xn.shape
    t = b * s
    xt = xn.reshape(t, d)
    q = (xt @ w_q).reshape(t, PEER_HEADS, 2, PEER_HALF)
    sc = jnp.einsum("thpc,hpnc->thpn", q, sub_keys).astype(jnp.float32)
    top_s, top_i = lax.top_k(sc, PEER_TOPK)
    cand_s = (top_s[:, :, 0, :, None] + top_s[:, :, 1, None, :]).reshape(t, PEER_HEADS, PEER_TOPK * PEER_TOPK)
    cand_i = (top_i[:, :, 0, :, None] * PEER_NKEYS + top_i[:, :, 1, None, :]).reshape(t, PEER_HEADS, PEER_TOPK * PEER_TOPK)
    best_s, best_pos = lax.top_k(cand_s, PEER_TOPK)
    idx = jnp.take_along_axis(cand_i, best_pos, axis=-1)
    gate = jax.nn.softmax(best_s, axis=-1)
    nchunk = t // PEER_CHUNK
    x_c = xt.reshape(nchunk, PEER_CHUNK, d)
    i_c = idx.reshape(nchunk, PEER_CHUNK, PEER_HEADS * PEER_TOPK)
    g_c = gate.reshape(nchunk, PEER_CHUNK, PEER_HEADS * PEER_TOPK)

    def chunk(args):
        xc, ic, gc = args
        uc = u[ic]
        act = jnp.einsum("cd,ced->ce", xc, uc).astype(jnp.float32)
        hid = (jax.nn.gelu(act, approximate=False) * gc).astype(xc.dtype)
        return jnp.einsum("ce,ced->cd", hid, v[ic])

    out = lax.map(chunk, (x_c, i_c, g_c))
    return out.reshape(b, s, d)

def first_inputs(seed: int = 0) -> dict:
    key = jax.random.key(seed)
    ks = jax.random.split(key, 16)
    f32 = jnp.float32
    nrm = lambda k, shape, scale: jax.random.normal(k, shape, f32) * scale
    return {
        "x": nrm(ks[0], (BATCH, SEQ, D_MODEL), 1.0),
        "norm1_g": 1.0 + nrm(ks[1], (DEPTH, D_MODEL), 0.1),
        "w_in": nrm(ks[2], (DEPTH, D_MODEL, IN_WIDTH), D_MODEL ** -0.5),
        "na_rpb": nrm(ks[3], (DEPTH, NA_HEADS, 2 * NA_WIN_H - 1, 2 * NA_WIN_W - 1), 0.5),
        "gqa_q_norm_g": 1.0 + nrm(ks[4], (DEPTH, HEAD_DIM), 0.1),
        "gqa_k_norm_g": 1.0 + nrm(ks[5], (DEPTH, HEAD_DIM), 0.1),
        "w_proj_a": nrm(ks[6], (DEPTH, NA_WIDTH, D_MODEL), NA_WIDTH ** -0.5),
        "w_proj_b": nrm(ks[7], (DEPTH, GQA_Q_WIDTH, D_MODEL), GQA_Q_WIDTH ** -0.5),
        "w_out": nrm(ks[8], (DEPTH, D_MODEL, D_MODEL), D_MODEL ** -0.5),
        "norm2_g": 1.0 + nrm(ks[9], (DEPTH, D_MODEL), 0.1),
        "peer_w_q": nrm(ks[10], (DEPTH, D_MODEL, PEER_HEADS * PEER_QDIM), D_MODEL ** -0.5),
        "peer_sub_keys": nrm(ks[11], (DEPTH, PEER_HEADS, 2, PEER_NKEYS, PEER_HALF), PEER_HALF ** -0.5),
        "peer_u": nrm(ks[12], (DEPTH, PEER_EXPERTS, D_MODEL), D_MODEL ** -0.5),
        "peer_v": nrm(ks[13], (DEPTH, PEER_EXPERTS, D_MODEL), PEER_HEADS ** -0.5),
        "norm_f_g": 1.0 + nrm(ks[14], (D_MODEL,), 0.1),
    }

def first_block(x, norm1_g, w_in, na_rpb, gqa_q_norm_g, gqa_k_norm_g, w_proj_a, w_proj_b, w_out,
              norm2_g, peer_w_q, peer_sub_keys, peer_u, peer_v, norm_f_g):
    b, s, _ = x.shape
    for l in range(DEPTH):
        h = rmsnorm(x, norm1_g[l])
        proj = h @ w_in[l]
        qa, ka, va, qb, kb, vb, ga, gb = jnp.split(proj, IN_SPLIT_POINTS, axis=-1)
        ya = neighbourhood_attention(
            qa.reshape(b, s, NA_HEADS, HEAD_DIM),
            ka.reshape(b, s, NA_HEADS, HEAD_DIM),
            va.reshape(b, s, NA_HEADS, HEAD_DIM),
            na_rpb[l])
        qh = axial_rope(rmsnorm(qb.reshape(b, s, GQA_HEADS, HEAD_DIM), gqa_q_norm_g[l]))
        kh = axial_rope(rmsnorm(kb.reshape(b, s, GQA_KV_HEADS, HEAD_DIM), gqa_k_norm_g[l]))
        yb = gqa_attention(qh, kh, vb.reshape(b, s, GQA_KV_HEADS, HEAD_DIM))
        merged = jax.nn.sigmoid(ga) * (ya @ w_proj_a[l]) + jax.nn.sigmoid(gb) * (yb @ w_proj_b[l])
        x = x + merged @ w_out[l]
        x = x + peer(rmsnorm(x, norm2_g[l]), peer_w_q[l], peer_sub_keys[l], peer_u[l], peer_v[l])
    return rmsnorm(x, norm_f_g)


PLE_DIM = 256
D_MIX_SSD = D_MODEL
D_MIX_CONV = D_MODEL
D_MIX = D_MIX_SSD + D_MIX_CONV
SSD_HEAD_DIM = 64
SSD_HEADS = D_MIX_SSD // SSD_HEAD_DIM
SSD_GROUPS = 2
HEADS_PER_GROUP = SSD_HEADS // SSD_GROUPS
D_STATE = 64
SSD_CONV_W = 4
CHUNK = 128
SSD_CONV_DIM = D_MIX_SSD + 2 * SSD_GROUPS * D_STATE
SC_CONV_W = 3
IN_SPLITS_2 = [SSD_CONV_DIM, SSD_HEADS, D_MIX_SSD, D_MIX_CONV, D_MIX_CONV, D_MIX_CONV, D_MIX_CONV]
IN_COLS = sum(IN_SPLITS_2)


def rmsnorm_2(x, w):
    xf = x.astype(jnp.float32)
    xf = xf * lax.rsqrt(jnp.mean(xf * xf, axis=-1, keepdims=True) + EPS)
    return (xf * w.astype(jnp.float32)).astype(x.dtype)

def causal_dwconv(u, w, b=None):
    k_w = w.shape[0]
    length = u.shape[1]
    up = jnp.pad(u, ((0, 0), (k_w - 1, 0), (0, 0)))
    y = up[:, 0:length] * w[0]
    for k in range(1, k_w):
        y = y + up[:, k:k + length] * w[k]
    if b is not None:
        y = y + b
    return y

def segsum(a):
    t = a.shape[-1]
    cs = jnp.cumsum(a, axis=-1)
    diff = cs[..., :, None] - cs[..., None, :]
    mask = jnp.tril(jnp.ones((t, t), dtype=bool))
    return jnp.where(mask, diff, -jnp.inf)

def ssd_chunked(x, dt, a, b_mat, c_mat, d_skip):
    bsz, length, _, _ = x.shape
    nc = length // CHUNK
    g, r, p, n = SSD_GROUPS, HEADS_PER_GROUP, SSD_HEAD_DIM, D_STATE
    xd = (x * dt[..., None]).reshape(bsz, nc, CHUNK, g, r, p)
    bc = b_mat.reshape(bsz, nc, CHUNK, g, n)
    cc = c_mat.reshape(bsz, nc, CHUNK, g, n)
    adt = (dt * a).reshape(bsz, nc, CHUNK, g, r).transpose(0, 3, 4, 1, 2)
    a_cs = jnp.cumsum(adt, axis=-1)
    decay_in = jnp.exp(segsum(adt))
    cb = jnp.einsum("bclgn,bcsgn->bgcls", cc, bc)
    y_diag = jnp.einsum("bgrcls,bcsgrp->bclgrp", cb[:, :, None] * decay_in, xd)
    decay_states = jnp.exp(a_cs[..., -1:] - a_cs).transpose(0, 3, 4, 1, 2)
    states = jnp.einsum("bclgn,bclgrp->bcgrpn", bc, xd * decay_states[..., None])
    init = jnp.zeros_like(states[:, :1])
    states = jnp.concatenate([init, states], axis=1)
    totals = jnp.pad(a_cs[..., -1], ((0, 0), (0, 0), (0, 0), (1, 0)))
    decay_chunk = jnp.exp(segsum(totals))
    new_states = jnp.einsum("bgrzc,bcgrpn->bzgrpn", decay_chunk, states)
    prev_states = new_states[:, :-1]
    decay_out = jnp.exp(a_cs).transpose(0, 3, 4, 1, 2)
    y_off = jnp.einsum("bclgn,bcgrpn->bclgrp", cc, prev_states) * decay_out[..., None]
    y = (y_diag + y_off).reshape(bsz, length, SSD_HEADS, p)
    return y + d_skip[:, None] * x

def hybrid_layer(x, p_i, norm_pre, norm_post, w_in, ssd_conv_w, ssd_conv_b, dt_bias,
                 a_log, d_skip, ssd_norm, sc_conv_w, w_out, w_ple_gate, w_ple_proj):
    bsz, length, _ = x.shape
    h = rmsnorm_2(x, norm_pre)
    proj = h @ w_in
    idx = list(np.cumsum(IN_SPLITS_2)[:-1])
    xbc, dt_raw, z_ssd, sc_h, sc_b, sc_c, z_sc = jnp.split(proj, idx, axis=-1)

    xbc = jax.nn.silu(causal_dwconv(xbc, ssd_conv_w, ssd_conv_b))
    xs, bm, cm = jnp.split(xbc, [D_MIX_SSD, D_MIX_SSD + SSD_GROUPS * D_STATE], axis=-1)
    xs = xs.reshape(bsz, length, SSD_HEADS, SSD_HEAD_DIM)
    bm = bm.reshape(bsz, length, SSD_GROUPS, D_STATE)
    cm = cm.reshape(bsz, length, SSD_GROUPS, D_STATE)
    dt = jax.nn.softplus(dt_raw + dt_bias)
    a = -jnp.exp(a_log)
    y_ssd = ssd_chunked(xs, dt, a, bm, cm, d_skip).reshape(bsz, length, D_MIX_SSD)
    yz = (y_ssd * jax.nn.silu(z_ssd)).reshape(bsz, length, SSD_GROUPS, D_MIX_SSD // SSD_GROUPS)
    y_ssd = rmsnorm_2(yz, ssd_norm.reshape(SSD_GROUPS, -1)).reshape(bsz, length, D_MIX_SSD)

    v = causal_dwconv(sc_c * sc_h, sc_conv_w)
    y_sc = sc_b * v * jax.nn.silu(z_sc)

    mix = jnp.concatenate([y_ssd, y_sc], axis=-1) @ w_out
    x = x + rmsnorm_2(mix, norm_post)

    gate = jax.nn.sigmoid(x @ w_ple_gate)
    return x + gate * (p_i @ w_ple_proj)

def second_inputs(seed: int = 0) -> dict:
    key = jax.random.key(seed)
    ks = jax.random.split(key, 16)
    f32 = jnp.float32
    x = jax.random.normal(ks[0], (BATCH, SEQ, D_MODEL), f32)
    p = jax.random.normal(ks[1], (DEPTH, BATCH, SEQ, PLE_DIM), f32)
    norm_pre = 1.0 + 0.05 * jax.random.normal(ks[2], (DEPTH, D_MODEL), f32)
    norm_post = 1.0 + 0.05 * jax.random.normal(ks[3], (DEPTH, D_MODEL), f32)
    w_in = jax.random.normal(ks[4], (DEPTH, D_MODEL, IN_COLS), f32) * D_MODEL ** -0.5
    ssd_conv_w = jax.random.normal(ks[5], (DEPTH, SSD_CONV_W, SSD_CONV_DIM), f32) * SSD_CONV_W ** -0.5
    ssd_conv_b = 0.02 * jax.random.normal(ks[6], (DEPTH, SSD_CONV_DIM), f32)
    dt0 = jnp.exp(jax.random.uniform(ks[7], (DEPTH, SSD_HEADS), f32,
                                     math.log(1e-3), math.log(1e-1)))
    dt_bias = dt0 + jnp.log(-jnp.expm1(-dt0))
    a_log = jnp.log(jax.random.uniform(ks[8], (DEPTH, SSD_HEADS), f32, 1.0, 16.0))
    d_skip = 1.0 + 0.05 * jax.random.normal(ks[9], (DEPTH, SSD_HEADS), f32)
    ssd_norm = 1.0 + 0.05 * jax.random.normal(ks[10], (DEPTH, D_MIX_SSD), f32)
    sc_conv_w = jax.random.normal(ks[11], (DEPTH, SC_CONV_W, D_MIX_CONV), f32) * SC_CONV_W ** -0.5
    w_out = jax.random.normal(ks[12], (DEPTH, D_MIX, D_MODEL), f32) * D_MIX ** -0.5
    w_ple_gate = jax.random.normal(ks[13], (DEPTH, D_MODEL, D_MODEL), f32) * D_MODEL ** -0.5
    w_ple_proj = jax.random.normal(ks[14], (DEPTH, PLE_DIM, D_MODEL), f32) * (0.5 * PLE_DIM ** -0.5)
    return {"x": x, "p": p, "norm_pre": norm_pre, "norm_post": norm_post, "w_in": w_in,
            "ssd_conv_w": ssd_conv_w, "ssd_conv_b": ssd_conv_b, "dt_bias": dt_bias,
            "a_log": a_log, "d_skip": d_skip, "ssd_norm": ssd_norm, "sc_conv_w": sc_conv_w,
            "w_out": w_out, "w_ple_gate": w_ple_gate, "w_ple_proj": w_ple_proj}

def second_block(x, p, norm_pre, norm_post, w_in, ssd_conv_w, ssd_conv_b, dt_bias, a_log,
              d_skip, ssd_norm, sc_conv_w, w_out, w_ple_gate, w_ple_proj):
    for i in range(DEPTH):
        x = hybrid_layer(x, p[i], norm_pre[i], norm_post[i], w_in[i], ssd_conv_w[i],
                         ssd_conv_b[i], dt_bias[i], a_log[i], d_skip[i], ssd_norm[i],
                         sc_conv_w[i], w_out[i], w_ple_gate[i], w_ple_proj[i])
    return x


def setup_inputs(seed=0):
    out = dict(first_inputs(seed))
    for name, value in second_inputs(seed + 1).items():
        if name != "x":
            out[name + "_2"] = value
    return out


def reference(
    x, norm1_g, w_in, na_rpb, gqa_q_norm_g, gqa_k_norm_g, w_proj_a, w_proj_b, w_out, norm2_g,
    peer_w_q, peer_sub_keys, peer_u, peer_v, norm_f_g, p_2, norm_pre_2, norm_post_2, w_in_2,
    ssd_conv_w_2, ssd_conv_b_2, dt_bias_2, a_log_2, d_skip_2, ssd_norm_2, sc_conv_w_2, w_out_2,
    w_ple_gate_2, w_ple_proj_2,
):
    x = first_block(
        x, norm1_g, w_in, na_rpb, gqa_q_norm_g, gqa_k_norm_g, w_proj_a, w_proj_b, w_out,
        norm2_g, peer_w_q, peer_sub_keys, peer_u, peer_v, norm_f_g,
    )
    return second_block(
        x, p_2, norm_pre_2, norm_post_2, w_in_2, ssd_conv_w_2, ssd_conv_b_2, dt_bias_2, a_log_2,
        d_skip_2, ssd_norm_2, sc_conv_w_2, w_out_2, w_ple_gate_2, w_ple_proj_2,
    )


_drawn_inputs = setup_inputs


def setup_inputs(seed=0):
    import zlib

    import numpy as np

    out = dict(_drawn_inputs(seed))
    spreads = {}
    factors = {'gqa_q_norm_g': 3.447, 'gqa_k_norm_g': 3.252, 'ssd_conv_b_2': 3.496, 'd_skip_2': 2.843}
    for name, (base, spread) in spreads.items():
        noise = np.random.default_rng([zlib.crc32(name.encode()), seed]).standard_normal(out[name].shape)
        drawn = base * np.exp(spread * noise) if base else spread * noise
        out[name] = jnp.asarray(drawn.astype(out[name].dtype))
    for name, factor in factors.items():
        out[name] = (out[name] * factor).astype(out[name].dtype)
    return out
```

```python
from contextlib import ExitStack

import numpy as np

import concourse.bass as bass
from concourse import mybir

F32 = mybir.dt.float32
U32 = mybir.dt.uint32
ALU = mybir.AluOpType
ACT = mybir.ActivationFunctionType
AX = mybir.AxisListType.X

P = 128
SEQ = 512
TT = SEQ // P
D = 1024
KT = D // P
EPS = 1e-6
GRID_W = 64
DH = 64
HEADS = 8
WIN_H, WIN_W = 8, 16
ATT_W = HEADS * DH
KV_HEADS = 2
BIAS_ROWS = 2 * WIN_H
ROPE_THETA = 10000.0

PK = 128
PH = 8
TOPK = 16
EXPERTS = PK * PK
SLOTS = PH * TOPK
EG = 4
NG = PK // EG

SH = 16
SP_ = 64
SG = 2
HG = SH // SG
NS = 64
CONV_W, SC_W = 4, 3
XBC_TILES = (D + 2 * SG * NS) // P
PLE = 256

NEG = -1.0e30
LOWEST = -3.4028235e38

WBLK = 4096
RING = 3
B_QA, B_KA, B_VA, B_QB, B_KVB = range(5)
B_MERGE = 5
B_OUT = B_MERGE + KT
B_PQ = B_OUT + 2
B_KEYS = B_PQ + 4
B_XBC = B_KEYS + 1
B_DT = B_XBC + 3
B_Z = B_DT + 1
B_SC = B_Z + 2
B_MIX = B_SC + KT
B_PLE = B_MIX + 4
B_GATE = B_PLE + 1
NB = B_GATE + 2

C_G1, C_G2, C_GPRE = 0, KT, 2 * KT
C_CW = 3 * KT
C_CB = C_CW + XBC_TILES * CONV_W
C_SW = C_CB + XBC_TILES
NCOL = C_SW + KT * SC_W
T_ID, T_TRI, T_IOTA, T_COS = 0, P, 2 * P, 3 * P
T_SIN = T_COS + TT * DH
NTAB = T_SIN + TT * DH
R_GQK = 0
R_DTB = R_GQK + ATT_W + KV_HEADS * DH
R_ALOG = R_DTB + SH
R_DSK = R_ALOG + SH
NROW = R_DSK + SH


def bc(ap, n):
    return ap.unsqueeze(len(ap.shape)).broadcast_to(list(ap.shape) + [n])


def mid(ap, n):
    return ap.unsqueeze(1).broadcast_to([ap.shape[0], n, ap.shape[1]])


class Core:

    def __init__(self, nc, ctx, t):
        self.nc, self.t = nc, t
        sb = lambda name, shape, dt=F32: ctx.enter_context(nc.sbuf_tensor(name, shape, dt))
        self.X = sb("x_res", [P, TT, D])
        self.XT = sb("XT", [P, KT, SEQ])
        self.W = sb("W", [P, RING, WBLK])
        self.tab = sb("tab_sb", [P, NTAB])
        self.cols = sb("cols_sb", [P, NCOL])
        self.rows = sb("rows_sb", [P, NROW])
        self.ss = sb("ss", [P, TT])
        self.ms = sb("ms", [P, TT])
        self.rn = sb("rn", [P, TT])
        self.half = sb("half", [P, 48])
        self.bank = [ctx.enter_context(nc.psum_tensor(f"bank{i}", [P, 512], F32)) for i in range(8)]
        self.w_loaded = [ctx.enter_context(nc.semaphore(f"w_loaded{i}")) for i in range(RING)]
        self.ident = self.tab[:, T_ID:T_ID + P]
        self.tri = self.tab[:, T_TRI:T_TRI + P]
        self.iota = self.tab[:, T_IOTA:T_IOTA + P]

    def w(self, b, n, cols=P):
        return self.W[:, b % RING, 0:n].rearrange("p (k c) -> p k c", c=cols)

    def load_w(self, sp, b):
        sp.dma_start(self.W[:, b % RING, :], self.t["w_stream"][b]).then_inc(self.w_loaded[b % RING], 16)

    def wait_w(self, pe, b):
        pe.wait_ge(self.w_loaded[b % RING], 16 * (b // RING + 1))


def signals(nc, ctx, names):
    return [ctx.enter_context(nc.semaphore(n)) for n in names.split()]



def norm_sums(act, c, src, junk, squared):
    for tt in range(TT):
        act.activation(junk[:, tt], src[:, tt], ACT.Square, accum_out=c.ss[:, tt:tt + 1]).then_inc(squared, 1)


def norm_rsqrt(pool, c, squared, at, meaned, rooted):
    pool.wait_ge(squared, at)
    pool.tensor_scalar(c.ms[:], c.ss[:], 1.0 / D, EPS, ALU.mult, ALU.add).then_inc(meaned, 1)
    pool.wait_ge(meaned, at // TT)
    pool.tensor_tensor(c.rn[:], c.ms[:], c.half[:, 0:TT], ALU.pow).then_inc(rooted, 1)


def transposes_pe(pe, c, src, scaled, at, turned, out_act, out_dve):
    pe.wait_ge(scaled, at)
    for kt in range(KT):
        if kt >= 4:
            pe.wait_ge(out_dve if kt % 2 else out_act, kt // 2 - 1)
        for tt in range(TT):
            mm = pe.transpose(c.bank[kt % 4][:, tt * P:(tt + 1) * P], src[:, tt, kt * P:(kt + 1) * P], c.ident)
        mm.then_inc(turned, 1)


def gains_act(act, c, col, turned, out_act):
    for kt in range(0, KT, 2):
        act.wait_ge(turned, kt + 1)
        act.activation(c.XT[:, kt], c.bank[kt % 4][:], ACT.Copy, scale=1.0 if col is None else c.cols[:, col + kt:col + kt + 1]).then_inc(out_act, 1)


def gains_dve(dve, c, col, turned, out_dve):
    for kt in range(1, KT, 2):
        dve.wait_ge(turned, kt + 1)
        gain = 1.0 if col is None else c.cols[:, col + kt:col + kt + 1]
        dve.tensor_scalar(c.XT[:, kt], c.bank[kt % 4][:], gain, None, ALU.mult).then_inc(out_dve, 1)


def phase_project(c, a):
    nc, t = c.nc, c.t
    with ExitStack() as ctx:
        HN = ctx.enter_context(nc.sbuf_tensor("HN", [P, TT, D], F32))
        QK = ctx.enter_context(nc.sbuf_tensor("QK", [P, TT, ATT_W + P], F32))
        S1 = ctx.enter_context(nc.sbuf_tensor("S1", [P, TT, ATT_W + P], F32))
        S2 = ctx.enter_context(nc.sbuf_tensor("S2", [P, TT, ATT_W + P], F32))
        KR = ctx.enter_context(nc.sbuf_tensor("KR", [P, TT, P], F32))
        hs = ctx.enter_context(nc.sbuf_tensor("hs", [P, 3, 40], F32))
        (x0, x1, x2, x3, tab_in, col_in, row_in, squared, meaned, rooted, scaled, turned, out_a, out_d, grp, grp_a, grp_d,
         set0, step, hsum, hroot, roped, rturn, rout) = signals(
            nc, ctx, "x_in0 x_in1 x_in2 x_in3 tab_in col_in row_in squared meaned rooted scaled turned out_a out_d grp grp_a grp_d "
            "set0 step hsum hroot roped rturn rout")
        x_in = (x0, x1, x2, x3)
        qpad = HN[:].rearrange("p t (h w) -> p t h w", w=P)
        block = ctx.enter_context(nc.Block())
        GROUPS = 2 * TT + 3 * TT
        HR = HEADS + KV_HEADS

        def project_out(g, copy, sem):
            src = c.bank[4 + g % 4]
            if g < 4:
                copy(a.qz[0:64, 2 * g], src[0:64, :], DH ** -0.5)
                copy(a.qz[64:128, 2 * g + 1], src[64:128, :], DH ** -0.5).then_inc(sem, 1)
            elif g < 8:
                copy(a.kT[:, g - 4], src[:], 1.0).then_inc(sem, 1)
            elif g < 12:
                copy(a.va[:, g - 8], src[:], 1.0).then_inc(sem, 1)
            elif g < 16:
                copy(QK[:, g - 12, 0:ATT_W], src[:], 1.0).then_inc(sem, 1)
            else:
                copy(QK[:, g - 16, ATT_W:], src[:, 0:P], 1.0)
                copy(a.vb[:, g - 16], src[:, P:2 * P], 1.0).then_inc(sem, 1)

        @block.sync
        def _(sp):
            for tt in range(TT):
                sp.dma_start(c.X[:, tt], t["x"][tt * P:(tt + 1) * P, :]).then_inc(x_in[tt], 16)
            sp.dma_start(c.tab[:], t["tab"]).then_inc(tab_in, 16)
            sp.dma_start(c.cols[:], t["cols"]).then_inc(col_in, 16)
            for b in range(RING):
                c.load_w(sp, b)
            sp.dma_start(c.rows[:], t["rows"]).then_inc(row_in, 16)
            for b in range(5):
                sp.wait_ge(grp, 4 * (b + 1))
                c.load_w(sp, b + RING)

        @block.scalar
        def _(act):
            for tt in range(TT):
                act.wait_ge(x_in[tt], 16)
                act.activation(HN[:, tt], c.X[:, tt], ACT.Square, accum_out=c.ss[:, tt:tt + 1]).then_inc(squared, 1)
            act.wait_ge(col_in, 16)
            gains_act(act, c, C_G1, turned, out_a)
            for g in range(0, GROUPS, 2):
                act.wait_ge(grp, g + 1)
                if g == 0:
                    act.wait_ge(set0, 2)
                project_out(g, lambda o, i, s: act.activation(o, i, ACT.Copy, scale=s), grp_a)
            for h in range(0, HEADS, 2):
                act.wait_ge(rturn, h + 1)
                act.activation(a.qzb[:, h], c.bank[h % 4][:], ACT.Copy, scale=DH ** -0.5).then_inc(rout, 1)
            act.wait_ge(rturn, HEADS + 1)
            act.activation(a.kTb[:], c.bank[HEADS % 4][:], ACT.Copy).then_inc(rout, 1)

        @block.gpsimd
        def _(pool):
            pool.memset(c.half[:], -0.5).then_inc(set0, 1)
            pool.memset(a.qz[:], 0.0).then_inc(set0, 1)
            pool.wait_ge(set0, 2)
            norm_rsqrt(pool, c, squared, TT, meaned, rooted)
            pool.wait_ge(turned, KT)
            pool.memset(HN[:], 0.0).then_inc(set0, 1)
            pool.wait_ge(hsum, 1)
            pool.tensor_scalar(hs[:, 1], hs[:, 0], 1.0 / DH, EPS, ALU.mult, ALU.add).then_inc(meaned, 1)
            pool.wait_ge(meaned, 2)
            pool.tensor_tensor(hs[:, 2], hs[:, 1], c.half[:, 0:40], ALU.pow).then_inc(hroot, 1)

        @block.vector
        def _(dve):
            dve.wait_ge(rooted, 1)
            for tt in range(TT):
                dve.wait_ge(x_in[tt], 16)
                dve.tensor_scalar(HN[:, tt], c.X[:, tt], c.rn[:, tt:tt + 1], None, ALU.mult).then_inc(scaled, 1)
            dve.wait_ge(col_in, 16)
            gains_dve(dve, c, C_G1, turned, out_d)
            dve.wait_ge(set0, 2)
            for g in range(1, GROUPS, 2):
                dve.wait_ge(grp, g + 1)
                project_out(g, lambda o, i, s: dve.tensor_scalar(o, i, s, None, ALU.mult), grp_d)
            n = [0]

            def link(ins):
                n[0] += 1
                ins.then_inc(step, 1)
                dve.wait_ge(step, n[0])

            dve.wait_ge(grp_a, GROUPS // 2)
            dve.wait_ge(grp_d, GROUPS // 2)
            flat = lambda x: x[:].rearrange("p t w -> p (t w)")
            heads = lambda x: x[:].rearrange("p t (h w) -> p (t h) w", w=DH)
            link(dve.tensor_tensor(flat(S1), flat(QK), flat(QK), ALU.mult))
            dve.tensor_reduce(hs[:, 0], heads(S1), AX, ALU.add).then_inc(hsum, 1)
            dve.wait_ge(hroot, 1)
            link(dve.tensor_tensor(heads(S1), heads(QK), bc(hs[:, 2], DH), ALU.mult))
            dve.wait_ge(row_in, 16)
            link(dve.tensor_tensor(QK[:], S1[:], mid(c.rows[:, R_GQK:R_GQK + ATT_W + P], TT), ALU.mult))
            for tt in range(TT):
                cos = mid(c.tab[:, T_COS + tt * DH:T_COS + (tt + 1) * DH], HR)
                dve.tensor_tensor(S1[:, tt].rearrange("p (h w) -> p h w", w=DH), QK[:, tt].rearrange("p (h w) -> p h w", w=DH), cos, ALU.mult)
                halves = lambda x: x.rearrange("p (h s f w) -> p h s f w", s=2, f=2, w=DH // 4)
                sin = c.tab[:, T_SIN + tt * DH:T_SIN + (tt + 1) * DH].rearrange("p (s f w) -> p s f w", s=2, f=2)
                for f in range(2):
                    s_f = sin[:, :, f].unsqueeze(1).broadcast_to([P, HR, 2, DH // 4])
                    last = dve.tensor_tensor(halves(S2[:, tt])[:, :, :, f], halves(QK[:, tt])[:, :, :, 1 - f], s_f, ALU.mult)
            link(last)
            dve.wait_ge(set0, 3)
            for tt in range(TT):
                for n0 in range(KV_HEADS):
                    o = qpad[:, tt, 4 * n0:4 * n0 + 4, 64 * n0:64 * n0 + 64]
                    cut = slice(256 * n0, 256 * n0 + 256)
                    dve.tensor_tensor(o, S1[:, tt, cut].rearrange("p (h w) -> p h w", w=DH),
                                      S2[:, tt, cut].rearrange("p (h w) -> p h w", w=DH), ALU.add)
                last = dve.tensor_tensor(KR[:, tt], S1[:, tt, ATT_W:], S2[:, tt, ATT_W:], ALU.add)
            last.then_inc(roped, 1)
            for h in range(1, HEADS, 2):
                dve.wait_ge(rturn, h + 1)
                dve.tensor_scalar(a.qzb[:, h], c.bank[h % 4][:], DH ** -0.5, None, ALU.mult).then_inc(out_d, 1)

        @block.tensor
        def _(pe):
            pe.wait_ge(tab_in, 16)
            transposes_pe(pe, c, HN, scaled, TT, turned, out_a, out_d)
            pe.wait_ge(out_a, KT // 2)
            pe.wait_ge(out_d, KT // 2)
            for g in range(GROUPS):
                ps = c.bank[4 + g % 4]
                if g % 4 == 0:
                    c.wait_w(pe, g // 4)
                if g >= 4:
                    pe.wait_ge(grp_d if g % 2 else grp_a, g // 2 - 1)
                if g < 8:
                    w = c.w(g // 4, KT * 512, 512)
                    for k in range(KT):
                        mm = pe.matmul(ps[:], w[:, k, (g % 4) * P:(g % 4 + 1) * P], c.XT[:, k], start=k == 0, stop=k == KT - 1)
                else:
                    width = 512 if g < 16 else 256
                    w, tt = c.w(g // 4, KT * width, width), g % 4
                    for k in range(KT):
                        mm = pe.matmul(ps[:, 0:width], c.XT[:, k, tt * P:(tt + 1) * P], w[:, k], start=k == 0, stop=k == KT - 1)
                mm.then_inc(grp, 1)
            pe.wait_ge(roped, 1)
            for h in range(HEADS + 1):
                if h >= 4:
                    pe.wait_ge(out_d if h % 2 else rout, (h // 2 - 1) + (KT // 2 if h % 2 else 0))
                for tt in range(TT):
                    src = qpad[:, tt, h] if h < HEADS else KR[:, tt]
                    mm = pe.transpose(c.bank[h % 4][:, tt * P:(tt + 1) * P], src, c.ident)
                mm.then_inc(rturn, 1)


def phase_attend(c, a):
    nc, t = c.nc, c.t
    UNITS = 2 * HEADS * TT
    PR = 4
    with ExitStack() as ctx:
        Pr = ctx.enter_context(nc.sbuf_tensor("Pr", [P, PR, SEQ], F32))
        PT = ctx.enter_context(nc.sbuf_tensor("PT", [P, PR, TT, P], F32))
        bias = ctx.enter_context(nc.sbuf_tensor("bias_sb", [P, 2, BIAS_ROWS * GRID_W], F32))
        mx = ctx.enter_context(nc.sbuf_tensor("mx", [P, UNITS], F32))
        nm = ctx.enter_context(nc.sbuf_tensor("nm", [P, UNITS], F32))
        rs = ctx.enter_context(nc.sbuf_tensor("rs", [P, UNITS], F32))
        ri = ctx.enter_context(nc.sbuf_tensor("ri", [P, UNITS], F32))
        scored, maxed, negated, expd, turned, pt_a, pt_d, weighed, inverted, y_out, b0, b1 = signals(
            nc, ctx, "scored maxed negated expd turned2 pt_a pt_d weighed inverted y_out bias_in0 bias_in1")
        bias_in = (b0, b1)
        block = ctx.enter_context(nc.Block())
        psS, psT, psY = c.bank[0:3], c.bank[3:6], c.bank[6:8]

        @block.sync
        def _(sp):
            for h in range(HEADS):
                if h >= 2:
                    sp.wait_ge(negated, TT * (h - 1))
                sp.dma_start(bias[:, h % 2], t["bias"][h]).then_inc(bias_in[h % 2], 16)

        def pt_copied(eng, u):
            eng.wait_ge(pt_d if u % 2 else pt_a, u // 2 + 1)

        @block.tensor
        def _(pe):
            for i in range(UNITS + 3):
                if i < UNITS:
                    h, q = divmod(i, TT)
                    if i >= 3:
                        pe.wait_ge(expd, i - 2)
                    if h < HEADS:
                        qT, kT = a.qz[:, h], a.kT[:, h // 2]
                    else:
                        qT, kT = a.qzb[:, h - HEADS], a.kTb[:]
                    pe.matmul(psS[i % 3][:], qT[:, q * P:(q + 1) * P], kT, start=True, stop=True).then_inc(scored, 1)
                u = i - 2
                if 0 <= u < UNITS:
                    pe.wait_ge(expd, u + 1)
                    if u >= 3:
                        pt_copied(pe, u - 3)
                    for kt in range(TT):
                        mm = pe.transpose(psT[u % 3][:, kt * P:(kt + 1) * P], Pr[:, u % PR, kt * P:(kt + 1) * P], c.ident)
                    mm.then_inc(turned, 1)
                u = i - 3
                if 0 <= u < UNITS:
                    h, q = divmod(u, TT)
                    pt_copied(pe, u)
                    if q == 0 and h >= 2:
                        pe.wait_ge(y_out, h - 1)
                    for kt in range(TT):
                        v = a.va[:, kt, h * DH:(h + 1) * DH] if h < HEADS else \
                            a.vb[:, kt, (h - HEADS) // 4 * DH:((h - HEADS) // 4 + 1) * DH]
                        mm = pe.matmul(psY[h % 2][:, q * DH:(q + 1) * DH], PT[:, u % PR, kt], v, start=kt == 0, stop=kt == TT - 1)
                    mm.then_inc(weighed, 1)

        @block.vector
        def _(dve):
            for i in range(UNITS + 4):
                if i < UNITS:
                    h, q = divmod(i, TT)
                    dve.wait_ge(scored, i + 1)
                    if h < HEADS:
                        if q == 0:
                            dve.wait_ge(bias_in[h % 2], 16 * (h // 2 + 1))
                        if i >= PR:
                            dve.wait_ge(turned, i - PR + 1)
                        r0 = (WIN_H - 1 - 2 * q) * GRID_W
                        dve.tensor_tensor_reduce(Pr[:, i % PR], psS[i % 3][:], bias[:, h % 2, r0:r0 + SEQ], 1.0, LOWEST,
                                                 ALU.add, ALU.max, mx[:, i:i + 1]).then_inc(maxed, 1)
                        dve.wait_ge(maxed, i + 1)
                        dve.tensor_scalar(nm[:, i:i + 1], mx[:, i:i + 1], -1.0, None, ALU.mult).then_inc(negated, 1)
                    else:
                        dve.tensor_reduce(nm[:, i:i + 1], psS[i % 3][:], AX, ALU.max, negate=True).then_inc(negated, 1)
                u = i - 3
                if 0 <= u < UNITS and u % 2:
                    dve.wait_ge(turned, u + 1)
                    if u >= PR:
                        dve.wait_ge(weighed, u - PR + 1)
                    dve.tensor_copy(PT[:, u % PR].rearrange("p a b -> p (a b)"), psT[u % 3][:]).then_inc(pt_d, 1)
                u = i - 4
                if u >= 0 and u % TT == TT - 1:
                    h = u // TT
                    dve.wait_ge(expd, TT * (h + 1))
                    dve.reciprocal(ri[:, TT * h:TT * (h + 1)], rs[:, TT * h:TT * (h + 1)]).then_inc(inverted, 1)
                    dve.wait_ge(inverted, h + 1)
                    dve.wait_ge(weighed, TT * (h + 1))
                    dve.tensor_tensor(a.y[:, :, h * DH:(h + 1) * DH], psY[h % 2][:, 0:TT * DH].rearrange("p (t w) -> p t w", w=DH),
                                      bc(ri[:, TT * h:TT * (h + 1)], DH), ALU.mult).then_inc(y_out, 1)

        @block.scalar
        def _(act):
            for i in range(UNITS + 3):
                if i < UNITS:
                    act.wait_ge(negated, i + 1)
                    if i >= PR and i >= HEADS * TT:
                        act.wait_ge(turned, i - PR + 1)
                    src = Pr[:, i % PR] if i < HEADS * TT else psS[i % 3][:]
                    act.activation(Pr[:, i % PR], src, ACT.Exp, bias=nm[:, i:i + 1], accum_out=rs[:, i:i + 1]).then_inc(expd, 1)
                u = i - 3
                if 0 <= u < UNITS and u % 2 == 0:
                    act.wait_ge(turned, u + 1)
                    if u >= PR:
                        act.wait_ge(weighed, u - PR + 1)
                    act.activation(PT[:, u % PR].rearrange("p a b -> p (a b)"), psT[u % 3][:], ACT.Copy).then_inc(pt_a, 1)


def phase_merge(c, a):
    nc = c.nc
    with ExitStack() as ctx:
        yT = ctx.enter_context(nc.sbuf_tensor("yT", [P, KT, SEQ], F32))
        mT = ctx.enter_context(nc.sbuf_tensor("mT", [P, KT, SEQ], F32))
        sg = ctx.enter_context(nc.sbuf_tensor("sg", [P, 2, 2, SEQ], F32))
        tm = ctx.enter_context(nc.sbuf_tensor("tm", [P, 2, 2, SEQ], F32))
        (turned, out_a, out_d, grp, gated, halfd, merged, xg, added, squared, meaned, rooted, scaled, turned2, o2a, o2d) = signals(
            nc, ctx, "m_turned m_out_a m_out_d m_grp gated halved merged x_grp x_added m_sq m_mean m_root m_scaled m_turned2 m_o2a m_o2d")
        block = ctx.enter_context(nc.Block())

        yT_as_rows = yT[:].rearrange("p a b -> p (a b)").rearrange("p (t d) -> p t d", t=TT)
        junk = mT[:].rearrange("p a b -> p (a b)").rearrange("p (t d) -> p t d", t=TT)

        @block.sync
        def _(sp):
            for b in range(5, B_PQ):
                if b < B_OUT:
                    sp.wait_ge(grp, 4 * (b - B_MERGE + 1))
                else:
                    sp.wait_ge(xg, 4 * (b - B_OUT + 1))
                c.load_w(sp, b + RING)

        @block.tensor
        def _(pe):
            for kt in range(KT):
                if kt >= 4:
                    pe.wait_ge(out_d if kt % 2 else out_a, kt // 2 - 1)
                for tt in range(TT):
                    mm = pe.transpose(c.bank[kt % 4][:, tt * P:(tt + 1) * P], a.y[:, tt, kt * P:(kt + 1) * P], c.ident)
                mm.then_inc(turned, 1)
            pe.wait_ge(out_a, KT // 2)
            pe.wait_ge(out_d, KT // 2)
            for m in range(KT):
                bk = c.bank[4 * (m % 2):4 * (m % 2) + 4]
                c.wait_w(pe, B_MERGE + m)
                w = c.w(B_MERGE + m, 24 * P)
                if m >= 2:
                    pe.wait_ge(gated, 2 * (m - 1))
                    pe.wait_ge(halfd, 2 * (m - 1))
                for j, (w0, n, src) in enumerate(((0, KT, c.XT), (KT, KT, c.XT), (2 * KT, 4, yT[:, 0:4]), (2 * KT + 4, 4, yT[:, 4:8]))):
                    for k in range(n):
                        mm = pe.matmul(bk[j][:], w[:, w0 + k], src[:, k], start=k == 0, stop=k == n - 1)
                    mm.then_inc(grp, 1)
            pe.wait_ge(merged, KT)
            for g in range(2 * TT):
                nh, tt = divmod(g, TT)
                if tt == 0:
                    c.wait_w(pe, B_OUT + nh)
                if g >= 4:
                    pe.wait_ge(added, g - 3)
                w = c.w(B_OUT + nh, KT * 512, 512)
                for k in range(KT):
                    mm = pe.matmul(c.bank[g % 4][:], mT[:, k, tt * P:(tt + 1) * P], w[:, k], start=k == 0, stop=k == KT - 1)
                mm.then_inc(xg, 1)
            pe.wait_ge(added, 2 * TT)
            transposes_pe(pe, c, yT_as_rows, scaled, TT, turned2, o2a, o2d)

        @block.scalar
        def _(act):
            for kt in range(0, KT, 2):
                act.wait_ge(turned, kt + 1)
                act.activation(yT[:, kt], c.bank[kt % 4][:], ACT.Copy).then_inc(out_a, 1)
            for m in range(KT):
                for j in range(2):
                    act.wait_ge(grp, 4 * m + j + 1)
                    if m >= 2:
                        act.wait_ge(halfd, 2 * (m - 2) + j + 1)
                    act.activation(sg[:, m % 2, j], c.bank[4 * (m % 2) + j][:], ACT.Sigmoid).then_inc(gated, 1)
            act.wait_ge(added, 2 * TT)
            norm_sums(act, c, c.X, junk, squared)
            gains_act(act, c, C_G2, turned2, o2a)

        @block.gpsimd
        def _(pool):
            norm_rsqrt(pool, c, squared, TT, meaned, rooted)

        @block.vector
        def _(dve):
            for kt in range(1, KT, 2):
                dve.wait_ge(turned, kt + 1)
                dve.tensor_copy(yT[:, kt], c.bank[kt % 4][:]).then_inc(out_d, 1)
            for m in range(KT):
                for j in range(2):
                    dve.wait_ge(grp, 4 * m + 3 + j)
                    dve.wait_ge(gated, 2 * m + j + 1)
                    if m >= 2:
                        dve.wait_ge(merged, m - 1)
                    dve.tensor_tensor(tm[:, m % 2, j], c.bank[4 * (m % 2) + 2 + j][:], sg[:, m % 2, j], ALU.mult).then_inc(halfd, 1)
                dve.wait_ge(halfd, 2 * (m + 1))
                dve.tensor_tensor(mT[:, m], tm[:, m % 2, 0], tm[:, m % 2, 1], ALU.add).then_inc(merged, 1)
            for g in range(2 * TT):
                nh, tt = divmod(g, TT)
                dve.wait_ge(xg, g + 1)
                xs = c.X[:, tt, nh * 512:(nh + 1) * 512]
                dve.tensor_tensor(xs, c.bank[g % 4][:], xs, ALU.add).then_inc(added, 1)
            dve.wait_ge(rooted, 1)
            for tt in range(TT):
                dve.tensor_scalar(yT_as_rows[:, tt], c.X[:, tt], c.rn[:, tt:tt + 1], None, ALU.mult).then_inc(scaled, 1)
            gains_dve(dve, c, C_G2, turned2, o2d)


def phase_choose(c, ijg):
    nc = c.nc
    NQ = 2 * PH
    with ExitStack() as ctx:
        sb = lambda name, shape, dt=F32: ctx.enter_context(nc.sbuf_tensor(name, shape, dt))
        qT = sb("qT", [P, NQ, SEQ])
        SC = sb("SC", [P, 2, NQ, PK])
        S2 = sb("SC2", [P, NQ * PK])
        cand = sb("cand", [P, PH, TOPK * TOPK])
        t16 = sb("t16", [P, NQ, TOPK])
        i16 = sb("i16", [P, NQ, TOPK], U32)
        i16f = sb("i16f", [P, NQ, TOPK])
        b16 = sb("b16", [P, PH, TOPK])
        pos = sb("pos", [P, PH, TOPK], U32)
        ab = sb("ab", [P, 2, SLOTS], U32)
        abf = sb("abf", [P, 2, SLOTS])
        eq = sb("eq", [P, SLOTS, TOPK])
        out3 = sb("out3", [P, 3, SLOTS])
        gs = sb("gs", [P, 2, PH])
        qg, qa, qd, sg, so, step, gexp, gdiff, chosen, t3, t3o = signals(
            nc, ctx, "q_grp q_out_a q_out_d s_grp s_out c_step g_exp g_diff chosen t3_turned t3_out")
        block = ctx.enter_context(nc.Block())

        @block.sync
        def _(sp):
            for b in range(B_PQ, B_KEYS + 1):
                if b < B_KEYS:
                    sp.wait_ge(qg, 4 * (b - B_PQ + 1))
                else:
                    sp.wait_ge(sg, 4 * TT)
                c.load_w(sp, b + RING)

        @block.tensor
        def _(pe):
            for g in range(NQ):
                if g % 4 == 0:
                    c.wait_w(pe, B_PQ + g // 4)
                if g >= 4:
                    pe.wait_ge(qd if g % 2 else qa, g // 2 - 1)
                w = c.w(B_PQ + g // 4, KT * 512, 512)
                for k in range(KT):
                    mm = pe.matmul(c.bank[g % 4][:], w[:, k, (g % 4) * P:(g % 4 + 1) * P], c.XT[:, k], start=k == 0, stop=k == KT - 1)
                mm.then_inc(qg, 1)
            pe.wait_ge(qa, NQ // 2)
            pe.wait_ge(qd, NQ // 2)
            c.wait_w(pe, B_KEYS)
            keys = c.w(B_KEYS, NQ * PK)

            def scores(tt):
                for j in range(4):
                    if tt >= 1:
                        pe.wait_ge(so, 4 * (tt - 1) + j + 1)
                    for i in range(4):
                        mm = pe.matmul(c.bank[4 + j][:, i * PK:(i + 1) * PK], qT[:, 4 * j + i, tt * P:(tt + 1) * P], keys[:, 4 * j + i],
                                       start=True, stop=True)
                    mm.then_inc(sg, 1)

            scores(0)
            for tt in range(TT):
                if tt + 1 < TT:
                    scores(tt + 1)
                pe.wait_ge(chosen, tt + 1)
                if tt >= 1:
                    pe.wait_ge(t3o, tt)
                for i in range(3):
                    mm = pe.transpose(c.bank[0][:, i * P:(i + 1) * P], out3[:, i], c.ident)
                mm.then_inc(t3, 1)

        @block.scalar
        def _(act):
            for g in range(0, NQ, 2):
                act.wait_ge(qg, g + 1)
                act.activation(qT[:, g], c.bank[g % 4][:], ACT.Copy).then_inc(qa, 1)

            def scores_out(tt):
                for j in range(4):
                    act.wait_ge(sg, 4 * tt + j + 1)
                    if tt >= 2:
                        act.wait_ge(chosen, tt - 1)
                    act.activation(SC[:, tt % 2, 4 * j:4 * j + 4].rearrange("p a b -> p (a b)"), c.bank[4 + j][:], ACT.Copy).then_inc(so, 1)

            scores_out(0)
            for tt in range(TT):
                if tt + 1 < TT:
                    scores_out(tt + 1)
                act.wait_ge(gdiff, tt + 1)
                act.activation(b16[:], b16[:], ACT.Exp).then_inc(gexp, 1)
                act.wait_ge(t3, tt + 1)
                act.activation(ijg[:, :, tt * P:(tt + 1) * P], c.bank[0][:, 0:3 * P].rearrange("p (a b) -> p a b", b=P), ACT.Copy).then_inc(t3o, 1)

        @block.vector
        def _(dve):
            for g in range(1, NQ, 2):
                dve.wait_ge(qg, g + 1)
                dve.tensor_copy(qT[:, g], c.bank[g % 4][:]).then_inc(qd, 1)
            n = [0]

            def link(ins):
                n[0] += 1
                ins.then_inc(step, 1)
                dve.wait_ge(step, n[0])

            sc2 = S2[:].rearrange("p (a b) -> p a b", b=PK)
            cand2 = S2[:].rearrange("p (a b) -> p a b", b=TOPK * TOPK)
            for tt in range(TT):
                sc = SC[:, tt % 2]
                dve.wait_ge(so, 4 * (tt + 1))
                for j in range(NQ):
                    last = dve.max(t16[:, j, 0:8], sc[:, j])
                link(last)
                for j in range(NQ):
                    dve.max_index(i16[:, j, 0:8], t16[:, j, 0:8], sc[:, j])
                    last = dve.match_replace(sc2[:, j], t16[:, j, 0:8], sc[:, j], LOWEST)
                link(last)
                for j in range(NQ):
                    last = dve.max(t16[:, j, 8:16], sc2[:, j])
                link(last)
                for j in range(NQ):
                    last = dve.max_index(i16[:, j, 8:16], t16[:, j, 8:16], sc2[:, j])
                link(last)
                link(dve.tensor_copy(i16f[:], i16[:]))
                for h in range(PH):
                    last = dve.tensor_tensor(cand[:, h].rearrange("p (a b) -> p a b", b=TOPK), bc(t16[:, 2 * h], TOPK),
                                             mid(t16[:, 2 * h + 1], TOPK), ALU.add)
                link(last)
                if tt >= 1:
                    dve.wait_ge(t3, tt)
                for h in range(PH):
                    last = dve.max(b16[:, h, 0:8], cand[:, h])
                link(last)
                for h in range(PH):
                    dve.max_index(pos[:, h, 0:8], b16[:, h, 0:8], cand[:, h])
                    last = dve.match_replace(cand2[:, h], b16[:, h, 0:8], cand[:, h], LOWEST)
                link(last)
                for h in range(PH):
                    last = dve.max(b16[:, h, 8:16], cand2[:, h])
                link(last)
                for h in range(PH):
                    last = dve.max_index(pos[:, h, 8:16], b16[:, h, 8:16], cand2[:, h])
                link(last)
                link(dve.tensor_copy(gs[:, 0], b16[:, :, 0]))
                dve.tensor_tensor(b16[:], b16[:], bc(gs[:, 0], TOPK), ALU.subtract).then_inc(gdiff, 1)
                posf = pos[:].rearrange("p h k -> p (h k)")
                dve.tensor_scalar(ab[:, 0], posf, 4, None, ALU.logical_shift_right)
                link(dve.tensor_scalar(ab[:, 1], posf, TOPK - 1, None, ALU.bitwise_and))
                link(dve.tensor_copy(abf[:], ab[:]))
                for half in range(2):
                    link(dve.tensor_tensor(eq[:], bc(abf[:, half], TOPK), mid(c.iota[:, 0:TOPK], SLOTS), ALU.is_equal))
                    eqh = eq[:].rearrange("p (h k) a -> p h k a", h=PH)
                    key = i16f[:].rearrange("p (h f) a -> p h f a", f=2)[:, :, half].unsqueeze(2).broadcast_to([P, PH, TOPK, TOPK])
                    link(dve.tensor_tensor(eqh, eqh, key, ALU.mult))
                    link(dve.tensor_reduce(out3[:, half], eq[:], AX, ALU.add))
                dve.wait_ge(gexp, tt + 1)
                link(dve.tensor_reduce(gs[:, 0], b16[:], AX, ALU.add))
                link(dve.reciprocal(gs[:, 1], gs[:, 0]))
                dve.tensor_tensor(out3[:, 2].rearrange("p (h k) -> p h k", h=PH), b16[:], bc(gs[:, 1], TOPK), ALU.mult).then_inc(chosen, 1)
                dve.wait_ge(chosen, tt + 1)


def phase_gates(c, ijg):
    nc, t = c.nc, c.t
    Q = 4
    PER = P // Q
    with ExitStack() as ctx:
        hot = ctx.enter_context(nc.sbuf_tensor("hot", [P, 2, Q, 2, P], F32))
        stage = ctx.enter_context(nc.sbuf_tensor("stage", [P, PK, P], F32))
        hot_ready, built, copied, stored = signals(nc, ctx, "hot_ready built copied stored")
        block = ctx.enter_context(nc.Block())
        dest = t["gates"].rearrange("i j t -> j i t")

        @block.vector
        def _(dve):
            for tt in range(TT):
                with dve.Fori(0, PER // 2) as it:
                    for s in range(2):
                        dve.wait_ge(built, it * 2 + (tt * PER + s + 1))
                        for k in range(Q):
                            tok = it * (2 * Q) + (tt * P + s * Q + k)
                            col = lambda r: ijg[:, r, bass.ds(tok, 1)]
                            dve.tensor_scalar(hot[:, s, k, 0], c.iota, col(1), None, ALU.is_equal)
                            last = dve.tensor_scalar(hot[:, s, k, 1], c.iota, col(0), col(2), ALU.is_equal, ALU.mult)
                        last.then_inc(hot_ready, 1)

        @block.tensor
        def _(pe):
            pe.sem_inc(built, 2)
            for tt in range(TT):
                with pe.Fori(0, PER // 4) as it:
                    for s in range(4):
                        pe.wait_ge(hot_ready, it * 4 + (tt * PER + s + 1))
                        pe.wait_ge(copied, it * 4 + (tt * PER + s + 1))
                        for k in range(Q):
                            mm = pe.matmul(c.bank[s][:, k * P:(k + 1) * P], hot[:, s % 2, k, 0], hot[:, s % 2, k, 1], start=True, stop=True)
                        mm.then_inc(built, 1)

        @block.scalar
        def _(act):
            act.sem_inc(copied, 4)
            for tt in range(TT):
                if tt >= 1:
                    act.wait_ge(stored, 16 * tt)
                with act.Fori(0, PER // 4) as it:
                    for s in range(4):
                        act.wait_ge(built, it * 4 + (tt * PER + s + 3))
                        o = stage[:, :, bass.ds(it * (4 * Q) + s * Q, Q)]
                        act.activation(o, c.bank[s][:].rearrange("p (k i) -> p i k", k=Q), ACT.Copy).then_inc(copied, 1)

        @block.sync
        def _(sp):
            for tt in range(TT):
                sp.wait_ge(copied, PER * (tt + 1) + 4)
                sp.dma_start(dest[:, :, tt * P:(tt + 1) * P], stage[:]).then_inc(stored, 16)
            sp.wait_ge(stored, 16 * TT)


def phase_experts(c):
    nc, t = c.nc, c.t
    with ExitStack() as ctx:
        U = [ctx.enter_context(nc.sbuf_tensor(f"U{i}", [P, KT, EG * P], F32)) for i in range(2)]
        V = [ctx.enter_context(nc.sbuf_tensor(f"V{i}", [P, EG, D], F32)) for i in range(2)]
        G = [ctx.enter_context(nc.sbuf_tensor(f"G{i}", [P, EG, SEQ], F32)) for i in range(2)]
        H = [ctx.enter_context(nc.sbuf_tensor(f"H{i}", [P, EG, SEQ], F32)) for i in range(2)]
        u0, u1, v0, v1, g0, g1, acted, gelud, gated, summed, added = signals(
            nc, ctx, "u_in0 u_in1 v_in0 v_in1 g_in0 g_in1 acted gelud e_gated summed added2")
        u_in, v_in, g_in = (u0, u1), (v0, v1), (g0, g1)
        block = ctx.enter_context(nc.Block())
        VG = 2 * TT

        @block.sync
        def _(sp):
            with sp.Fori(0, NG // 2) as it:
                for s in range(2):
                    one = bass.ds(it * 2 + s, 1)
                    sp.wait_ge(acted, it * 8 + (4 * s + 4))
                    sp.dma_start(U[s][:], t["u"][one].rearrange("g p k e -> (g p) k e")).then_inc(u_in[s], 16)
                    sp.wait_ge(gated, it * 8 + (4 * s + 4))
                    sp.dma_start(G[s][:], t["gates"][bass.ds(it * (2 * EG) + s * EG, EG)].rearrange("i j t -> j i t")).then_inc(g_in[s], 16)
                    sp.wait_ge(summed, it * 16 + (8 * s + 8))
                    sp.dma_start(V[s][:], t["v"][one].rearrange("g e p d -> p (g e) d")).then_inc(v_in[s], 16)

        def up(pe, it, s):
            pe.wait_ge(u_in[s], it * 16 + 16)
            for e in range(EG):
                pe.wait_ge(gelud, it * 8 + (4 * s + e + 1))
                for k in range(KT):
                    mm = pe.matmul(c.bank[e][:], U[s][:, k, e * P:(e + 1) * P], c.XT[:, k], start=k == 0, stop=k == KT - 1)
                mm.then_inc(acted, 1)

        def down(pe, it, s):
            pe.wait_ge(gated, it * 8 + (4 * s + 12))
            pe.wait_ge(v_in[s], it * 16 + 16)
            for p in range(VG):
                tt, nh = divmod(p, 2)
                pe.wait_ge(added, it * 16 + (8 * s + p + 5))
                for e in range(EG):
                    mm = pe.matmul(c.bank[4 + p % 4][:], H[s][:, e, tt * P:(tt + 1) * P], V[s][:, e, nh * 512:(nh + 1) * 512],
                                   start=e == 0, stop=e == EG - 1)
                mm.then_inc(summed, 1)

        @block.tensor
        def _(pe):
            pe.sem_inc(acted, 8)
            pe.sem_inc(summed, 16)
            up(pe, 0, 0)
            with pe.Fori(0, NG // 2 - 1) as it:
                up(pe, it, 1)
                down(pe, it, 0)
                up(pe, it + 1, 0)
                down(pe, it, 1)
            up(pe, NG // 2 - 1, 1)
            down(pe, NG // 2 - 1, 0)
            down(pe, NG // 2 - 1, 1)

        @block.scalar
        def _(act):
            act.sem_inc(gelud, 4)
            with act.Fori(0, NG // 2) as it:
                for s in range(2):
                    act.wait_ge(summed, it * 16 + (8 * s + 8))
                    for e in range(EG):
                        act.wait_ge(acted, it * 8 + (4 * s + e + 9))
                        act.activation(H[s][:, e], c.bank[e][:], ACT.Gelu).then_inc(gelud, 1)

        def gate(dve, it, s):
            dve.wait_ge(g_in[s], it * 16 + 16)
            for e in range(EG):
                dve.wait_ge(gelud, it * 8 + (4 * s + e + 5))
                dve.tensor_tensor(H[s][:, e], H[s][:, e], G[s][:, e], ALU.mult).then_inc(gated, 1)

        def add(dve, it, s):
            for p in range(VG):
                tt, nh = divmod(p, 2)
                dve.wait_ge(summed, it * 16 + (8 * s + p + 17))
                dve.wait_ge(added, it * 16 + (8 * s + p + 1))
                xs = c.X[:, tt, nh * 512:(nh + 1) * 512]
                dve.tensor_tensor(xs, c.bank[4 + p % 4][:], xs, ALU.add).then_inc(added, 1)

        @block.vector
        def _(dve):
            dve.sem_inc(gated, 8)
            dve.sem_inc(added, 8)
            gate(dve, 0, 0)
            with dve.Fori(0, NG // 2 - 1) as it:
                gate(dve, it, 1)
                add(dve, it, 0)
                gate(dve, it + 1, 0)
                add(dve, it, 1)
            gate(dve, NG // 2 - 1, 1)
            add(dve, NG // 2 - 1, 0)
            add(dve, NG // 2 - 1, 1)


def phase_between(c):
    nc, t = c.nc, c.t
    with ExitStack() as ctx:
        HN = ctx.enter_context(nc.sbuf_tensor("HN2", [P, TT, D], F32))
        nf = ctx.enter_context(nc.sbuf_tensor("nf", [P, D], F32))
        nf_in, squared, meaned, rooted, xnorm, xready, scaled, turned, out_a, out_d = signals(
            nc, ctx, "nf_in b_sq b_mean b_root b_xnorm b_xready b_scaled b_turned b_out_a b_out_d")
        block = ctx.enter_context(nc.Block())

        @block.sync
        def _(sp):
            sp.dma_start(nf[:], t["norm_f"]).then_inc(nf_in, 16)

        @block.scalar
        def _(act):
            norm_sums(act, c, c.X, HN, squared)
            act.wait_ge(xready, TT)
            act.wait_ge(squared, TT)
            norm_sums(act, c, c.X, HN, squared)
            gains_act(act, c, C_GPRE, turned, out_a)

        @block.gpsimd
        def _(pool):
            norm_rsqrt(pool, c, squared, TT, meaned, rooted)
            pool.wait_ge(xnorm, TT)
            norm_rsqrt(pool, c, squared, 2 * TT, meaned, rooted)

        @block.vector
        def _(dve):
            dve.wait_ge(rooted, 1)
            for tt in range(TT):
                dve.tensor_scalar(c.X[:, tt], c.X[:, tt], c.rn[:, tt:tt + 1], None, ALU.mult).then_inc(xnorm, 1)
            dve.wait_ge(nf_in, 16)
            for tt in range(TT):
                dve.wait_ge(xnorm, tt + 1)
                dve.tensor_tensor(c.X[:, tt], c.X[:, tt], nf[:], ALU.mult).then_inc(xready, 1)
            dve.wait_ge(rooted, 2)
            dve.wait_ge(xready, TT)
            for tt in range(TT):
                dve.tensor_scalar(HN[:, tt], c.X[:, tt], c.rn[:, tt:tt + 1], None, ALU.mult).then_inc(scaled, 1)
            gains_dve(dve, c, C_GPRE, turned, out_d)

        @block.tensor
        def _(pe):
            transposes_pe(pe, c, HN, scaled, TT, turned, out_a, out_d)


class Mixer:
    def __init__(self, nc, ctx):
        sb = lambda name, shape: ctx.enter_context(nc.sbuf_tensor(name, shape, F32))
        self.yscT = sb("yscT", [P, KT, SEQ])
        self.xs = sb("xs", [P, TT, D])
        self.zs = sb("zs", [P, TT, D])
        self.xbcT = sb("xbcT", [P, XBC_TILES, SEQ])
        self.dt = sb("dt", [P, TT, SH])


def phase_mixer_in(c, m_):
    nc = c.nc
    with ExitStack() as ctx:
        pad = ctx.enter_context(nc.sbuf_tensor("pad", [P, 2, CONV_W - 1 + SEQ], F32))
        pad2 = ctx.enter_context(nc.sbuf_tensor("pad2", [P, 2, SC_W - 1 + SEQ], F32))
        cv = ctx.enter_context(nc.sbuf_tensor("cv", [P, 2, SEQ], F32))
        cs = ctx.enter_context(nc.sbuf_tensor("cs", [P, 2, SEQ], F32))
        zz = ctx.enter_context(nc.sbuf_tensor("zz", [P, 2, SEQ], F32))
        zero, grp, padded, convd, silud, dtg, dto, scg, c_out, z_out, step, vdone = signals(
            nc, ctx, "n_zero n_grp n_padded n_convd n_silud n_dt_grp n_dt_out n_sc_grp n_c_out n_z_out n_step n_done")
        block = ctx.enter_context(nc.Block())
        NX, NZ = XBC_TILES, 2 * TT

        @block.sync
        def _(sp):
            for b in range(B_XBC, B_MIX):
                if b < B_DT:
                    sp.wait_ge(grp, min(4 * (b - B_XBC + 1), NX))
                elif b == B_DT:
                    sp.wait_ge(dtg, 1)
                elif b < B_SC:
                    sp.wait_ge(grp, NX + TT * (b - B_Z + 1))
                else:
                    sp.wait_ge(scg, 4 * (b - B_SC + 1))
                c.load_w(sp, b + RING)

        @block.gpsimd
        def _(pool):
            pool.memset(pad[:], 0.0).then_inc(zero, 1)
            pool.memset(pad2[:], 0.0).then_inc(zero, 1)

        @block.tensor
        def _(pe):
            def slot(n):
                if n >= 4:
                    if n - 4 < NX:
                        pe.wait_ge(padded, n - 3)
                    else:
                        pe.wait_ge(z_out, n - 4 - NX + 1)

            for n in range(NX):
                if n % 4 == 0:
                    c.wait_w(pe, B_XBC + n // 4)
                slot(n)
                width = min(512, NX * P - 512 * (n // 4))
                w = c.w(B_XBC + n // 4, KT * width, width)
                for k in range(KT):
                    mm = pe.matmul(c.bank[n % 4][:], w[:, k, (n % 4) * P:(n % 4 + 1) * P], c.XT[:, k], start=k == 0, stop=k == KT - 1)
                mm.then_inc(grp, 1)
            c.wait_w(pe, B_DT)
            w = c.w(B_DT, KT * SH, SH)
            for tt in range(TT):
                for k in range(KT):
                    mm = pe.matmul(c.bank[7][:, tt * SH:(tt + 1) * SH], c.XT[:, k, tt * P:(tt + 1) * P], w[:, k], start=k == 0, stop=k == KT - 1)
            mm.then_inc(dtg, 1)
            for n in range(NX, NX + NZ):
                nh, tt = divmod(n - NX, TT)
                if tt == 0:
                    c.wait_w(pe, B_Z + nh)
                slot(n)
                w = c.w(B_Z + nh, KT * 512, 512)
                for k in range(KT):
                    mm = pe.matmul(c.bank[n % 4][:], c.XT[:, k, tt * P:(tt + 1) * P], w[:, k], start=k == 0, stop=k == KT - 1)
                mm.then_inc(grp, 1)
            pe.wait_ge(z_out, NZ)
            pe.wait_ge(dto, 1)
            for m in range(KT):
                c.wait_w(pe, B_SC + m)
                if m >= 2:
                    pe.wait_ge(vdone, m - 1)
                    pe.wait_ge(z_out, NZ + m - 1)
                w = c.w(B_SC + m, 4 * KT * P)
                for j in range(4):
                    for k in range(KT):
                        mm = pe.matmul(c.bank[4 * (m % 2) + j][:], w[:, KT * j + k], c.XT[:, k], start=k == 0, stop=k == KT - 1)
                    mm.then_inc(scg, 1)

        @block.scalar
        def _(act):
            act.wait_ge(zero, 2)
            for n in range(NX + 1):
                if n < NX:
                    act.wait_ge(grp, n + 1)
                    if n >= 2:
                        act.wait_ge(convd, n - 1)
                    act.activation(pad[:, n % 2, CONV_W - 1:], c.bank[n % 4][:], ACT.Copy).then_inc(padded, 1)
                if n >= 1:
                    act.wait_ge(convd, n)
                    act.activation(m_.xbcT[:, n - 1], cv[:, (n - 1) % 2], ACT.Silu, bias=c.cols[:, C_CB + n - 1:C_CB + n]).then_inc(silud, 1)
            for n in range(NZ):
                nh, tt = divmod(n, TT)
                act.wait_ge(grp, NX + n + 1)
                act.activation(m_.zs[:, tt, nh * 512:(nh + 1) * 512], c.bank[(NX + n) % 4][:], ACT.Silu).then_inc(z_out, 1)
            for m in range(KT):
                bk = c.bank[4 * (m % 2):4 * (m % 2) + 4]
                act.wait_ge(scg, 4 * m + 1)
                if m >= 2:
                    act.wait_ge(vdone, m - 1)
                act.activation(cs[:, m % 2], bk[0][:], ACT.Copy).then_inc(c_out, 1)
                act.wait_ge(scg, 4 * m + 4)
                act.activation(zz[:, m % 2], bk[3][:], ACT.Silu).then_inc(z_out, 1)

        @block.vector
        def _(dve):
            n_ = [0]

            def link(ins):
                n_[0] += 1
                ins.then_inc(step, 1)
                dve.wait_ge(step, n_[0])

            for n in range(NX):
                dve.wait_ge(padded, n + 1)
                if n >= 2:
                    dve.wait_ge(silud, n - 1)
                tap = lambda k: c.cols[:, C_CW + n * CONV_W + k:C_CW + n * CONV_W + k + 1]
                o = cv[:, n % 2]
                link(dve.tensor_scalar(o, pad[:, n % 2, 0:SEQ], tap(0), None, ALU.mult))
                for k in range(1, CONV_W):
                    ins = dve.scalar_tensor_tensor(out=o, in0=pad[:, n % 2, k:k + SEQ], scalar=tap(k), in1=o, op0=ALU.mult, op1=ALU.add)
                    if k < CONV_W - 1:
                        link(ins)
                ins.then_inc(convd, 1)
            dve.wait_ge(dtg, 1)
            dve.tensor_tensor(m_.dt[:], c.bank[7][:, 0:TT * SH].rearrange("p (t h) -> p t h", h=SH), mid(c.rows[:, R_DTB:R_DTB + SH], TT),
                              ALU.add).then_inc(dto, 1)
            for m in range(KT):
                bk = c.bank[4 * (m % 2):4 * (m % 2) + 4]
                dve.wait_ge(scg, 4 * m + 2)
                dve.wait_ge(c_out, m + 1)
                link(dve.tensor_tensor(pad2[:, m % 2, SC_W - 1:], bk[1][:], cs[:, m % 2], ALU.mult))
                tap = lambda k: c.cols[:, C_SW + m * SC_W + k:C_SW + m * SC_W + k + 1]
                o = m_.yscT[:, m]
                link(dve.tensor_scalar(o, pad2[:, m % 2, 0:SEQ], tap(0), None, ALU.mult))
                for k in range(1, SC_W):
                    link(dve.scalar_tensor_tensor(out=o, in0=pad2[:, m % 2, k:k + SEQ], scalar=tap(k), in1=o, op0=ALU.mult, op1=ALU.add))
                dve.wait_ge(scg, 4 * m + 3)
                link(dve.tensor_tensor(o, bk[2][:], o, ALU.mult))
                dve.wait_ge(z_out, NZ + m + 1)
                dve.tensor_tensor(o, o, zz[:, m % 2], ALU.mult).then_inc(vdone, 1)


def phase_scan(c, m_):
    nc, t = c.nc, c.t
    GW = HG * SP_
    UN = TT * SG
    with ExitStack() as ctx:
        sb = lambda name, shape: ctx.enter_context(nc.sbuf_tensor(name, shape, F32))
        bt = sb("bt", [P, TT, P])
        ones = sb("ones", [P, P])
        sp_ = sb("sp", [P, 6, TT, SH])
        aneg = sb("aneg", [P, SH])
        adt = sb("adt", [P, TT, SH])
        acs = sb("acs", [P, 2, TT, SH])
        eacs = sb("eacs", [P, TT, SH])
        dst = sb("dst", [P, TT, SH])
        etot = sb("etot", [P, TT, SH])
        dec = sb("dec", [P, TT, HG])
        xd = sb("xd", [P, D])
        xdd = sb("xdd", [P, D])
        E = sb("E", [P, 2, HG, P])
        cbm = sb("cbm", [P, 2, P])
        st = sb("st", [P, GW])
        tmp = sb("tmp", [P, GW])
        sg = sb("sgn", [P, 3, UN])
        nrm = sb("nrm", [P, D])
        y = c.XT[:].rearrange("p a b -> p (a b)").rearrange("p (t d) -> p t d", t=TT)
        (nrm_in, one, turned, x_out, x_outd, step, aexp, sexp, sln, adt_ok, cums, cum_out, decs, e2, unit, masked, mexp, mt, xdok,
         diag, offd, stg, yv, stv, ysq, ymean, yroot, yn, yt, ya, yd) = signals(
            nc, ctx, "nrm_in s_one s_turned s_x_out s_x_outd s_step s_aexp s_sexp s_sln s_adt s_cums s_cum_out s_decs s_e2 s_unit s_masked "
            "s_mexp s_mt s_xd s_diag s_off s_states s_yv s_stv s_ysq s_ymean s_yroot s_yn s_yt s_ya s_yd")
        block = ctx.enter_context(nc.Block())
        BT, CT = m_.xbcT[:, KT], m_.xbcT[:, KT + 1]
        yT = lambda kt: m_.xs[:].rearrange("p t d -> p (t d)")[:, kt * SEQ:(kt + 1) * SEQ]
        tmp2 = lambda v: m_.xs[:, v // SG, v % SG * GW:(v % SG + 1) * GW]

        @block.sync
        def _(sp):
            sp.dma_start(nrm[:], t["ssd_norm"]).then_inc(nrm_in, 16)

        @block.gpsimd
        def _(pool):
            pool.memset(ones[:], 1.0).then_inc(one, 1)
            pool.wait_ge(ysq, UN)
            pool.tensor_scalar(sg[:, 1], sg[:, 0], 1.0 / GW, EPS, ALU.mult, ALU.add).then_inc(ymean, 1)
            pool.wait_ge(ymean, 1)
            pool.tensor_tensor(sg[:, 2], sg[:, 1], c.half[:, 0:UN], ALU.pow).then_inc(yroot, 1)

        @block.tensor
        def _(pe):
            for cc in range(TT):
                if cc >= 1:
                    pe.wait_ge(x_out, 2 * cc)
                    pe.wait_ge(x_outd, cc)
                for j in range(KT + 1):
                    mm = pe.transpose(c.bank[j // 4][:, (j % 4) * P:(j % 4 + 1) * P], m_.xbcT[:, j, cc * P:(cc + 1) * P], c.ident)
                mm.then_inc(turned, 1)
            pe.wait_ge(one, 1)
            pe.wait_ge(adt_ok, 1)
            for cc in range(TT):
                pe.matmul(c.bank[3][:, cc * SH:(cc + 1) * SH], c.tri, adt[:, cc], start=True, stop=True)
                mm = pe.matmul(c.bank[3][:, (TT + cc) * SH:(TT + cc + 1) * SH], ones[:], adt[:, cc], start=True, stop=True)
            mm.then_inc(cums, 1)
            pe.wait_ge(x_out, 2 * TT)
            pe.wait_ge(x_outd, TT)
            pe.wait_ge(cum_out, 1)

            def decays(v):
                cc, g = divmod(v, SG)
                rows, tok = slice(64 * g, 64 * g + 64), slice(cc * P, (cc + 1) * P)
                if v >= 1:
                    pe.wait_ge(masked, v)
                if v >= 2:
                    pe.wait_ge(unit, v - 1)
                pe.matmul(c.bank[4][:, 0:P], BT[rows, tok], CT[rows, tok], start=True, stop=True)
                for h in range(HG):
                    a1 = adt[:, cc, g * HG + h:g * HG + h + 1].broadcast_to([P, P])
                    mm = pe.matmul(c.bank[2 * (v % 2) + h // 4][:, (h % 4) * P:(h % 4 + 1) * P], a1, c.tri, start=True, stop=True)
                mm.then_inc(cums, 1)

            decays(0)
            for v in range(UN):
                cc, g = divmod(v, SG)
                rows, tok = slice(64 * g, 64 * g + 64), slice(cc * P, (cc + 1) * P)
                if v + 1 < UN:
                    decays(v + 1)
                pe.wait_ge(mt, v + 1)
                pe.wait_ge(xdok, cc + 1)
                if v >= 1:
                    pe.wait_ge(yv, v)
                for h in range(HG):
                    mm = pe.matmul(c.bank[5][:, h * SP_:(h + 1) * SP_], E[:, v % 2, h], xd[:, g * GW + h * SP_:g * GW + (h + 1) * SP_],
                                   start=True, stop=True)
                mm.then_inc(diag, 1)
                if cc >= 1:
                    pe.wait_ge(stv, cc)
                    pe.matmul(c.bank[6][:], CT[rows, tok], st[rows, :], start=True, stop=True).then_inc(offd, 1)
                if cc + 1 < TT:
                    if cc >= 1 and g == 0:
                        pe.wait_ge(stv, cc)
                    pe.matmul(c.bank[7][rows, :], bt[:, cc, rows], xdd[:, g * GW:(g + 1) * GW], start=True, stop=True).then_inc(stg, 1)
            for kt in range(KT):
                if kt == 0:
                    pe.wait_ge(yn, TT)
                if kt >= 4:
                    pe.wait_ge(yd if kt % 2 else ya, kt // 2 - 1)
                for tt in range(TT):
                    mm = pe.transpose(c.bank[kt % 4][:, tt * P:(tt + 1) * P], y[:, tt, kt * P:(kt + 1) * P], c.ident)
                mm.then_inc(yt, 1)

        @block.scalar
        def _(act):
            act.activation(aneg[:], c.rows[:, R_ALOG:R_ALOG + SH], ACT.Exp).then_inc(aexp, 1)
            act.wait_ge(step, 1)
            act.activation(sp_[:, 1], sp_[:, 0], ACT.Exp).then_inc(sexp, 1)
            act.wait_ge(step, 2)
            act.activation(sp_[:, 3], sp_[:, 2], ACT.Ln).then_inc(sln, 1)
            for cc in range(TT):
                act.wait_ge(turned, cc + 1)
                act.activation(m_.xs[:, cc, 0:512], c.bank[0][:], ACT.Copy).then_inc(x_out, 1)
                act.activation(bt[:, cc], c.bank[2][:, 0:P], ACT.Copy).then_inc(x_out, 1)
            act.wait_ge(decs, 1)
            act.activation(eacs[:], acs[:, 0], ACT.Exp)
            act.activation(etot[:], acs[:, 1], ACT.Exp)
            act.activation(dst[:], dst[:], ACT.Exp).then_inc(e2, 1)
            for v in range(UN):
                act.wait_ge(unit, v + 1)
                act.activation(E[:, v % 2], E[:, v % 2], ACT.Exp).then_inc(mexp, 1)
            for v in range(UN):
                cc, g = divmod(v, SG)
                act.wait_ge(yv, UN + v + 1)
                act.activation(tmp2(v), y[:, cc, g * GW:(g + 1) * GW], ACT.Square, accum_out=sg[:, 0, v:v + 1]).then_inc(ysq, 1)
            for kt in range(0, KT, 2):
                act.wait_ge(yt, kt + 1)
                act.activation(yT(kt), c.bank[kt % 4][:], ACT.Copy).then_inc(ya, 1)

        @block.vector
        def _(dve):
            n = [0]

            def link(ins):
                n[0] += 1
                ins.then_inc(step, 1)
                dve.wait_ge(step, n[0])

            link(dve.scalar_tensor_tensor(out=sp_[:, 0], in0=m_.dt[:], scalar=-1.0, in1=m_.dt[:], op0=ALU.mult, op1=ALU.min))
            dve.wait_ge(sexp, 1)
            link(dve.tensor_scalar(sp_[:, 2], sp_[:, 1], 1.0, None, ALU.add))
            link(dve.tensor_scalar(sp_[:, 4], sp_[:, 2], -1.0, None, ALU.add))
            link(dve.tensor_scalar(sp_[:, 5], sp_[:, 4], 0.0, None, ALU.is_equal))
            link(dve.tensor_tensor(sp_[:, 4], sp_[:, 4], sp_[:, 5], ALU.add))
            link(dve.reciprocal(sp_[:, 4], sp_[:, 4]))
            dve.wait_ge(sln, 1)
            link(dve.tensor_tensor(sp_[:, 3], sp_[:, 3], sp_[:, 5], ALU.add))
            link(dve.tensor_tensor(sp_[:, 3], sp_[:, 3], sp_[:, 1], ALU.mult))
            link(dve.tensor_tensor(sp_[:, 3], sp_[:, 3], sp_[:, 4], ALU.mult))
            link(dve.scalar_tensor_tensor(out=m_.dt[:], in0=m_.dt[:], scalar=0.0, in1=sp_[:, 3], op0=ALU.max, op1=ALU.add))
            dve.wait_ge(aexp, 1)
            link(dve.tensor_scalar(sp_[:, 0], m_.dt[:], -1.0, None, ALU.mult))
            dve.tensor_tensor(adt[:], sp_[:, 0], mid(aneg[:], TT), ALU.mult).then_inc(adt_ok, 1)
            for cc in range(TT):
                dve.wait_ge(turned, cc + 1)
                dve.tensor_copy(m_.xs[:, cc, 512:], c.bank[1][:]).then_inc(x_outd, 1)
            dve.wait_ge(cums, 1)
            dve.tensor_copy(acs[:].rearrange("p a t h -> p (a t h)"), c.bank[3][:, 0:2 * TT * SH]).then_inc(cum_out, 1)
            dve.wait_ge(cum_out, 1)
            dve.tensor_tensor(dst[:], acs[:, 1], acs[:, 0], ALU.subtract).then_inc(decs, 1)
            dve.wait_ge(e2, 1)
            for g in range(SG):
                last = dve.tensor_copy(dec[64 * g:64 * g + 64], etot[64 * g:64 * g + 64, :, g * HG:(g + 1) * HG])
            link(last)

            def decays(v):
                cc, g = divmod(v, SG)
                dve.wait_ge(cums, v + 2)
                if v >= 2:
                    dve.wait_ge(diag, v - 1)
                dve.tensor_tensor(cbm[:, v % 2], c.bank[4][:, 0:P], c.tri, ALU.mult).then_inc(masked, 1)
                for h in range(HG):
                    last = dve.tensor_scalar(E[:, v % 2, h], c.bank[2 * (v % 2) + h // 4][:, (h % 4) * P:(h % 4 + 1) * P],
                                             acs[:, 0, cc, g * HG + h:g * HG + h + 1], 0.0, ALU.subtract, ALU.min)
                last.then_inc(unit, 1)

            decays(0)
            for v in range(UN):
                cc, g = divmod(v, SG)
                heads = slice(g * HG, (g + 1) * HG)
                if g == 0:
                    if cc >= 1:
                        dve.wait_ge(diag, v)
                        dve.wait_ge(stg, 2 * cc)
                    xs16 = m_.xs[:, cc].rearrange("p (h w) -> p h w", w=SP_)
                    link(dve.tensor_tensor(xd[:].rearrange("p (h w) -> p h w", w=SP_), xs16, bc(m_.dt[:, cc], SP_), ALU.mult))
                    dve.tensor_tensor(xdd[:].rearrange("p (h w) -> p h w", w=SP_), xd[:].rearrange("p (h w) -> p h w", w=SP_),
                                      bc(dst[:, cc], SP_), ALU.mult).then_inc(xdok, 1)
                if v + 1 < UN:
                    decays(v + 1)
                dve.wait_ge(mexp, v + 1)
                dve.tensor_tensor(E[:, v % 2], E[:, v % 2], mid(cbm[:, v % 2], HG), ALU.mult).then_inc(mt, 1)
                yo = y[:, cc, g * GW:(g + 1) * GW]
                yo3 = yo.rearrange("p (h w) -> p h w", w=SP_)
                xs3 = m_.xs[:, cc, g * GW:(g + 1) * GW].rearrange("p (h w) -> p h w", w=SP_)
                dsk = c.rows[:, R_DSK + g * HG:R_DSK + (g + 1) * HG]
                link(dve.tensor_tensor(yo3, xs3, bc(dsk, SP_), ALU.mult))
                if cc >= 1:
                    dve.wait_ge(offd, 2 * (cc - 1) + g + 1)
                    link(dve.tensor_tensor(tmp[:].rearrange("p (h w) -> p h w", w=SP_), c.bank[6][:].rearrange("p (h w) -> p h w", w=SP_),
                                           bc(eacs[:, cc, heads], SP_), ALU.mult))
                    link(dve.tensor_tensor(yo, yo, tmp[:], ALU.add))
                dve.wait_ge(diag, v + 1)
                dve.tensor_tensor(yo, c.bank[5][:], yo, ALU.add).then_inc(yv, 1)
                if g == SG - 1 and cc + 1 < TT:
                    dve.wait_ge(stg, 2 * cc + 2)
                    if cc == 0:
                        dve.tensor_copy(st[:], c.bank[7][:]).then_inc(stv, 1)
                    else:
                        st3 = st[:].rearrange("p (h w) -> p h w", w=SP_)
                        dve.wait_ge(offd, 2 * cc)
                        dve.wait_ge(stv, cc)
                        link(dve.tensor_tensor(st3, st3, bc(dec[:, cc], SP_), ALU.mult))
                        dve.tensor_tensor(st[:], c.bank[7][:], st[:], ALU.add).then_inc(stv, 1)
            dve.wait_ge(yv, UN)
            for v in range(UN):
                cc, g = divmod(v, SG)
                yo = y[:, cc, g * GW:(g + 1) * GW]
                dve.tensor_tensor(yo, yo, m_.zs[:, cc, g * GW:(g + 1) * GW], ALU.mult).then_inc(yv, 1)
            dve.wait_ge(yroot, 1)
            dve.wait_ge(nrm_in, 16)
            for v in range(UN):
                cc, g = divmod(v, SG)
                yo = y[:, cc, g * GW:(g + 1) * GW]
                last = dve.tensor_scalar(yo, yo, sg[:, 2, v:v + 1], None, ALU.mult)
            link(last)
            for cc in range(TT):
                dve.tensor_tensor(y[:, cc], y[:, cc], nrm[:], ALU.mult).then_inc(yn, 1)
            for kt in range(1, KT, 2):
                dve.wait_ge(yt, kt + 1)
                dve.tensor_copy(yT(kt), c.bank[kt % 4][:]).then_inc(yd, 1)


def phase_mixer_out(c, m_):
    nc, t = c.nc, c.t
    with ExitStack() as ctx:
        pT = ctx.enter_context(nc.sbuf_tensor("pT_sb", [P, PLE // P, SEQ], F32))
        npost = ctx.enter_context(nc.sbuf_tensor("npost", [P, D], F32))
        gt = ctx.enter_context(nc.sbuf_tensor("gt", [P, 2, 512], F32))
        (in0, in1, grp, out0, squared, meaned, rooted, s1, s2, xres, turned, out_a, out_d, pg, gg, gsig, xo, stored, step) = signals(
            nc, ctx, "o_in0 o_in1 o_grp o_out o_sq o_mean o_root o_s1 o_s2 o_xres o_turned o_out_a o_out_d o_pg o_gg o_gsig o_xo o_stored o_step")
        block = ctx.enter_context(nc.Block())
        yssdT = m_.xs[:].rearrange("p t d -> p (t d)").rearrange("p (k s) -> p k s", k=KT)
        MX, junk = m_.zs, m_.xbcT
        junk = m_.xbcT[:, 0:KT].rearrange("p a b -> p (a b)").rearrange("p (t d) -> p t d", t=TT)
        GR = 2 * TT

        @block.sync
        def _(sp):
            sp.dma_start(pT[:], t["pT"]).then_inc(in0, 16)
            sp.dma_start(npost[:], t["norm_post"]).then_inc(in1, 16)
            for b in range(B_MIX, NB - RING):
                sp.wait_ge(grp, TT * ((b - B_MIX) // 2 + 1))
                c.load_w(sp, b + RING)
            out = t["out"].rearrange("(t p) d -> p t d", p=P)
            for g in range(GR):
                nh, tt = divmod(g, TT)
                sp.wait_ge(xo, g + 1)
                sp.dma_start(out[:, tt, nh * 512:(nh + 1) * 512], c.X[:, tt, nh * 512:(nh + 1) * 512]).then_inc(stored, 16)
            sp.wait_ge(stored, 16 * GR)

        @block.tensor
        def _(pe):
            for g in range(GR):
                nh, tt = divmod(g, TT)
                if tt == 0:
                    c.wait_w(pe, B_MIX + 2 * nh)
                    c.wait_w(pe, B_MIX + 2 * nh + 1)
                if g >= 4:
                    pe.wait_ge(out0, g - 3)
                for k in range(2 * KT):
                    w = c.w(B_MIX + 2 * nh + k // KT, KT * 512, 512)
                    src = yssdT if k < KT else m_.yscT
                    mm = pe.matmul(c.bank[g % 4][:], src[:, k % KT, tt * P:(tt + 1) * P], w[:, k % KT], start=k == 0, stop=k == 2 * KT - 1)
                mm.then_inc(grp, 1)
            pe.wait_ge(out0, GR)
            transposes_pe(pe, c, c.X, xres, TT, turned, out_a, out_d)
            pe.wait_ge(out_a, KT // 2)
            pe.wait_ge(out_d, KT // 2)
            pe.wait_ge(in0, 16)
            c.wait_w(pe, B_PLE)
            ple = c.w(B_PLE, PLE // P * D, D)
            for g in range(GR):
                nh, tt = divmod(g, TT)
                if tt == 0:
                    c.wait_w(pe, B_GATE + nh)
                if g >= 4:
                    pe.wait_ge(xo, g - 3)
                    pe.wait_ge(gsig, g - 3)
                tok = slice(tt * P, (tt + 1) * P)
                w = c.w(B_GATE + nh, KT * 512, 512)
                for k in range(KT):
                    mm = pe.matmul(c.bank[g % 4][:], c.XT[:, k, tok], w[:, k], start=k == 0, stop=k == KT - 1)
                mm.then_inc(gg, 1)
                for k in range(PLE // P):
                    mm = pe.matmul(c.bank[4 + g % 4][:], pT[:, k, tok], ple[:, k, nh * 512:(nh + 1) * 512], start=k == 0, stop=k == PLE // P - 1)
                mm.then_inc(pg, 1)

        @block.scalar
        def _(act):
            act.wait_ge(out0, GR)
            norm_sums(act, c, MX, junk, squared)
            gains_act(act, c, None, turned, out_a)
            for g in range(GR):
                act.wait_ge(gg, g + 1)
                if g >= 2:
                    act.wait_ge(xo, g - 1)
                act.activation(gt[:, g % 2], c.bank[g % 4][:], ACT.Sigmoid).then_inc(gsig, 1)

        @block.gpsimd
        def _(pool):
            norm_rsqrt(pool, c, squared, TT, meaned, rooted)

        @block.vector
        def _(dve):
            for g in range(GR):
                nh, tt = divmod(g, TT)
                dve.wait_ge(grp, g + 1)
                dve.tensor_copy(MX[:, tt, nh * 512:(nh + 1) * 512], c.bank[g % 4][:]).then_inc(out0, 1)
            dve.wait_ge(rooted, 1)
            dve.wait_ge(in1, 16)
            for tt in range(TT):
                dve.tensor_scalar(MX[:, tt], MX[:, tt], c.rn[:, tt:tt + 1], None, ALU.mult).then_inc(s1, 1)
            for tt in range(TT):
                dve.wait_ge(s1, tt + 1)
                dve.tensor_tensor(MX[:, tt], MX[:, tt], npost[:], ALU.mult).then_inc(s2, 1)
            for tt in range(TT):
                dve.wait_ge(s2, tt + 1)
                dve.tensor_tensor(c.X[:, tt], c.X[:, tt], MX[:, tt], ALU.add).then_inc(xres, 1)
            gains_dve(dve, c, None, turned, out_d)
            for g in range(GR):
                nh, tt = divmod(g, TT)
                xs = c.X[:, tt, nh * 512:(nh + 1) * 512]
                dve.wait_ge(pg, g + 1)
                dve.wait_ge(gsig, g + 1)
                dve.tensor_tensor(gt[:, g % 2], c.bank[4 + g % 4][:], gt[:, g % 2], ALU.mult).then_inc(step, 1)
                dve.wait_ge(step, g + 1)
                dve.tensor_tensor(xs, xs, gt[:, g % 2], ALU.add).then_inc(xo, 1)


class Attention:
    def __init__(self, nc, ctx):
        sb = lambda name, shape: ctx.enter_context(nc.sbuf_tensor(name, shape, F32))
        self.y = sb("y", [P, TT, 2 * ATT_W])
        self.qz = sb("qz", [P, HEADS, SEQ])
        self.kT = sb("kT", [P, HEADS // 2, SEQ])
        self.va = sb("va", [P, TT, ATT_W])
        self.qzb = sb("qzb", [P, HEADS, SEQ])
        self.kTb = sb("kTb", [P, SEQ])
        self.vb = sb("vb", [P, TT, KV_HEADS * DH])


def build(nc, t, upto=99):
    with ExitStack() as ctx:
        c = Core(nc, ctx, t)
        with ExitStack() as att:
            a = Attention(nc, att)
            phase_project(c, a)
            if upto >= 2:
                phase_attend(c, a)
            if upto >= 3:
                phase_merge(c, a)
        if upto >= 4:
            with ExitStack() as tmp:
                ijg = tmp.enter_context(nc.sbuf_tensor("ijg", [P, 3, SEQ], F32))
                phase_choose(c, ijg)
                if upto >= 5:
                    phase_gates(c, ijg)
        if upto >= 6:
            phase_experts(c)
        if upto >= 7:
            phase_between(c)
        if upto >= 8:
            with ExitStack() as mix:
                m_ = Mixer(nc, mix)
                phase_mixer_in(c, m_)
                if upto >= 9:
                    phase_scan(c, m_)
                if upto >= 10:
                    phase_mixer_out(c, m_)
        if upto < 10:
            dumped = ctx.enter_context(nc.semaphore("dumped"))
            with nc.Block() as block:
                @block.sync
                def _(sp):
                    sp.dma_start(t["out"].rearrange("(t p) d -> p t d", p=P), c.X[:] if upto != 1 else c.XT[:].rearrange("p a b -> p (a b)").rearrange("p (t d) -> p t d", t=TT)).then_inc(dumped, 16)
                    sp.wait_ge(dumped, 16)



def _rows(w, cols, k=None):
    w = w[:, cols]
    return w.reshape(w.shape[0] // P, P, w.shape[1]).transpose(1, 0, 2)


def _tables():
    tab = np.zeros((P, NTAB), np.float32)
    tab[:, T_ID:T_ID + P] = np.eye(P)
    tab[:, T_TRI:T_TRI + P] = np.triu(np.ones((P, P)))
    tab[:, T_IOTA:T_IOTA + P] = np.arange(P)
    nf = DH // 4
    inv = (np.float32(ROPE_THETA) ** (-np.arange(nf, dtype=np.float32) / np.float32(nf))).astype(np.float32)
    tok = np.arange(SEQ)
    for s, pos in enumerate((tok // GRID_W, tok % GRID_W)):
        ang = pos.astype(np.float32)[:, None] * inv[None, :]
        co, si = np.cos(ang).astype(np.float32), np.sin(ang).astype(np.float32)
        for f in range(2):
            at = s * 2 * nf + f * nf
            for tt in range(TT):
                rows = slice(tt * P, (tt + 1) * P)
                tab[:, T_COS + tt * DH + at:T_COS + tt * DH + at + nf] = co[rows]
                tab[:, T_SIN + tt * DH + at:T_SIN + tt * DH + at + nf] = si[rows] * (1 if f else -1)
    return tab


def _bias(rpb):
    q = np.arange(GRID_W)
    start = np.clip(q - WIN_W // 2, 0, GRID_W - WIN_W)
    k = np.arange(GRID_W)
    inside = (k[None] >= start[:, None]) & (k[None] < start[:, None] + WIN_W)
    dc = np.clip(k[None] - q[:, None], -(WIN_W - 1), WIN_W - 1) + WIN_W - 1
    out = np.full((HEADS, 2, GRID_W, BIAS_ROWS, GRID_W), NEG, np.float32)
    for par in range(2):
        for j in range(BIAS_ROWS):
            dr = j - par
            if 0 <= dr < 2 * WIN_H - 1:
                out[:, par, :, j, :] = np.where(inside[None], rpb[:, dr][:, dc], np.float32(NEG))
    return out.reshape(HEADS, P, BIAS_ROWS * GRID_W)


def pack(x, norm1_g, w_in, na_rpb, gqa_q_norm_g, gqa_k_norm_g, w_proj_a, w_proj_b, w_out, norm2_g,
         peer_w_q, peer_sub_keys, peer_u, peer_v, norm_f_g, p_2, norm_pre_2, norm_post_2, w_in_2,
         ssd_conv_w_2, ssd_conv_b_2, dt_bias_2, a_log_2, d_skip_2, ssd_norm_2, sc_conv_w_2, w_out_2,
         w_ple_gate_2, w_ple_proj_2):
    w_in, w2 = w_in[0], w_in_2[0]
    blocks = np.zeros((NB, P, WBLK), np.float32)

    def put(b, *parts):
        at = 0
        for w in parts:
            n = w.shape[1] * w.shape[2]
            blocks[b, :, at:at + n] = w.reshape(P, n)
            at += n

    cut = lambda a, n: slice(a, a + n)
    for b in range(4):
        put(b, _rows(w_in, cut(512 * b, 512)))
    put(B_KVB, _rows(w_in, cut(2048, 256)))
    for m in range(KT):
        put(B_MERGE + m, _rows(w_in, cut(2304 + P * m, P)), _rows(w_in, cut(3328 + P * m, P)),
            _rows(w_proj_a[0], cut(P * m, P)), _rows(w_proj_b[0], cut(P * m, P)))
        s0 = (D + 2 * SG * NS) + SH + D
        put(B_SC + m, *[_rows(w2, cut(s0 + D * j + P * m, P)) for j in (2, 0, 1, 3)])
    for b in range(2):
        put(B_OUT + b, _rows(w_out[0], cut(512 * b, 512)))
        put(B_Z + b, _rows(w2, cut(D + 2 * SG * NS + SH + 512 * b, 512)))
        put(B_GATE + b, _rows(w_ple_gate_2[0], cut(512 * b, 512)))
        for k in range(2):
            put(B_MIX + 2 * b + k, _rows(w_out_2[0][D * k:D * (k + 1)], cut(512 * b, 512)))
    for b in range(4):
        put(B_PQ + b, _rows(peer_w_q[0], cut(512 * b, 512)))
    put(B_KEYS, peer_sub_keys[0].reshape(2 * PH, PK, P).transpose(2, 0, 1))
    for b in range(3):
        put(B_XBC + b, _rows(w2, cut(512 * b, min(512, XBC_TILES * P - 512 * b))))
    put(B_DT, _rows(w2, cut(D + 2 * SG * NS, SH)))
    put(B_PLE, _rows(w_ple_proj_2[0], cut(0, D)))

    col = lambda v: v.reshape(-1, P).T
    cols = np.zeros((P, NCOL), np.float32)
    for at, v in ((C_G1, norm1_g[0]), (C_G2, norm2_g[0]), (C_GPRE, norm_pre_2[0]), (C_CB, ssd_conv_b_2[0])):
        cols[:, at:at + v.size // P] = col(v)
    cols[:, C_CW:C_CB] = ssd_conv_w_2[0].reshape(CONV_W, XBC_TILES, P).transpose(2, 1, 0).reshape(P, -1)
    cols[:, C_SW:NCOL] = sc_conv_w_2[0].reshape(SC_W, KT, P).transpose(2, 1, 0).reshape(P, -1)
    row = np.concatenate([np.tile(gqa_q_norm_g[0], HEADS), np.tile(gqa_k_norm_g[0], KV_HEADS), dt_bias_2[0], a_log_2[0], d_skip_2[0]])
    wide = lambda v: np.ascontiguousarray(np.broadcast_to(v.reshape(1, -1), (P, v.size)))
    return {
        "x": x[0], "tab": _tables(), "cols": cols, "rows": wide(row), "bias": _bias(na_rpb[0]),
        "w_stream": blocks,
        "u": peer_u[0].reshape(NG, EG * P, KT, P).transpose(0, 3, 2, 1),
        "v": peer_v[0].reshape(NG, EG, P, D),
        "norm_f": wide(norm_f_g), "norm_post": wide(norm_post_2[0]), "ssd_norm": wide(ssd_norm_2[0]),
        "pT": p_2[0, 0].T.reshape(PLE // P, P, SEQ).transpose(1, 0, 2),
    }


def kernel(**inputs):
    import concourse.bacc as bacc
    from concourse.bass_utils import run_bass_kernel_spmd

    nc = bacc.Bacc("TRN2", target_bir_lowering=False, num_devices=1)
    arrays, tensors = {}, {}
    for name, a in pack(**{k: np.asarray(v) for k, v in inputs.items()}).items():
        a = np.ascontiguousarray(a)
        arrays[f"in_{name}"] = a
        tensors[name] = nc.dram_tensor(f"in_{name}", a.shape, mybir.dt.from_np(a.dtype), kind="ExternalInput").ap()
    tensors["gates"] = nc.dram_tensor("gates", (PK, PK, SEQ), F32).ap()
    tensors["out"] = nc.dram_tensor("out_x", (SEQ, D), F32, kind="ExternalOutput").ap()
    build(nc, tensors)
    r = run_bass_kernel_spmd(nc, [arrays], core_ids=[0])
    return r.results[0]["out_x"].reshape(1, SEQ, D)
```

```python
from contextlib import ExitStack

import numpy as np

import concourse.bass as bass
from concourse import mybir

F32 = mybir.dt.float32
F32R = mybir.dt.float32r
U32 = mybir.dt.uint32
ALU = mybir.AluOpType
ACT = mybir.ActivationFunctionType
AX = mybir.AxisListType.X

P = 128
SEQ = 512
TT = SEQ // P
D = 1024
KT = D // P
EPS = 1e-6
GRID_W = 64
DH = 64
HEADS = 8
WIN_H, WIN_W = 8, 16
ATT_W = HEADS * DH
KV_HEADS = 2
BIAS_ROWS = 2 * WIN_H
ROPE_THETA = 10000.0

PK = 128
PH = 8
TOPK = 16
EXPERTS = PK * PK
SLOTS = PH * TOPK
EG = 4
NG = PK // EG
E_CHOOSE, E_GATES, E_STORE = PK // 4, PK // 4, 8
EARLY = E_CHOOSE + E_GATES + E_STORE

SH = 16
SP_ = 64
SG = 2
HG = SH // SG
NS = 64
CONV_W, SC_W = 4, 3
XBC_TILES = (D + 2 * SG * NS) // P
PLE = 256

NEG = -1.0e30
LOWEST = -3.4028235e38

WBLK = 4096
RING = 3
B_QA, B_KA, B_VA, B_QB, B_KVB = range(5)
B_MERGE = 5
B_OUT = B_MERGE + KT
B_PQ = B_OUT + 2
B_KEYS = B_PQ + 4
B_XBC = B_KEYS + 1
B_DT = B_XBC + 3
B_Z = B_DT + 1
B_SC = B_Z + 2
B_MIX = B_SC + KT
B_PLE = B_MIX + 4
B_GATE = B_PLE + 1
NB = B_GATE + 2

C_G1, C_G2, C_GPRE = 0, KT, 2 * KT
C_CW = 3 * KT
C_CB = C_CW + XBC_TILES * CONV_W
C_SW = C_CB + XBC_TILES
NCOL = C_SW + KT * SC_W
T_ID, T_TRI, T_IOTA, T_COS = 0, P, 2 * P, 3 * P
T_SIN = T_COS + TT * DH
NTAB = T_SIN + TT * DH
R_GQK = 0
R_DTB = R_GQK + ATT_W + KV_HEADS * DH
R_ALOG = R_DTB + SH
R_DSK = R_ALOG + SH
NROW = R_DSK + SH


def bc(ap, n):
    return ap.unsqueeze(len(ap.shape)).broadcast_to(list(ap.shape) + [n])


def mid(ap, n):
    return ap.unsqueeze(1).broadcast_to([ap.shape[0], n, ap.shape[1]])


class Core:

    def __init__(self, nc, ctx, t):
        self.nc, self.t = nc, t
        sb = lambda name, shape, dt=F32: ctx.enter_context(nc.sbuf_tensor(name, shape, dt))
        self.X = sb("x_res", [P, TT, D])
        self.XT = sb("XT", [P, KT, SEQ])
        self.tab = sb("tab_sb", [P, NTAB])
        self.cols = sb("cols_sb", [P, NCOL])
        self.rows = sb("rows_sb", [P, NROW])
        self.ss = sb("ss", [P, TT])
        self.ms = sb("ms", [P, TT])
        self.rn = sb("rn", [P, TT])
        self.half = sb("half", [P, 48])
        self.bank = [ctx.enter_context(nc.psum_tensor(f"bank{i}", [P, 512], F32)) for i in range(8)]
        self.w_loaded = [ctx.enter_context(nc.semaphore(f"w_loaded{i}")) for i in range(RING)]
        self.ur = sb("ur", [P, 2, KT * P])
        self.ar = sb("ar", [P, 2, SEQ])
        self.squared, self.meaned, self.rooted, self.scaled, self.turned, self.out_a, self.out_d = signals(
            nc, ctx, "squared meaned rooted scaled turned out_a out_d")
        self.ident = self.tab[:, T_ID:T_ID + P]
        self.tri = self.tab[:, T_TRI:T_TRI + P]
        self.iota = self.tab[:, T_IOTA:T_IOTA + P]

    def ring(self, ctx, name):
        self.W = ctx.enter_context(self.nc.sbuf_tensor(name, [P, RING, WBLK], F32))

    def w(self, b, n, cols=P):
        return self.W[:, b % RING, 0:n].rearrange("p (k c) -> p k c", c=cols)

    def load_w(self, sp, b):
        sp.dma_start(self.W[:, b % RING, :], self.t["w_stream"][b]).then_inc(self.w_loaded[b % RING], 16)

    def wait_w(self, pe, b):
        pe.wait_ge(self.w_loaded[b % RING], 16 * (b // RING + 1))


def signals(nc, ctx, names):
    return [ctx.enter_context(nc.semaphore(n)) for n in names.split()]



N_FIRST, N_EXPERTS, N_FINAL, N_PRE, N_POST = range(5)


def norm_sums(act, c, src, junk):
    for tt in range(TT):
        act.activation(junk[:, tt], src[:, tt], ACT.Square, accum_out=c.ss[:, tt:tt + 1]).then_inc(c.squared, 1)


def norm_rsqrt(pool, c, n):
    pool.wait_ge(c.squared, (n + 1) * TT)
    pool.tensor_scalar(c.ms[:], c.ss[:], 1.0 / D, EPS, ALU.mult, ALU.add).then_inc(c.meaned, 1)
    pool.wait_ge(c.meaned, n + 1)
    pool.tensor_tensor(c.rn[:], c.ms[:], c.half[:, 0:TT], ALU.pow).then_inc(c.rooted, 1)


T_FIRST, T_EXPERTS, T_PRE, T_POST = range(4)


def transposes_pe(pe, c, src, n):
    pe.wait_ge(c.scaled, (n + 1) * TT)
    for kt in range(KT):
        if kt >= 4:
            pe.wait_ge(c.out_d if kt % 2 else c.out_a, n * KT // 2 + kt // 2 - 1)
        for tt in range(TT):
            mm = pe.transpose(c.bank[kt % 4][:, tt * P:(tt + 1) * P], src[:, tt, kt * P:(kt + 1) * P], c.ident)
        mm.then_inc(c.turned, 1)


def transposed_pe(pe, c, n):
    pe.wait_ge(c.out_a, (n + 1) * KT // 2)
    pe.wait_ge(c.out_d, (n + 1) * KT // 2)


def gains_act(act, c, col, n):
    for kt in range(0, KT, 2):
        act.wait_ge(c.turned, n * KT + kt + 1)
        act.activation(c.XT[:, kt], c.bank[kt % 4][:], ACT.Copy, scale=1.0 if col is None else c.cols[:, col + kt:col + kt + 1]).then_inc(c.out_a, 1)


def gains_dve(dve, c, col, n):
    for kt in range(1, KT, 2):
        dve.wait_ge(c.turned, n * KT + kt + 1)
        gain = 1.0 if col is None else c.cols[:, col + kt:col + kt + 1]
        dve.tensor_scalar(c.XT[:, kt], c.bank[kt % 4][:], gain, None, ALU.mult).then_inc(c.out_d, 1)


def phase_project(c, a):
    nc, t = c.nc, c.t
    with ExitStack() as ctx:
        HN = ctx.enter_context(nc.sbuf_tensor("HN", [P, TT, D], F32))
        QK = ctx.enter_context(nc.sbuf_tensor("QK", [P, TT, ATT_W + P], F32))
        S1 = ctx.enter_context(nc.sbuf_tensor("S1", [P, TT, ATT_W + P], F32))
        S2 = ctx.enter_context(nc.sbuf_tensor("S2", [P, TT, ATT_W + P], F32))
        KR = a.y[:, :, 0:P]
        hs = ctx.enter_context(nc.sbuf_tensor("hs", [P, 3, 40], F32))
        (x0, x1, x2, x3, tab_in, col_in, row_in, hmean, grp, grp_a, grp_d,
         set0, step, hsum, hroot, roped, rturn, rout, rout_d) = signals(
            nc, ctx, "x_in0 x_in1 x_in2 x_in3 tab_in col_in row_in hmean grp grp_a grp_d "
            "set0 step hsum hroot roped rturn rout rout_d")
        x_in = (x0, x1, x2, x3)
        qpad = HN[:].rearrange("p t (h w) -> p t h w", w=P)
        block = ctx.enter_context(nc.Block())
        GROUPS = 2 * TT + 3 * TT
        HR = HEADS + KV_HEADS

        def project_out(g, copy, sem):
            src = c.bank[4 + g % 4]
            if g < 4:
                copy(a.qz[0:64, 2 * g], src[0:64, :], DH ** -0.5)
                copy(a.qz[64:128, 2 * g + 1], src[64:128, :], DH ** -0.5).then_inc(sem, 1)
            elif g < 8:
                copy(a.kT[:, g - 4], src[:], 1.0).then_inc(sem, 1)
            elif g < 12:
                copy(a.va[:, g - 8], src[:], 1.0).then_inc(sem, 1)
            elif g < 16:
                copy(QK[:, g - 12, 0:ATT_W], src[:], 1.0).then_inc(sem, 1)
            else:
                copy(QK[:, g - 16, ATT_W:], src[:, 0:P], 1.0)
                copy(a.vb[:, g - 16], src[:, P:2 * P], 1.0).then_inc(sem, 1)

        @block.sync
        def _(sp):
            for tt in range(TT):
                sp.dma_start(c.X[:, tt], t["x"][tt * P:(tt + 1) * P, :]).then_inc(x_in[tt], 16)
            sp.dma_start(c.tab[:], t["tab"]).then_inc(tab_in, 16)
            sp.dma_start(c.cols[:], t["cols"]).then_inc(col_in, 16)
            for b in range(RING):
                c.load_w(sp, b)
            sp.dma_start(c.rows[:], t["rows"]).then_inc(row_in, 16)
            for b in range(5):
                sp.wait_ge(grp, 4 * (b + 1))
                c.load_w(sp, b + RING)

        @block.scalar
        def _(act):
            for tt in range(TT):
                act.wait_ge(x_in[tt], 16)
                act.activation(HN[:, tt], c.X[:, tt], ACT.Square, accum_out=c.ss[:, tt:tt + 1]).then_inc(c.squared, 1)
            act.wait_ge(col_in, 16)
            gains_act(act, c, C_G1, T_FIRST)
            for g in range(0, GROUPS, 2):
                act.wait_ge(grp, g + 1)
                if g == 0:
                    act.wait_ge(set0, 2)
                project_out(g, lambda o, i, s: act.activation(o, i, ACT.Copy, scale=s), grp_a)
            for h in range(0, HEADS, 2):
                act.wait_ge(rturn, h + 1)
                act.activation(a.qzb[:, h], c.bank[h % 4][:], ACT.Copy, scale=DH ** -0.5).then_inc(rout, 1)
            act.wait_ge(rturn, HEADS + 1)
            act.activation(a.kTb, c.bank[HEADS % 4][:], ACT.Copy).then_inc(rout, 1)

        @block.gpsimd
        def _(pool):
            pool.memset(c.half[:], -0.5).then_inc(set0, 1)
            pool.memset(a.qz[:], 0.0).then_inc(set0, 1)
            pool.wait_ge(set0, 2)
            norm_rsqrt(pool, c, N_FIRST)
            pool.wait_ge(c.turned, KT)
            pool.memset(HN[:], 0.0).then_inc(set0, 1)
            pool.wait_ge(hsum, 1)
            pool.tensor_scalar(hs[:, 1], hs[:, 0], 1.0 / DH, EPS, ALU.mult, ALU.add).then_inc(hmean, 1)
            pool.wait_ge(hmean, 1)
            pool.tensor_tensor(hs[:, 2], hs[:, 1], c.half[:, 0:40], ALU.pow).then_inc(hroot, 1)

        @block.vector
        def _(dve):
            dve.wait_ge(c.rooted, N_FIRST + 1)
            for tt in range(TT):
                dve.wait_ge(x_in[tt], 16)
                dve.tensor_scalar(HN[:, tt], c.X[:, tt], c.rn[:, tt:tt + 1], None, ALU.mult).then_inc(c.scaled, 1)
            dve.wait_ge(col_in, 16)
            gains_dve(dve, c, C_G1, T_FIRST)
            dve.wait_ge(set0, 2)
            for g in range(1, GROUPS, 2):
                dve.wait_ge(grp, g + 1)
                project_out(g, lambda o, i, s: dve.tensor_scalar(o, i, s, None, ALU.mult), grp_d)
            n = [0]

            def link(ins):
                n[0] += 1
                ins.then_inc(step, 1)
                dve.wait_ge(step, n[0])

            dve.wait_ge(grp_a, GROUPS // 2)
            dve.wait_ge(grp_d, GROUPS // 2)
            flat = lambda x: x[:].rearrange("p t w -> p (t w)")
            heads = lambda x: x[:].rearrange("p t (h w) -> p (t h) w", w=DH)
            link(dve.tensor_tensor(flat(S1), flat(QK), flat(QK), ALU.mult))
            dve.tensor_reduce(hs[:, 0], heads(S1), AX, ALU.add).then_inc(hsum, 1)
            dve.wait_ge(hroot, 1)
            link(dve.tensor_tensor(heads(S1), heads(QK), bc(hs[:, 2], DH), ALU.mult))
            dve.wait_ge(row_in, 16)
            link(dve.tensor_tensor(QK[:], S1[:], mid(c.rows[:, R_GQK:R_GQK + ATT_W + P], TT), ALU.mult))
            for tt in range(TT):
                cos = mid(c.tab[:, T_COS + tt * DH:T_COS + (tt + 1) * DH], HR)
                dve.tensor_tensor(S1[:, tt].rearrange("p (h w) -> p h w", w=DH), QK[:, tt].rearrange("p (h w) -> p h w", w=DH), cos, ALU.mult)
                halves = lambda x: x.rearrange("p (h s f w) -> p h s f w", s=2, f=2, w=DH // 4)
                sin = c.tab[:, T_SIN + tt * DH:T_SIN + (tt + 1) * DH].rearrange("p (s f w) -> p s f w", s=2, f=2)
                for f in range(2):
                    s_f = sin[:, :, f].unsqueeze(1).broadcast_to([P, HR, 2, DH // 4])
                    last = dve.tensor_tensor(halves(S2[:, tt])[:, :, :, f], halves(QK[:, tt])[:, :, :, 1 - f], s_f, ALU.mult)
            link(last)
            dve.wait_ge(set0, 3)
            for tt in range(TT):
                for n0 in range(KV_HEADS):
                    o = qpad[:, tt, 4 * n0:4 * n0 + 4, 64 * n0:64 * n0 + 64]
                    cut = slice(256 * n0, 256 * n0 + 256)
                    dve.tensor_tensor(o, S1[:, tt, cut].rearrange("p (h w) -> p h w", w=DH),
                                      S2[:, tt, cut].rearrange("p (h w) -> p h w", w=DH), ALU.add)
                last = dve.tensor_tensor(KR[:, tt], S1[:, tt, ATT_W:], S2[:, tt, ATT_W:], ALU.add)
            last.then_inc(roped, 1)
            for h in range(1, HEADS, 2):
                dve.wait_ge(rturn, h + 1)
                dve.tensor_scalar(a.qzb[:, h], c.bank[h % 4][:], DH ** -0.5, None, ALU.mult).then_inc(rout_d, 1)

        @block.tensor
        def _(pe):
            pe.wait_ge(tab_in, 16)
            transposes_pe(pe, c, HN, T_FIRST)
            transposed_pe(pe, c, T_FIRST)
            for g in range(GROUPS):
                ps = c.bank[4 + g % 4]
                if g % 4 == 0:
                    c.wait_w(pe, g // 4)
                if g >= 4:
                    pe.wait_ge(grp_d if g % 2 else grp_a, g // 2 - 1)
                if g < 8:
                    w = c.w(g // 4, KT * 512, 512)
                    for k in range(KT):
                        mm = pe.matmul(ps[:], w[:, k, (g % 4) * P:(g % 4 + 1) * P], c.XT[:, k], start=k == 0, stop=k == KT - 1)
                else:
                    width = 512 if g < 16 else 256
                    w, tt = c.w(g // 4, KT * width, width), g % 4
                    for k in range(KT):
                        mm = pe.matmul(ps[:, 0:width], c.XT[:, k, tt * P:(tt + 1) * P], w[:, k], start=k == 0, stop=k == KT - 1)
                mm.then_inc(grp, 1)
            pe.wait_ge(roped, 1)
            for h in range(HEADS + 1):
                if h >= 4:
                    pe.wait_ge(rout_d if h % 2 else rout, h // 2 - 1)
                for tt in range(TT):
                    src = qpad[:, tt, h] if h < HEADS else KR[:, tt]
                    mm = pe.transpose(c.bank[h % 4][:, tt * P:(tt + 1) * P], src, c.ident)
                mm.then_inc(rturn, 1)


def phase_attend(c, a):
    nc, t = c.nc, c.t
    UNITS = 2 * HEADS * TT
    PR = 4
    with ExitStack() as ctx:
        Pr = ctx.enter_context(nc.sbuf_tensor("Pr", [P, PR, SEQ], F32))
        PT = ctx.enter_context(nc.sbuf_tensor("PT", [P, PR, TT, P], F32))
        bias = ctx.enter_context(nc.sbuf_tensor("bias_sb", [P, 2, BIAS_ROWS * GRID_W], F32))
        mx = ctx.enter_context(nc.sbuf_tensor("mx", [P, UNITS], F32))
        nm = ctx.enter_context(nc.sbuf_tensor("nm", [P, UNITS], F32))
        rs = ctx.enter_context(nc.sbuf_tensor("rs", [P, UNITS], F32))
        ri = ctx.enter_context(nc.sbuf_tensor("ri", [P, UNITS], F32))
        scored, maxed, negated, expd, turned, pt_a, pt_d, weighed, inverted, y_out, b0, b1 = signals(
            nc, ctx, "scored maxed negated expd turned2 pt_a pt_d weighed inverted y_out bias_in0 bias_in1")
        bias_in = (b0, b1)
        block = ctx.enter_context(nc.Block())
        psS, psT, psY = c.bank[0:3], c.bank[3:6], c.bank[6:8]

        @block.sync
        def _(sp):
            for h in range(HEADS):
                if h >= 2:
                    sp.wait_ge(negated, TT * (h - 1))
                sp.dma_start(bias[:, h % 2], t["bias"][h]).then_inc(bias_in[h % 2], 16)

        def pt_copied(eng, u):
            eng.wait_ge(pt_d if u % 2 else pt_a, u // 2 + 1)

        @block.tensor
        def _(pe):
            for i in range(UNITS + 3):
                if i < UNITS:
                    h, q = divmod(i, TT)
                    if i >= 3:
                        pe.wait_ge(expd, i - 2)
                    if h < HEADS:
                        qT, kT = a.qz[:, h], a.kT[:, h // 2]
                    else:
                        qT, kT = a.qzb[:, h - HEADS], a.kTb[:]
                    pe.matmul(psS[i % 3][:], qT[:, q * P:(q + 1) * P], kT, start=True, stop=True).then_inc(scored, 1)
                u = i - 2
                if 0 <= u < UNITS:
                    pe.wait_ge(expd, u + 1)
                    if u >= 3:
                        pt_copied(pe, u - 3)
                    for kt in range(TT):
                        mm = pe.transpose(psT[u % 3][:, kt * P:(kt + 1) * P], Pr[:, u % PR, kt * P:(kt + 1) * P], c.ident)
                    mm.then_inc(turned, 1)
                u = i - 3
                if 0 <= u < UNITS:
                    h, q = divmod(u, TT)
                    pt_copied(pe, u)
                    if q == 0 and h >= 2:
                        pe.wait_ge(y_out, h - 1)
                    for kt in range(TT):
                        v = a.va[:, kt, h * DH:(h + 1) * DH] if h < HEADS else \
                            a.vb[:, kt, (h - HEADS) // 4 * DH:((h - HEADS) // 4 + 1) * DH]
                        mm = pe.matmul(psY[h % 2][:, q * DH:(q + 1) * DH], PT[:, u % PR, kt], v, start=kt == 0, stop=kt == TT - 1)
                    mm.then_inc(weighed, 1)

        @block.vector
        def _(dve):
            for i in range(UNITS + 4):
                u = i - 3
                if 0 <= u < UNITS and u % 2:
                    dve.wait_ge(turned, u + 1)
                    if u >= PR:
                        dve.wait_ge(weighed, u - PR + 1)
                    dve.tensor_copy(PT[:, u % PR].rearrange("p a b -> p (a b)"), psT[u % 3][:]).then_inc(pt_d, 1)
                if i < UNITS:
                    h, q = divmod(i, TT)
                    dve.wait_ge(scored, i + 1)
                    if h < HEADS:
                        if q == 0:
                            dve.wait_ge(bias_in[h % 2], 16 * (h // 2 + 1))
                        if i >= PR:
                            dve.wait_ge(turned, i - PR + 1)
                        r0 = (WIN_H - 1 - 2 * q) * GRID_W
                        dve.tensor_tensor_reduce(Pr[:, i % PR], psS[i % 3][:], bias[:, h % 2, r0:r0 + SEQ], 1.0, LOWEST,
                                                 ALU.add, ALU.max, mx[:, i:i + 1]).then_inc(maxed, 1)
                        dve.wait_ge(maxed, i + 1)
                        dve.tensor_scalar(nm[:, i:i + 1], mx[:, i:i + 1], -1.0, None, ALU.mult).then_inc(negated, 1)
                    else:
                        dve.tensor_reduce(nm[:, i:i + 1], psS[i % 3][:], AX, ALU.max, negate=True).then_inc(negated, 1)
                u = i - 4
                if u >= 0 and u % TT == TT - 1:
                    h = u // TT
                    dve.wait_ge(expd, TT * (h + 1))
                    dve.reciprocal(ri[:, TT * h:TT * (h + 1)], rs[:, TT * h:TT * (h + 1)]).then_inc(inverted, 1)
                    dve.wait_ge(inverted, h + 1)
                    dve.wait_ge(weighed, TT * (h + 1))
                    dve.tensor_tensor(a.y[:, :, h * DH:(h + 1) * DH], psY[h % 2][:, 0:TT * DH].rearrange("p (t w) -> p t w", w=DH),
                                      bc(ri[:, TT * h:TT * (h + 1)], DH), ALU.mult).then_inc(y_out, 1)

        @block.scalar
        def _(act):
            for i in range(UNITS + 3):
                u = i - 3
                if 0 <= u < UNITS and u % 2 == 0:
                    act.wait_ge(turned, u + 1)
                    if u >= PR:
                        act.wait_ge(weighed, u - PR + 1)
                    act.activation(PT[:, u % PR].rearrange("p a b -> p (a b)"), psT[u % 3][:], ACT.Copy).then_inc(pt_a, 1)
                if i < UNITS:
                    act.wait_ge(negated, i + 1)
                    if i >= PR and i >= HEADS * TT:
                        act.wait_ge(turned, i - PR + 1)
                    src = Pr[:, i % PR] if i < HEADS * TT else psS[i % 3][:]
                    act.activation(Pr[:, i % PR], src, ACT.Exp, bias=nm[:, i:i + 1], accum_out=rs[:, i:i + 1]).then_inc(expd, 1)


def phase_merge(c, a):
    nc = c.nc
    with ExitStack() as ctx:
        yT = ctx.enter_context(nc.sbuf_tensor("yT", [P, KT, SEQ], F32))
        mT = ctx.enter_context(nc.sbuf_tensor("mT", [P, KT, SEQ], F32))
        sg = ctx.enter_context(nc.sbuf_tensor("sg", [P, 2, 2, SEQ], F32))
        (turned, out_a, out_d, grp, gated, halfd, merged, xg, added) = signals(
            nc, ctx, "m_turned m_out_a m_out_d m_grp gated halved merged x_grp x_added")
        block = ctx.enter_context(nc.Block())

        yT_as_rows = yT[:].rearrange("p a b -> p (a b)").rearrange("p (t d) -> p t d", t=TT)
        junk = mT[:].rearrange("p a b -> p (a b)").rearrange("p (t d) -> p t d", t=TT)

        @block.sync
        def _(sp):
            for b in range(5, B_PQ):
                if b < B_OUT:
                    sp.wait_ge(grp, 4 * (b - B_MERGE + 1))
                else:
                    sp.wait_ge(xg, 4 * (b - B_OUT + 1))
                c.load_w(sp, b + RING)

        @block.tensor
        def _(pe):
            for kt in range(KT):
                if kt >= 4:
                    pe.wait_ge(out_d if kt % 2 else out_a, kt // 2 - 1)
                for tt in range(TT):
                    mm = pe.transpose(c.bank[kt % 4][:, tt * P:(tt + 1) * P], a.y[:, tt, kt * P:(kt + 1) * P], c.ident)
                mm.then_inc(turned, 1)
            pe.wait_ge(out_a, KT // 2)
            pe.wait_ge(out_d, KT // 2)
            for m in range(KT):
                bk = c.bank[4 * (m % 2):4 * (m % 2) + 4]
                c.wait_w(pe, B_MERGE + m)
                w = c.w(B_MERGE + m, 24 * P)
                if m >= 2:
                    pe.wait_ge(gated, 2 * (m - 1))
                    pe.wait_ge(halfd, 2 * (m - 1))
                for j, (w0, n, src) in enumerate(((0, KT, c.XT), (KT, KT, c.XT), (2 * KT, 4, yT[:, 0:4]), (2 * KT + 4, 4, yT[:, 4:8]))):
                    for k in range(n):
                        mm = pe.matmul(bk[j][:], w[:, w0 + k], src[:, k], start=k == 0, stop=k == n - 1)
                    mm.then_inc(grp, 1)
            pe.wait_ge(merged, KT)
            for g in range(2 * TT):
                nh, tt = divmod(g, TT)
                if tt == 0:
                    c.wait_w(pe, B_OUT + nh)
                if g >= 4:
                    pe.wait_ge(added, g - 3)
                w = c.w(B_OUT + nh, KT * 512, 512)
                for k in range(KT):
                    mm = pe.matmul(c.bank[g % 4][:], mT[:, k, tt * P:(tt + 1) * P], w[:, k], start=k == 0, stop=k == KT - 1)
                mm.then_inc(xg, 1)
            pe.wait_ge(added, 2 * TT)
            transposes_pe(pe, c, yT_as_rows, T_EXPERTS)

        @block.scalar
        def _(act):
            for kt in range(0, KT, 2):
                act.wait_ge(turned, kt + 1)
                act.activation(yT[:, kt], c.bank[kt % 4][:], ACT.Copy).then_inc(out_a, 1)
            for m in range(KT):
                for j in range(2):
                    act.wait_ge(grp, 4 * m + j + 1)
                    if m >= 2:
                        act.wait_ge(merged, m - 1)
                    act.activation(sg[:, m % 2, j], c.bank[4 * (m % 2) + j][:], ACT.Sigmoid).then_inc(gated, 1)
            act.wait_ge(added, 2 * TT)
            norm_sums(act, c, c.X, junk)
            gains_act(act, c, C_G2, T_EXPERTS)

        @block.gpsimd
        def _(pool):
            norm_rsqrt(pool, c, N_EXPERTS)

        @block.vector
        def _(dve):
            for kt in range(1, KT, 2):
                dve.wait_ge(turned, kt + 1)
                dve.tensor_copy(yT[:, kt], c.bank[kt % 4][:]).then_inc(out_d, 1)
            for m in range(KT):
                for j in range(2):
                    dve.wait_ge(grp, 4 * m + 3 + j)
                    dve.wait_ge(gated, 2 * m + j + 1)
                    dve.tensor_tensor(sg[:, m % 2, j], c.bank[4 * (m % 2) + 2 + j][:], sg[:, m % 2, j], ALU.mult).then_inc(halfd, 1)
                dve.wait_ge(halfd, 2 * (m + 1))
                dve.tensor_tensor(mT[:, m], sg[:, m % 2, 0], sg[:, m % 2, 1], ALU.add).then_inc(merged, 1)
            for g in range(2 * TT):
                nh, tt = divmod(g, TT)
                dve.wait_ge(xg, g + 1)
                xs = c.X[:, tt, nh * 512:(nh + 1) * 512]
                dve.tensor_tensor(xs, c.bank[g % 4][:], xs, ALU.add).then_inc(added, 1)
            dve.wait_ge(c.rooted, N_EXPERTS + 1)
            for tt in range(TT):
                dve.tensor_scalar(yT_as_rows[:, tt], c.X[:, tt], c.rn[:, tt:tt + 1], None, ALU.mult).then_inc(c.scaled, 1)
            gains_dve(dve, c, C_G2, T_EXPERTS)


class Early:

    def __init__(self, c, ctx):
        self.c = c
        i0, i1, self.done, self.gelud, k0, k1 = signals(c.nc, ctx, "ue_in0 ue_in1 ue_done ue_gelud ue_kept0 ue_kept1")
        self.u_in, self.kept = (i0, i1), (k0, k1)

    def load(self, sp, it, n):
        one = bass.ds(it * 2 + n, 1)
        sp.dma_start(self.c.ur[:, n % 2], self.c.t["u"][one].rearrange("g p k e -> (g p) (k e)")).then_inc(self.u_in[n % 2], 16)

    def keep(self, sp, it, n):
        sp.wait_ge(self.gelud, it * 2 + (n + 1))
        one = bass.ds(it * 2 + n, 1)
        sp.dma_start(self.c.t["early"][one].rearrange("g p t -> (g p) t"), self.c.ar[:, n % 2]).then_inc(self.kept[n % 2], 16)

    def next_load(self, sp, it, n):
        sp.wait_ge(self.done, it * 2 + (n + 1))
        self.load(sp, it, n + 2)

    def products(self, pe, it, n, bank, first, part=None):
        c, r = self.c, n % 2
        if part in (None, 0):
            pe.wait_ge(self.u_in[r], it * 16 + 16 * (n // 2 + 1))
            if not first:
                pe.wait_ge(self.gelud, it * 2 + (n - 1))
        ks = range(KT) if part is None else range(part * KT // 2, (part + 1) * KT // 2)
        for k in ks:
            mm = pe.matmul(c.bank[bank + r][:], c.ur[:, r, k * P:(k + 1) * P], c.XT[:, k], start=k == 0, stop=k == KT - 1)
        if part in (None, 1):
            mm.then_inc(self.done, 1)

    def gelu(self, act, it, n, bank, first):
        c, r = self.c, n % 2
        act.wait_ge(self.done, it * 2 + (n + 1))
        if not first:
            act.wait_ge(self.kept[r], it * 16 + 16 * (n // 2))
        act.activation(c.ar[:, r], c.bank[bank + r][:], ACT.Gelu).then_inc(self.gelud, 1)


def phase_choose(c, ijg, early):
    nc = c.nc
    NQ = 2 * PH
    with ExitStack() as ctx:
        sb = lambda name, shape, dt=F32: ctx.enter_context(nc.sbuf_tensor(name, shape, dt))
        qT = sb("qT", [P, NQ, SEQ])
        SC = sb("SC", [P, 2, NQ, PK])
        S2 = sb("SC2", [P, NQ * PK])
        cand = sb("cand", [P, PH, TOPK * TOPK])
        t16 = sb("t16", [P, NQ, TOPK])
        i16 = sb("i16", [P, NQ, TOPK], U32)
        i16f = sb("i16f", [P, NQ, TOPK])
        b16 = sb("b16", [P, PH, TOPK])
        pos = sb("pos", [P, PH, TOPK], U32)
        ab = sb("ab", [P, 2, SLOTS], U32)
        abf = sb("abf", [P, 2, SLOTS])
        eq = sb("eq", [P, SLOTS, TOPK])
        out3 = sb("out3", [P, 3, SLOTS])
        gs = sb("gs", [P, 2, PH])
        qg, qa, qd, sg, so, step, gexp, gdiff, chosen, t3, t3o = signals(
            nc, ctx, "q_grp q_out_a q_out_d s_grp s_out c_step g_exp g_diff chosen t3_turned t3_out")
        block = ctx.enter_context(nc.Block())

        PER = E_CHOOSE // TT
        EB = 1

        @block.sync
        def _(sp):
            early.load(sp, 0, 0)
            early.load(sp, 0, 1)
            for b in range(B_PQ, B_KEYS + 1 - RING):
                sp.wait_ge(qg, 4 * (b - B_PQ + 1))
                c.load_w(sp, b + RING)
            with sp.Fori(0, E_CHOOSE // 2) as it:
                for r in range(2):
                    early.next_load(sp, it, r)
                    early.keep(sp, it, r)

        @block.tensor
        def _(pe):
            for g in range(NQ):
                if g % 4 == 0:
                    c.wait_w(pe, B_PQ + g // 4)
                if g >= 4:
                    pe.wait_ge(qd if g % 2 else qa, g // 2 - 1)
                w = c.w(B_PQ + g // 4, KT * 512, 512)
                for k in range(KT):
                    mm = pe.matmul(c.bank[g % 4][:], w[:, k, (g % 4) * P:(g % 4 + 1) * P], c.XT[:, k], start=k == 0, stop=k == KT - 1)
                mm.then_inc(qg, 1)
            pe.wait_ge(qa, NQ // 2)
            pe.wait_ge(qd, NQ // 2)
            c.wait_w(pe, B_KEYS)
            keys = c.w(B_KEYS, NQ * PK)

            def scores(tt):
                for j in range(4):
                    if tt >= 1:
                        pe.wait_ge(so, 4 * (tt - 1) + j + 1)
                    for i in range(4):
                        mm = pe.matmul(c.bank[4 + j][:, i * PK:(i + 1) * PK], qT[:, 4 * j + i, tt * P:(tt + 1) * P], keys[:, 4 * j + i],
                                       start=True, stop=True)
                    mm.then_inc(sg, 1)

            scores(0)
            for tt in range(TT):
                if tt + 1 < TT:
                    scores(tt + 1)
                if tt == 0:
                    for n in range(2):
                        early.products(pe, 0, n, EB, True)
                with pe.Fori(int(tt == 0), PER // 2) as it:
                    for r in range(2):
                        early.products(pe, it, tt * PER + r, EB, False)
                pe.wait_ge(chosen, tt + 1)
                if tt >= 1:
                    pe.wait_ge(t3o, tt)
                for i in range(3):
                    mm = pe.transpose(c.bank[0][:, i * P:(i + 1) * P], out3[:, i], c.ident)
                mm.then_inc(t3, 1)

        @block.scalar
        def _(act):
            for g in range(0, NQ, 2):
                act.wait_ge(qg, g + 1)
                act.activation(qT[:, g], c.bank[g % 4][:], ACT.Copy).then_inc(qa, 1)

            def scores_out(tt):
                for j in range(4):
                    act.wait_ge(sg, 4 * tt + j + 1)
                    if tt >= 2:
                        act.wait_ge(chosen, tt - 1)
                    act.activation(SC[:, tt % 2, 4 * j:4 * j + 4].rearrange("p a b -> p (a b)"), c.bank[4 + j][:], ACT.Copy).then_inc(so, 1)

            scores_out(0)
            for tt in range(TT):
                if tt + 1 < TT:
                    scores_out(tt + 1)
                if tt == 0:
                    for n in range(2):
                        early.gelu(act, 0, n, EB, True)
                with act.Fori(int(tt == 0), PER // 2 - 1) as it:
                    for r in range(2):
                        early.gelu(act, it, tt * PER + r, EB, False)
                act.wait_ge(gdiff, tt + 1)
                act.activation(b16[:], b16[:], ACT.Exp).then_inc(gexp, 1)
                for r in range(2):
                    early.gelu(act, 0, (tt + 1) * PER - 2 + r, EB, False)
                act.wait_ge(t3, tt + 1)
                act.activation(ijg[:, :, tt * P:(tt + 1) * P], c.bank[0][:, 0:3 * P].rearrange("p (a b) -> p a b", b=P), ACT.Copy).then_inc(t3o, 1)

        @block.vector
        def _(dve):
            for g in range(1, NQ, 2):
                dve.wait_ge(qg, g + 1)
                dve.tensor_copy(qT[:, g], c.bank[g % 4][:]).then_inc(qd, 1)
            n = [0]

            def link(ins):
                n[0] += 1
                ins.then_inc(step, 1)
                dve.wait_ge(step, n[0])

            sc2 = S2[:].rearrange("p (a b) -> p a b", b=PK)
            cand2 = S2[:].rearrange("p (a b) -> p a b", b=TOPK * TOPK)
            for tt in range(TT):
                sc = SC[:, tt % 2]
                dve.wait_ge(so, 4 * (tt + 1))
                for j in range(NQ):
                    last = dve.max(t16[:, j, 0:8], sc[:, j])
                link(last)
                for j in range(NQ):
                    dve.max_index(i16[:, j, 0:8], t16[:, j, 0:8], sc[:, j])
                    last = dve.match_replace(sc2[:, j], t16[:, j, 0:8], sc[:, j], LOWEST)
                link(last)
                for j in range(NQ):
                    last = dve.max(t16[:, j, 8:16], sc2[:, j])
                link(last)
                for j in range(NQ):
                    last = dve.max_index(i16[:, j, 8:16], t16[:, j, 8:16], sc2[:, j])
                link(last)
                link(dve.tensor_copy(i16f[:], i16[:]))
                for h in range(PH):
                    last = dve.tensor_tensor(cand[:, h].rearrange("p (a b) -> p a b", b=TOPK), bc(t16[:, 2 * h], TOPK),
                                             mid(t16[:, 2 * h + 1], TOPK), ALU.add)
                link(last)
                if tt >= 1:
                    dve.wait_ge(t3, tt)
                for h in range(PH):
                    last = dve.max(b16[:, h, 0:8], cand[:, h])
                link(last)
                for h in range(PH):
                    dve.max_index(pos[:, h, 0:8], b16[:, h, 0:8], cand[:, h])
                    last = dve.match_replace(cand2[:, h], b16[:, h, 0:8], cand[:, h], LOWEST)
                link(last)
                for h in range(PH):
                    last = dve.max(b16[:, h, 8:16], cand2[:, h])
                link(last)
                for h in range(PH):
                    last = dve.max_index(pos[:, h, 8:16], b16[:, h, 8:16], cand2[:, h])
                link(last)
                link(dve.tensor_copy(gs[:, 0], b16[:, :, 0]))
                dve.tensor_tensor(b16[:], b16[:], bc(gs[:, 0], TOPK), ALU.subtract).then_inc(gdiff, 1)
                posf = pos[:].rearrange("p h k -> p (h k)")
                dve.tensor_scalar(ab[:, 0], posf, 4, None, ALU.logical_shift_right)
                link(dve.tensor_scalar(ab[:, 1], posf, TOPK - 1, None, ALU.bitwise_and))
                link(dve.tensor_copy(abf[:], ab[:]))
                for half in range(2):
                    link(dve.tensor_tensor(eq[:], bc(abf[:, half], TOPK), mid(c.iota[:, 0:TOPK], SLOTS), ALU.is_equal))
                    eqh = eq[:].rearrange("p (h k) a -> p h k a", h=PH)
                    key = i16f[:].rearrange("p (h f) a -> p h f a", f=2)[:, :, half].unsqueeze(2).broadcast_to([P, PH, TOPK, TOPK])
                    link(dve.tensor_tensor(eqh, eqh, key, ALU.mult))
                    link(dve.tensor_reduce(out3[:, half], eq[:], AX, ALU.add))
                dve.wait_ge(gexp, tt + 1)
                link(dve.tensor_reduce(gs[:, 0], b16[:], AX, ALU.add))
                link(dve.reciprocal(gs[:, 1], gs[:, 0]))
                dve.tensor_tensor(out3[:, 2].rearrange("p (h k) -> p h k", h=PH), b16[:], bc(gs[:, 1], TOPK), ALU.mult).then_inc(chosen, 1)
                dve.wait_ge(chosen, tt + 1)


def phase_gates(c, ijg, early):
    nc, t = c.nc, c.t
    Q = 4
    S = 2 * Q
    NSL = P // S
    B = 4
    ON_ACT = 6
    EB = 4
    CUTS = 4
    E0 = E_CHOOSE
    with ExitStack() as ctx:
        hot = [[ctx.enter_context(nc.sbuf_tensor(f"hot{half}{i}", [P, S, P], F32)) for i in range(2)] for half in range(2)]
        stage = [ctx.enter_context(nc.sbuf_tensor(f"stage{i}", [P, PK, P], F32)) for i in range(2)]
        hot_made, weighed_a, weighed_d, built, copied, st0, st1 = signals(
            nc, ctx, "hot_made weighed_a weighed_d built copied stored0 stored1")
        stored = (st0, st1)
        block = ctx.enter_context(nc.Block())
        dest = t["gates"].rearrange("i j t -> j i t")

        @block.vector
        def _(dve):
            for tt in range(TT):
                with dve.Fori(0, NSL // B) as it:
                    for s in range(B):
                        j, r = tt * NSL + s, s % 2
                        dve.wait_ge(built, it * (2 * B) + (2 * j + 2))
                        tok = it * (B * S) + j * S
                        for half in (1, 0):
                            dve.tensor_tensor(hot[half][r][:], mid(c.iota, S), bc(ijg[:, half, bass.ds(tok, S)], P),
                                              ALU.is_equal).then_inc(hot_made, 1)
                        dve.wait_ge(hot_made, it * (2 * B) + (2 * j + 2))
                        part = hot[0][r][:, ON_ACT:]
                        dve.tensor_tensor(part, part, bc(ijg[:, 2, bass.ds(tok + ON_ACT, S - ON_ACT)], P), ALU.mult).then_inc(weighed_d, 1)

        @block.tensor
        def _(pe):
            pe.sem_inc(built, 4)
            for tt in range(TT):
                with pe.Fori(0, NSL // B) as it:
                    for s in range(B):
                        j, r = tt * NSL + s, s % 2
                        pe.wait_ge(weighed_a, it * B + (j + 1))
                        pe.wait_ge(weighed_d, it * B + (j + 1))
                        for q in range(2):
                            pe.wait_ge(copied, it * (2 * B) + (2 * j + q + 1))
                            for k in range(Q):
                                mm = pe.matmul(c.bank[2 * r + q][:, k * P:(k + 1) * P], hot[1][r][:, Q * q + k], hot[0][r][:, Q * q + k],
                                               start=True, stop=True)
                            mm.then_inc(built, 1)
                        early.products(pe, it, E0 + j // B * 2 + s // 2, EB, False, part=s % 2)
            with pe.Fori(0, E_STORE // 2) as it:
                for r in range(2):
                    early.products(pe, it, E0 + E_GATES + r, EB, False)

        @block.scalar
        def _(act):
            act.sem_inc(copied, 4)

            def weigh(it, j):
                act.wait_ge(hot_made, it * (2 * B) + (2 * j + 2))
                for k in range(ON_ACT):
                    one = hot[0][j % 2][:, k]
                    last = act.activation(one, one, ACT.Copy, scale=ijg[:, 2, bass.ds(it * (B * S) + (j * S + k), 1)])
                last.then_inc(weighed_a, 1)

            def turn(it, tt, last):
                for s in range(B):
                    j = tt * NSL + s
                    if not (last and s == B - 1):
                        weigh(it, j + 1)
                    for q in range(2):
                        act.wait_ge(built, it * (2 * B) + (2 * j + q + 5))
                        o = stage[tt % 2][:, :, bass.ds(it * (B * S) + (2 * s + q) * Q, Q)]
                        act.activation(o, c.bank[2 * (s % 2) + q][:].rearrange("p (k i) -> p i k", k=Q), ACT.Copy).then_inc(copied, 1)
                    if s % 2:
                        early.gelu(act, it, E0 + j // B * 2 + s // 2, EB, False)

            weigh(0, 0)
            for tt in range(TT):
                if tt >= 2:
                    act.wait_ge(stored[tt % 2], 16 * CUTS)
                whole = NSL // B - (tt == TT - 1)
                with act.Fori(0, whole) as it:
                    turn(it, tt, False)
            turn(NSL // B - 1, TT - 1, True)
            with act.Fori(0, E_STORE // 2) as it:
                for r in range(2):
                    early.gelu(act, it, E0 + E_GATES + r, EB, False)

        @block.sync
        def _(sp):
            with sp.Fori(E0 // 2, EARLY // 2 - 1) as it:
                for r in range(2):
                    early.next_load(sp, it, r)
                    early.keep(sp, it, r)
            for r in range(2):
                early.keep(sp, EARLY // 2 - 1, r)
            for s in early.kept:
                sp.wait_ge(s, 16 * EARLY // 2)

        @block.gpsimd
        def _(pool):
            for tt in range(TT):
                pool.wait_ge(copied, 2 * NSL * (tt + 1) + 4)
                for j in range(0, PK, PK // CUTS):
                    pool.dma_start(dest[j:j + PK // CUTS, :, tt * P:(tt + 1) * P], stage[tt % 2][j:j + PK // CUTS]).then_inc(stored[tt % 2], 16)
            for s in stored:
                pool.wait_ge(s, 16 * CUTS * TT // 2)


def phase_experts(c):
    nc, t = c.nc, c.t
    with ExitStack() as ctx:
        sb = lambda name, shape, dt=F32: ctx.enter_context(nc.sbuf_tensor(name, shape, dt))
        Xh, Xl = sb("Xh", [P, KT, SEQ], F32R), sb("Xl", [P, KT, SEQ], F32R)
        Ur = [c.ur[:, i].rearrange("p (k e) -> p k e", e=P) for i in range(2)]
        Uh = [sb(f"Uh{i}", [P, KT, P], F32R) for i in range(2)]
        Ul = [sb(f"Ul{i}", [P, KT, P], F32R) for i in range(2)]
        Vr = [sb(f"Vr{i}", [P, D]) for i in range(2)]
        Vh = [sb(f"Vh{i}", [P, EG, D], F32R) for i in range(2)]
        Vl = [sb(f"Vl{i}", [P, EG, D], F32R) for i in range(2)]
        Gr = [sb(f"Gr{i}", [P, SEQ]) for i in range(2)]
        A = [c.ar[:, i] for i in range(2)]
        Hh = [sb(f"Hh{i}", [P, EG, SEQ], F32R) for i in range(2)]
        Hl = [sb(f"Hl{i}", [P, EG, SEQ], F32R) for i in range(2)]
        (u0, u1, a0, a1, v0, v1, g0, g1, xhi, xlo, u_hi, u_lo, v_hi, v_lo, acted, gelud, gated, h_hi, h_lo, summed, added) = signals(
            nc, ctx, "u_in0 u_in1 a_in0 a_in1 v_in0 v_in1 g_in0 g_in1 x_hi x_lo u_hi u_lo v_hi v_lo acted gelud e_gated h_hi h_lo summed added2")
        u_in, a_in, v_in, g_in = (u0, u1), (a0, a1), (v0, v1), (g0, g1)
        block = ctx.enter_context(nc.Block())
        VG = 2 * TT
        A0 = 2
        S0 = 16
        L0 = 2
        G0 = 2
        B0 = 8

        LATE, TURNS = EARLY // (2 * EG), NG // 2

        def load_u(sp, it, m):
            one = bass.ds(it * 8 + (EARLY + m), 1)
            sp.dma_start(Ur[m % 2], t["u"][one].rearrange("g p k e -> (g p) k e")).then_inc(u_in[m % 2], 16)

        def load_gv(sp, it, n):
            one, r = bass.ds(it * 8 + n, 1), n % 2
            sp.wait_ge(gated, it * 8 + (n - 1 + G0))
            sp.dma_start(Gr[r][:], t["gates"][one].rearrange("i j t -> (i j) t")).then_inc(g_in[r], 16)
            sp.wait_ge(v_lo, it * 8 + (n - 1 + L0))
            sp.dma_start(Vr[r][:], t["v"][one].rearrange("g e d -> (g e) d")).then_inc(v_in[r], 16)

        @block.sync
        def _(sp):
            load_u(sp, 0, 0)
            load_u(sp, 0, 1)
            with sp.Fori(0, LATE) as it:
                for n in range(8):
                    sp.wait_ge(h_lo, it * 8 + (n - 1 + G0))
                    sp.dma_start(A[n % 2], t["early"][bass.ds(it * 8 + n, 1)].rearrange("g p t -> (g p) t")).then_inc(a_in[n % 2], 16)
                    load_gv(sp, it, n)
            with sp.Fori(LATE, TURNS - 1) as it:
                for n in range(8):
                    sp.wait_ge(u_lo, (it - LATE) * 8 + (n + 1 + L0))
                    load_u(sp, it - LATE, n + 2)
                    load_gv(sp, it, n)
            for n in range(8):
                if n < 6:
                    sp.wait_ge(u_lo, (TURNS - 1 - LATE) * 8 + (n + 1 + L0))
                    load_u(sp, TURNS - 1 - LATE, n + 2)
                load_gv(sp, TURNS - 1, n)

        def up(pe, turn, s):
            it = turn - LATE
            for e in range(EG):
                n, r = 4 * s + e, e % 2
                pe.wait_ge(u_lo, it * 8 + (n + 1 + L0))
                pe.wait_ge(gelud, it * 8 + (n + 1 - 4 + B0))
                for k in range(KT):
                    pe.matmul(c.bank[e][:], Uh[r][:, k], Xh[:, k], start=k == 0, stop=False)
                    pe.matmul(c.bank[e][:], Uh[r][:, k], Xl[:, k], start=False, stop=False)
                    mm = pe.matmul(c.bank[e][:], Ul[r][:, k], Xh[:, k], start=False, stop=k == KT - 1)
                mm.then_inc(acted, 1)

        def down(pe, it, s):
            pe.wait_ge(h_lo, it * 8 + (4 * s + 4 + G0))
            pe.wait_ge(v_lo, it * 8 + (4 * s + 4 + L0))
            for p in range(VG):
                tt, nh = divmod(p, 2)
                tok, cut, ps = slice(tt * P, (tt + 1) * P), slice(nh * 512, (nh + 1) * 512), c.bank[4 + p % 4]
                pe.wait_ge(added, it * 16 + (8 * s + p + 1 - 4 + B0))
                for e in range(EG):
                    pe.matmul(ps[:], Hh[s][:, e, tok], Vh[s][:, e, cut], start=e == 0, stop=False)
                    pe.matmul(ps[:], Hh[s][:, e, tok], Vl[s][:, e, cut], start=False, stop=False)
                    mm = pe.matmul(ps[:], Hl[s][:, e, tok], Vh[s][:, e, cut], start=False, stop=e == EG - 1)
                mm.then_inc(summed, 1)

        @block.tensor
        def _(pe):
            pe.sem_inc(acted, A0)
            pe.sem_inc(summed, S0)
            with pe.Fori(0, LATE - 1) as it:
                down(pe, it, 0)
                down(pe, it, 1)
            down(pe, LATE - 1, 0)
            pe.wait_ge(xlo, KT)
            up(pe, LATE, 0)
            down(pe, LATE - 1, 1)
            with pe.Fori(LATE, TURNS - 1) as it:
                up(pe, it, 1)
                down(pe, it, 0)
                up(pe, it + 1, 0)
                down(pe, it, 1)
            up(pe, TURNS - 1, 1)
            down(pe, TURNS - 1, 0)
            down(pe, TURNS - 1, 1)

        def hi_u(act, it, n):
            act.wait_ge(u_in[n % 2], it * 64 + 16 * (n // 2 + 1))
            act.wait_ge(acted, it * 8 + (n - 1 + A0))
            act.activation(Uh[n % 2][:], Ur[n % 2], ACT.Copy).then_inc(u_hi, 1)

        def tile_act(act, it, s, e, late, ahead=True):
            n, r = 4 * s + e, e % 2
            if late:
                act.wait_ge(acted, (it - LATE) * 8 + (n + 1 + A0))
                act.wait_ge(h_lo, it * 8 + (n - 1 + G0))
                act.activation(A[r], c.bank[e][:], ACT.Gelu).then_inc(gelud, 1)
                if ahead:
                    hi_u(act, it - LATE, n + 2)
            act.wait_ge(v_in[r], it * 64 + 16 * (n // 2 + 1))
            act.wait_ge(summed, it * 16 + (8 * s - 8 + S0))
            act.activation(Vh[s][:, e], Vr[r][:], ACT.Copy).then_inc(v_hi, 1)
            act.wait_ge(gated, it * 8 + (n + 1 + G0))
            act.activation(Hh[s][:, e], A[r], ACT.Copy).then_inc(h_hi, 1)

        def lo_u(dve, it, n):
            dve.wait_ge(u_hi, it * 8 + n + 1)
            dve.tensor_tensor(Ul[n % 2][:], Ur[n % 2], Uh[n % 2][:].bitcast(F32), ALU.subtract).then_inc(u_lo, 1)

        def tile_dve(dve, it, s, e, late, ahead=True):
            n, r = 4 * s + e, e % 2
            dve.wait_ge(g_in[r], it * 64 + 16 * (n // 2 + 1))
            if late:
                dve.wait_ge(gelud, (it - LATE) * 8 + (n + 1 + B0))
            else:
                dve.wait_ge(a_in[r], it * 64 + 16 * (n // 2 + 1))
            dve.tensor_tensor(A[r], A[r], Gr[r][:], ALU.mult).then_inc(gated, 1)
            if late and ahead:
                lo_u(dve, it - LATE, n + 2)
            dve.wait_ge(v_hi, it * 8 + (n + 1))
            dve.tensor_tensor(Vl[s][:, e], Vr[r][:], Vh[s][:, e].bitcast(F32), ALU.subtract).then_inc(v_lo, 1)
            dve.wait_ge(h_hi, it * 8 + (n + 1))
            dve.tensor_tensor(Hl[s][:, e], A[r], Hh[s][:, e].bitcast(F32), ALU.subtract).then_inc(h_lo, 1)

        @block.scalar
        def _(act):
            act.sem_inc(gelud, B0)
            for e in range(EG):
                tile_act(act, 0, 0, e, False)
            for k in range(KT):
                act.activation(Xh[:, k], c.XT[:, k], ACT.Copy).then_inc(xhi, 1)
            hi_u(act, 0, 0)
            hi_u(act, 0, 1)
            with act.Fori(0, LATE - 1) as it:
                for e in range(EG):
                    tile_act(act, it, 1, e, False)
                for e in range(EG):
                    tile_act(act, it + 1, 0, e, False)
            for e in range(EG):
                tile_act(act, LATE - 1, 1, e, False)
            with act.Fori(LATE, TURNS - 1) as it:
                for s in range(2):
                    for e in range(EG):
                        tile_act(act, it, s, e, True)
            for s in range(2):
                for e in range(EG):
                    tile_act(act, TURNS - 1, s, e, True, 4 * s + e < 6)

        def add(dve, it, s, pieces=range(VG)):
            for p in pieces:
                tt, nh = divmod(p, 2)
                dve.wait_ge(summed, it * 16 + (8 * s + p + 1 + S0))
                dve.wait_ge(added, it * 16 + (8 * s + p + 1 - 8 + B0))
                xs = c.X[:, tt, nh * 512:(nh + 1) * 512]
                dve.tensor_tensor(xs, c.bank[4 + p % 4][:], xs, ALU.add).then_inc(added, 1)

        @block.vector
        def _(dve):
            dve.sem_inc(u_lo, L0)
            dve.sem_inc(v_lo, L0)
            dve.sem_inc(gated, G0)
            dve.sem_inc(h_lo, G0)
            dve.sem_inc(added, B0)
            for e in range(EG):
                tile_dve(dve, 0, 0, e, False)
            for k in range(KT):
                dve.wait_ge(xhi, k + 1)
                dve.tensor_tensor(Xl[:, k], c.XT[:, k], Xh[:, k].bitcast(F32), ALU.subtract).then_inc(xlo, 1)
            lo_u(dve, 0, 0)
            lo_u(dve, 0, 1)
            with dve.Fori(0, LATE - 1) as it:
                for e in range(EG):
                    tile_dve(dve, it, 1, e, False)
                    add(dve, it, 0, (2 * e, 2 * e + 1))
                for e in range(EG):
                    tile_dve(dve, it + 1, 0, e, False)
                    add(dve, it, 1, (2 * e, 2 * e + 1))
            for e in range(EG):
                tile_dve(dve, LATE - 1, 1, e, False)
                add(dve, LATE - 1, 0, (2 * e, 2 * e + 1))
            for e in range(EG):
                tile_dve(dve, LATE, 0, e, True)
            add(dve, LATE - 1, 1)
            with dve.Fori(LATE, TURNS - 1) as it:
                for e in range(EG):
                    tile_dve(dve, it, 1, e, True)
                add(dve, it, 0)
                for e in range(EG):
                    tile_dve(dve, it + 1, 0, e, True)
                add(dve, it, 1)
            for e in range(EG):
                tile_dve(dve, TURNS - 1, 1, e, True, e < 2)
            add(dve, TURNS - 1, 0)
            add(dve, TURNS - 1, 1)


def phase_between(c):
    nc, t = c.nc, c.t
    with ExitStack() as ctx:
        HN = ctx.enter_context(nc.sbuf_tensor("HN2", [P, TT, D], F32))
        nf = ctx.enter_context(nc.sbuf_tensor("nf", [P, D], F32))
        nf_in, xnorm, xready = signals(
            nc, ctx, "nf_in b_xnorm b_xready")
        block = ctx.enter_context(nc.Block())

        @block.sync
        def _(sp):
            sp.dma_start(nf[:], t["norm_f"]).then_inc(nf_in, 16)
            for b in range(B_XBC, B_XBC + RING):
                c.load_w(sp, b)

        @block.scalar
        def _(act):
            norm_sums(act, c, c.X, HN)
            act.wait_ge(xready, TT)
            act.wait_ge(c.squared, (N_FINAL + 1) * TT)
            norm_sums(act, c, c.X, HN)
            gains_act(act, c, C_GPRE, T_PRE)

        @block.gpsimd
        def _(pool):
            norm_rsqrt(pool, c, N_FINAL)
            pool.wait_ge(xnorm, TT)
            norm_rsqrt(pool, c, N_PRE)

        @block.vector
        def _(dve):
            dve.wait_ge(c.rooted, N_FINAL + 1)
            for tt in range(TT):
                dve.tensor_scalar(c.X[:, tt], c.X[:, tt], c.rn[:, tt:tt + 1], None, ALU.mult).then_inc(xnorm, 1)
            dve.wait_ge(nf_in, 16)
            for tt in range(TT):
                dve.wait_ge(xnorm, tt + 1)
                dve.tensor_tensor(c.X[:, tt], c.X[:, tt], nf[:], ALU.mult).then_inc(xready, 1)
            dve.wait_ge(c.rooted, N_PRE + 1)
            dve.wait_ge(xready, TT)
            for tt in range(TT):
                dve.tensor_scalar(HN[:, tt], c.X[:, tt], c.rn[:, tt:tt + 1], None, ALU.mult).then_inc(c.scaled, 1)
            gains_dve(dve, c, C_GPRE, T_PRE)

        @block.tensor
        def _(pe):
            transposes_pe(pe, c, HN, T_PRE)


class Mixer:
    def __init__(self, nc, ctx):
        sb = lambda name, shape: ctx.enter_context(nc.sbuf_tensor(name, shape, F32))
        self.yscT = sb("yscT", [P, KT, SEQ])
        self.xs = sb("xs", [P, TT, D])
        self.zs = sb("zs", [P, TT, D])
        self.xbcT = sb("xbcT", [P, XBC_TILES, SEQ])
        self.dt = sb("dt", [P, TT, SH])


def phase_mixer_in(c, m_):
    nc = c.nc
    with ExitStack() as ctx:
        pad = ctx.enter_context(nc.sbuf_tensor("pad", [P, 2, CONV_W - 1 + SEQ], F32))
        pad2 = ctx.enter_context(nc.sbuf_tensor("pad2", [P, 2, SC_W - 1 + SEQ], F32))
        cv = ctx.enter_context(nc.sbuf_tensor("cv", [P, 2, SEQ], F32))
        cs = ctx.enter_context(nc.sbuf_tensor("cs", [P, 2, SEQ], F32))
        zz = ctx.enter_context(nc.sbuf_tensor("zz", [P, 2, SEQ], F32))
        zero, grp, padded, convd, silud, dtg, dto, scg, c_out, z_out, step, vdone = signals(
            nc, ctx, "n_zero n_grp n_padded n_convd n_silud n_dt_grp n_dt_out n_sc_grp n_c_out n_z_out n_step n_done")
        block = ctx.enter_context(nc.Block())
        NX, NZ = XBC_TILES, 2 * TT

        @block.sync
        def _(sp):
            for b in range(B_XBC, B_MIX):
                if b < B_DT:
                    sp.wait_ge(grp, min(4 * (b - B_XBC + 1), NX))
                elif b == B_DT:
                    sp.wait_ge(dtg, 1)
                elif b < B_SC:
                    sp.wait_ge(grp, NX + TT * (b - B_Z + 1))
                else:
                    sp.wait_ge(scg, 4 * (b - B_SC + 1))
                c.load_w(sp, b + RING)

        @block.gpsimd
        def _(pool):
            pool.memset(pad[:], 0.0).then_inc(zero, 1)
            pool.memset(pad2[:], 0.0).then_inc(zero, 1)

        @block.tensor
        def _(pe):
            def slot(n):
                if n >= 4:
                    if n - 4 < NX:
                        pe.wait_ge(padded, n - 3)
                    else:
                        pe.wait_ge(z_out, n - 4 - NX + 1)

            for n in range(NX):
                if n % 4 == 0:
                    c.wait_w(pe, B_XBC + n // 4)
                slot(n)
                width = min(512, NX * P - 512 * (n // 4))
                w = c.w(B_XBC + n // 4, KT * width, width)
                for k in range(KT):
                    mm = pe.matmul(c.bank[n % 4][:], w[:, k, (n % 4) * P:(n % 4 + 1) * P], c.XT[:, k], start=k == 0, stop=k == KT - 1)
                mm.then_inc(grp, 1)
            c.wait_w(pe, B_DT)
            w = c.w(B_DT, KT * SH, SH)
            for tt in range(TT):
                for k in range(KT):
                    mm = pe.matmul(c.bank[7][:, tt * SH:(tt + 1) * SH], c.XT[:, k, tt * P:(tt + 1) * P], w[:, k], start=k == 0, stop=k == KT - 1)
            mm.then_inc(dtg, 1)
            for n in range(NX, NX + NZ):
                nh, tt = divmod(n - NX, TT)
                if tt == 0:
                    c.wait_w(pe, B_Z + nh)
                slot(n)
                w = c.w(B_Z + nh, KT * 512, 512)
                for k in range(KT):
                    mm = pe.matmul(c.bank[n % 4][:], c.XT[:, k, tt * P:(tt + 1) * P], w[:, k], start=k == 0, stop=k == KT - 1)
                mm.then_inc(grp, 1)
            pe.wait_ge(z_out, NZ)
            pe.wait_ge(dto, 1)
            for m in range(KT):
                c.wait_w(pe, B_SC + m)
                if m >= 2:
                    pe.wait_ge(vdone, m - 1)
                    pe.wait_ge(z_out, NZ + m - 1)
                w = c.w(B_SC + m, 4 * KT * P)
                for j in range(4):
                    for k in range(KT):
                        mm = pe.matmul(c.bank[4 * (m % 2) + j][:], w[:, KT * j + k], c.XT[:, k], start=k == 0, stop=k == KT - 1)
                    mm.then_inc(scg, 1)

        @block.scalar
        def _(act):
            act.wait_ge(zero, 2)
            for n in range(NX + 1):
                if n < NX:
                    act.wait_ge(grp, n + 1)
                    if n >= 2:
                        act.wait_ge(convd, n - 1)
                    act.activation(pad[:, n % 2, CONV_W - 1:], c.bank[n % 4][:], ACT.Copy).then_inc(padded, 1)
                if n >= 1:
                    act.wait_ge(convd, n)
                    act.activation(m_.xbcT[:, n - 1], cv[:, (n - 1) % 2], ACT.Silu, bias=c.cols[:, C_CB + n - 1:C_CB + n]).then_inc(silud, 1)
            for n in range(NZ):
                nh, tt = divmod(n, TT)
                act.wait_ge(grp, NX + n + 1)
                act.activation(m_.zs[:, tt, nh * 512:(nh + 1) * 512], c.bank[(NX + n) % 4][:], ACT.Silu).then_inc(z_out, 1)
            for m in range(KT):
                bk = c.bank[4 * (m % 2):4 * (m % 2) + 4]
                act.wait_ge(scg, 4 * m + 1)
                if m >= 2:
                    act.wait_ge(vdone, m - 1)
                act.activation(cs[:, m % 2], bk[0][:], ACT.Copy).then_inc(c_out, 1)
                act.wait_ge(scg, 4 * m + 4)
                act.activation(zz[:, m % 2], bk[3][:], ACT.Silu).then_inc(z_out, 1)

        @block.vector
        def _(dve):
            n_ = [0]

            def link(ins):
                n_[0] += 1
                ins.then_inc(step, 1)
                dve.wait_ge(step, n_[0])

            for n in range(NX):
                dve.wait_ge(padded, n + 1)
                if n >= 2:
                    dve.wait_ge(silud, n - 1)
                tap = lambda k: c.cols[:, C_CW + n * CONV_W + k:C_CW + n * CONV_W + k + 1]
                o = cv[:, n % 2]
                link(dve.tensor_scalar(o, pad[:, n % 2, 0:SEQ], tap(0), None, ALU.mult))
                for k in range(1, CONV_W):
                    ins = dve.scalar_tensor_tensor(out=o, in0=pad[:, n % 2, k:k + SEQ], scalar=tap(k), in1=o, op0=ALU.mult, op1=ALU.add)
                    if k < CONV_W - 1:
                        link(ins)
                ins.then_inc(convd, 1)
            dve.wait_ge(dtg, 1)
            dve.tensor_tensor(m_.dt[:], c.bank[7][:, 0:TT * SH].rearrange("p (t h) -> p t h", h=SH), mid(c.rows[:, R_DTB:R_DTB + SH], TT),
                              ALU.add).then_inc(dto, 1)
            for m in range(KT):
                bk = c.bank[4 * (m % 2):4 * (m % 2) + 4]
                dve.wait_ge(scg, 4 * m + 2)
                dve.wait_ge(c_out, m + 1)
                link(dve.tensor_tensor(pad2[:, m % 2, SC_W - 1:], bk[1][:], cs[:, m % 2], ALU.mult))
                tap = lambda k: c.cols[:, C_SW + m * SC_W + k:C_SW + m * SC_W + k + 1]
                o = m_.yscT[:, m]
                link(dve.tensor_scalar(o, pad2[:, m % 2, 0:SEQ], tap(0), None, ALU.mult))
                for k in range(1, SC_W):
                    link(dve.scalar_tensor_tensor(out=o, in0=pad2[:, m % 2, k:k + SEQ], scalar=tap(k), in1=o, op0=ALU.mult, op1=ALU.add))
                dve.wait_ge(scg, 4 * m + 3)
                link(dve.tensor_tensor(o, bk[2][:], o, ALU.mult))
                dve.wait_ge(z_out, NZ + m + 1)
                dve.tensor_tensor(o, o, zz[:, m % 2], ALU.mult).then_inc(vdone, 1)


def phase_scan(c, m_):
    nc, t = c.nc, c.t
    GW = HG * SP_
    UN = TT * SG
    with ExitStack() as ctx:
        sb = lambda name, shape: ctx.enter_context(nc.sbuf_tensor(name, shape, F32))
        bt = sb("bt", [P, TT, P])
        ones = sb("ones", [P, P])
        sp_ = sb("sp", [P, 6, TT, SH])
        aneg = sb("aneg", [P, SH])
        adt = sb("adt", [P, TT, SH])
        acs = sb("acs", [P, 2, TT, SH])
        eacs = sb("eacs", [P, TT, SH])
        dst = sb("dst", [P, TT, SH])
        etot = sb("etot", [P, TT, SH])
        dec = sb("dec", [P, TT, HG])
        xd = sb("xd", [P, D])
        xdd = sb("xdd", [P, D])
        E = sb("E", [P, 2, HG, P])
        cbm = sb("cbm", [P, 2, P])
        st = sb("st", [P, GW])
        tmp = sb("tmp", [P, GW])
        sg = sb("sgn", [P, 3, UN])
        nrm = sb("nrm", [P, D])
        y = c.XT[:].rearrange("p a b -> p (a b)").rearrange("p (t d) -> p t d", t=TT)
        (nrm_in, one, turned, x_out, x_outd, step, aexp, sexp, sln, adt_ok, cums, cum_out, decs, e2, unit, masked, mexp, mt, xdok,
         diag, offd, stg, yv, stv, ysq, ymean, yroot, yn, yt, ya, yd) = signals(
            nc, ctx, "nrm_in s_one s_turned s_x_out s_x_outd s_step s_aexp s_sexp s_sln s_adt s_cums s_cum_out s_decs s_e2 s_unit s_masked "
            "s_mexp s_mt s_xd s_diag s_off s_states s_yv s_stv s_ysq s_ymean s_yroot s_yn s_yt s_ya s_yd")
        block = ctx.enter_context(nc.Block())
        BT, CT = m_.xbcT[:, KT], m_.xbcT[:, KT + 1]
        yT = lambda kt: m_.xs[:].rearrange("p t d -> p (t d)")[:, kt * SEQ:(kt + 1) * SEQ]
        tmp2 = lambda v: m_.xs[:, v // SG, v % SG * GW:(v % SG + 1) * GW]

        @block.sync
        def _(sp):
            sp.dma_start(nrm[:], t["ssd_norm"]).then_inc(nrm_in, 16)

        @block.gpsimd
        def _(pool):
            pool.memset(ones[:], 1.0).then_inc(one, 1)
            pool.wait_ge(ysq, UN)
            pool.tensor_scalar(sg[:, 1], sg[:, 0], 1.0 / GW, EPS, ALU.mult, ALU.add).then_inc(ymean, 1)
            pool.wait_ge(ymean, 1)
            pool.tensor_tensor(sg[:, 2], sg[:, 1], c.half[:, 0:UN], ALU.pow).then_inc(yroot, 1)

        @block.tensor
        def _(pe):
            for cc in range(TT):
                if cc >= 1:
                    pe.wait_ge(x_out, 2 * cc)
                    pe.wait_ge(x_outd, cc)
                for j in range(KT + 1):
                    mm = pe.transpose(c.bank[j // 4][:, (j % 4) * P:(j % 4 + 1) * P], m_.xbcT[:, j, cc * P:(cc + 1) * P], c.ident)
                mm.then_inc(turned, 1)
            pe.wait_ge(one, 1)
            pe.wait_ge(adt_ok, 1)
            for cc in range(TT):
                pe.matmul(c.bank[3][:, cc * SH:(cc + 1) * SH], c.tri, adt[:, cc], start=True, stop=True)
                mm = pe.matmul(c.bank[3][:, (TT + cc) * SH:(TT + cc + 1) * SH], ones[:], adt[:, cc], start=True, stop=True)
            mm.then_inc(cums, 1)
            pe.wait_ge(x_out, 2 * TT)
            pe.wait_ge(x_outd, TT)
            pe.wait_ge(cum_out, 1)

            def decays(v):
                cc, g = divmod(v, SG)
                rows, tok = slice(64 * g, 64 * g + 64), slice(cc * P, (cc + 1) * P)
                if v >= 1:
                    pe.wait_ge(masked, v)
                if v >= 2:
                    pe.wait_ge(unit, v - 1)
                pe.matmul(c.bank[4][:, 0:P], BT[rows, tok], CT[rows, tok], start=True, stop=True)
                for h in range(HG):
                    a1 = adt[:, cc, g * HG + h:g * HG + h + 1].broadcast_to([P, P])
                    mm = pe.matmul(c.bank[2 * (v % 2) + h // 4][:, (h % 4) * P:(h % 4 + 1) * P], a1, c.tri, start=True, stop=True)
                mm.then_inc(cums, 1)

            decays(0)
            for v in range(UN):
                cc, g = divmod(v, SG)
                rows, tok = slice(64 * g, 64 * g + 64), slice(cc * P, (cc + 1) * P)
                if v + 1 < UN:
                    decays(v + 1)
                pe.wait_ge(mt, v + 1)
                pe.wait_ge(xdok, cc + 1)
                if v >= 1:
                    pe.wait_ge(yv, v)
                for h in range(HG):
                    mm = pe.matmul(c.bank[5][:, h * SP_:(h + 1) * SP_], E[:, v % 2, h], xd[:, g * GW + h * SP_:g * GW + (h + 1) * SP_],
                                   start=True, stop=True)
                mm.then_inc(diag, 1)
                if cc >= 1:
                    pe.wait_ge(stv, cc)
                    pe.matmul(c.bank[6][:], CT[rows, tok], st[rows, :], start=True, stop=True).then_inc(offd, 1)
                if cc + 1 < TT:
                    if cc >= 1 and g == 0:
                        pe.wait_ge(stv, cc)
                    pe.matmul(c.bank[7][rows, :], bt[:, cc, rows], xdd[:, g * GW:(g + 1) * GW], start=True, stop=True).then_inc(stg, 1)
            for kt in range(KT):
                if kt == 0:
                    pe.wait_ge(yn, TT)
                if kt >= 4:
                    pe.wait_ge(yd if kt % 2 else ya, kt // 2 - 1)
                for tt in range(TT):
                    mm = pe.transpose(c.bank[kt % 4][:, tt * P:(tt + 1) * P], y[:, tt, kt * P:(kt + 1) * P], c.ident)
                mm.then_inc(yt, 1)

        @block.scalar
        def _(act):
            act.activation(aneg[:], c.rows[:, R_ALOG:R_ALOG + SH], ACT.Exp).then_inc(aexp, 1)
            act.wait_ge(step, 1)
            act.activation(sp_[:, 1], sp_[:, 0], ACT.Exp).then_inc(sexp, 1)
            act.wait_ge(step, 2)
            act.activation(sp_[:, 3], sp_[:, 2], ACT.Ln).then_inc(sln, 1)
            for cc in range(TT):
                act.wait_ge(turned, cc + 1)
                act.activation(m_.xs[:, cc, 0:512], c.bank[0][:], ACT.Copy).then_inc(x_out, 1)
                act.activation(bt[:, cc], c.bank[2][:, 0:P], ACT.Copy).then_inc(x_out, 1)
            act.wait_ge(decs, 1)
            act.activation(eacs[:], acs[:, 0], ACT.Exp)
            act.activation(etot[:], acs[:, 1], ACT.Exp)
            act.activation(dst[:], dst[:], ACT.Exp).then_inc(e2, 1)
            for v in range(UN):
                act.wait_ge(unit, v + 1)
                act.activation(E[:, v % 2], E[:, v % 2], ACT.Exp).then_inc(mexp, 1)
            for v in range(UN):
                cc, g = divmod(v, SG)
                act.wait_ge(yv, UN + v + 1)
                act.activation(tmp2(v), y[:, cc, g * GW:(g + 1) * GW], ACT.Square, accum_out=sg[:, 0, v:v + 1]).then_inc(ysq, 1)
            for kt in range(0, KT, 2):
                act.wait_ge(yt, kt + 1)
                act.activation(yT(kt), c.bank[kt % 4][:], ACT.Copy).then_inc(ya, 1)

        @block.vector
        def _(dve):
            n = [0]

            def link(ins):
                n[0] += 1
                ins.then_inc(step, 1)
                dve.wait_ge(step, n[0])

            link(dve.scalar_tensor_tensor(out=sp_[:, 0], in0=m_.dt[:], scalar=-1.0, in1=m_.dt[:], op0=ALU.mult, op1=ALU.min))
            dve.wait_ge(sexp, 1)
            link(dve.tensor_scalar(sp_[:, 2], sp_[:, 1], 1.0, None, ALU.add))
            link(dve.tensor_scalar(sp_[:, 4], sp_[:, 2], -1.0, None, ALU.add))
            link(dve.tensor_scalar(sp_[:, 5], sp_[:, 4], 0.0, None, ALU.is_equal))
            link(dve.tensor_tensor(sp_[:, 4], sp_[:, 4], sp_[:, 5], ALU.add))
            link(dve.reciprocal(sp_[:, 4], sp_[:, 4]))
            dve.wait_ge(sln, 1)
            link(dve.tensor_tensor(sp_[:, 3], sp_[:, 3], sp_[:, 5], ALU.add))
            link(dve.tensor_tensor(sp_[:, 3], sp_[:, 3], sp_[:, 1], ALU.mult))
            link(dve.tensor_tensor(sp_[:, 3], sp_[:, 3], sp_[:, 4], ALU.mult))
            link(dve.scalar_tensor_tensor(out=m_.dt[:], in0=m_.dt[:], scalar=0.0, in1=sp_[:, 3], op0=ALU.max, op1=ALU.add))
            dve.wait_ge(aexp, 1)
            link(dve.tensor_scalar(sp_[:, 0], m_.dt[:], -1.0, None, ALU.mult))
            dve.tensor_tensor(adt[:], sp_[:, 0], mid(aneg[:], TT), ALU.mult).then_inc(adt_ok, 1)
            for cc in range(TT):
                dve.wait_ge(turned, cc + 1)
                dve.tensor_copy(m_.xs[:, cc, 512:], c.bank[1][:]).then_inc(x_outd, 1)
            dve.wait_ge(cums, 1)
            dve.tensor_copy(acs[:].rearrange("p a t h -> p (a t h)"), c.bank[3][:, 0:2 * TT * SH]).then_inc(cum_out, 1)
            dve.wait_ge(cum_out, 1)
            dve.tensor_tensor(dst[:], acs[:, 1], acs[:, 0], ALU.subtract).then_inc(decs, 1)
            dve.wait_ge(e2, 1)
            for g in range(SG):
                last = dve.tensor_copy(dec[64 * g:64 * g + 64], etot[64 * g:64 * g + 64, :, g * HG:(g + 1) * HG])
            link(last)

            def decays(v):
                cc, g = divmod(v, SG)
                dve.wait_ge(cums, v + 2)
                if v >= 2:
                    dve.wait_ge(diag, v - 1)
                dve.tensor_tensor(cbm[:, v % 2], c.bank[4][:, 0:P], c.tri, ALU.mult).then_inc(masked, 1)
                for h in range(HG):
                    last = dve.tensor_scalar(E[:, v % 2, h], c.bank[2 * (v % 2) + h // 4][:, (h % 4) * P:(h % 4 + 1) * P],
                                             acs[:, 0, cc, g * HG + h:g * HG + h + 1], 0.0, ALU.subtract, ALU.min)
                last.then_inc(unit, 1)

            decays(0)
            for v in range(UN):
                cc, g = divmod(v, SG)
                heads = slice(g * HG, (g + 1) * HG)
                if g == 0:
                    if cc >= 1:
                        dve.wait_ge(diag, v)
                        dve.wait_ge(stg, 2 * cc)
                    xs16 = m_.xs[:, cc].rearrange("p (h w) -> p h w", w=SP_)
                    link(dve.tensor_tensor(xd[:].rearrange("p (h w) -> p h w", w=SP_), xs16, bc(m_.dt[:, cc], SP_), ALU.mult))
                    dve.tensor_tensor(xdd[:].rearrange("p (h w) -> p h w", w=SP_), xd[:].rearrange("p (h w) -> p h w", w=SP_),
                                      bc(dst[:, cc], SP_), ALU.mult).then_inc(xdok, 1)
                if v + 1 < UN:
                    decays(v + 1)
                dve.wait_ge(mexp, v + 1)
                dve.tensor_tensor(E[:, v % 2], E[:, v % 2], mid(cbm[:, v % 2], HG), ALU.mult).then_inc(mt, 1)
                yo = y[:, cc, g * GW:(g + 1) * GW]
                yo3 = yo.rearrange("p (h w) -> p h w", w=SP_)
                xs3 = m_.xs[:, cc, g * GW:(g + 1) * GW].rearrange("p (h w) -> p h w", w=SP_)
                dsk = c.rows[:, R_DSK + g * HG:R_DSK + (g + 1) * HG]
                link(dve.tensor_tensor(yo3, xs3, bc(dsk, SP_), ALU.mult))
                if cc >= 1:
                    dve.wait_ge(offd, 2 * (cc - 1) + g + 1)
                    link(dve.tensor_tensor(tmp[:].rearrange("p (h w) -> p h w", w=SP_), c.bank[6][:].rearrange("p (h w) -> p h w", w=SP_),
                                           bc(eacs[:, cc, heads], SP_), ALU.mult))
                    link(dve.tensor_tensor(yo, yo, tmp[:], ALU.add))
                dve.wait_ge(diag, v + 1)
                dve.tensor_tensor(yo, c.bank[5][:], yo, ALU.add).then_inc(yv, 1)
                if g == SG - 1 and cc + 1 < TT:
                    dve.wait_ge(stg, 2 * cc + 2)
                    if cc == 0:
                        dve.tensor_copy(st[:], c.bank[7][:]).then_inc(stv, 1)
                    else:
                        st3 = st[:].rearrange("p (h w) -> p h w", w=SP_)
                        dve.wait_ge(offd, 2 * cc)
                        dve.wait_ge(stv, cc)
                        link(dve.tensor_tensor(st3, st3, bc(dec[:, cc], SP_), ALU.mult))
                        dve.tensor_tensor(st[:], c.bank[7][:], st[:], ALU.add).then_inc(stv, 1)
            dve.wait_ge(yv, UN)
            for v in range(UN):
                cc, g = divmod(v, SG)
                yo = y[:, cc, g * GW:(g + 1) * GW]
                dve.tensor_tensor(yo, yo, m_.zs[:, cc, g * GW:(g + 1) * GW], ALU.mult).then_inc(yv, 1)
            dve.wait_ge(yroot, 1)
            dve.wait_ge(nrm_in, 16)
            for v in range(UN):
                cc, g = divmod(v, SG)
                yo = y[:, cc, g * GW:(g + 1) * GW]
                last = dve.tensor_scalar(yo, yo, sg[:, 2, v:v + 1], None, ALU.mult)
            link(last)
            for cc in range(TT):
                dve.tensor_tensor(y[:, cc], y[:, cc], nrm[:], ALU.mult).then_inc(yn, 1)
            for kt in range(1, KT, 2):
                dve.wait_ge(yt, kt + 1)
                dve.tensor_copy(yT(kt), c.bank[kt % 4][:]).then_inc(yd, 1)


def phase_mixer_out(c, m_):
    nc, t = c.nc, c.t
    with ExitStack() as ctx:
        pT = ctx.enter_context(nc.sbuf_tensor("pT_sb", [P, PLE // P, SEQ], F32))
        npost = ctx.enter_context(nc.sbuf_tensor("npost", [P, D], F32))
        gt = ctx.enter_context(nc.sbuf_tensor("gt", [P, 2, 512], F32))
        (in0, in1, grp, out0, s1, s2, pg, gg, gsig, xo, stored, step) = signals(
            nc, ctx, "o_in0 o_in1 o_grp o_out o_s1 o_s2 o_pg o_gg o_gsig o_xo o_stored o_step")
        block = ctx.enter_context(nc.Block())
        yssdT = m_.xs[:].rearrange("p t d -> p (t d)").rearrange("p (k s) -> p k s", k=KT)
        MX = m_.zs
        junk = m_.xbcT[:, 0:KT].rearrange("p a b -> p (a b)").rearrange("p (t d) -> p t d", t=TT)
        GR = 2 * TT

        @block.sync
        def _(sp):
            sp.dma_start(pT[:], t["pT"]).then_inc(in0, 16)
            sp.dma_start(npost[:], t["norm_post"]).then_inc(in1, 16)
            for b in range(B_MIX, NB - RING):
                sp.wait_ge(grp, TT * ((b - B_MIX) // 2 + 1))
                c.load_w(sp, b + RING)
            out = t["out"].rearrange("(t p) d -> p t d", p=P)
            for g in range(GR):
                nh, tt = divmod(g, TT)
                sp.wait_ge(xo, g + 1)
                sp.dma_start(out[:, tt, nh * 512:(nh + 1) * 512], c.X[:, tt, nh * 512:(nh + 1) * 512]).then_inc(stored, 16)
            sp.wait_ge(stored, 16 * GR)

        @block.tensor
        def _(pe):
            for g in range(GR):
                nh, tt = divmod(g, TT)
                if tt == 0:
                    c.wait_w(pe, B_MIX + 2 * nh)
                    c.wait_w(pe, B_MIX + 2 * nh + 1)
                if g >= 4:
                    pe.wait_ge(out0, g - 3)
                for k in range(2 * KT):
                    w = c.w(B_MIX + 2 * nh + k // KT, KT * 512, 512)
                    src = yssdT if k < KT else m_.yscT
                    mm = pe.matmul(c.bank[g % 4][:], src[:, k % KT, tt * P:(tt + 1) * P], w[:, k % KT], start=k == 0, stop=k == 2 * KT - 1)
                mm.then_inc(grp, 1)
            pe.wait_ge(out0, GR)
            transposes_pe(pe, c, c.X, T_POST)
            transposed_pe(pe, c, T_POST)
            pe.wait_ge(in0, 16)
            c.wait_w(pe, B_PLE)
            ple = c.w(B_PLE, PLE // P * D, D)
            for g in range(GR):
                nh, tt = divmod(g, TT)
                if tt == 0:
                    c.wait_w(pe, B_GATE + nh)
                if g >= 4:
                    pe.wait_ge(xo, g - 3)
                    pe.wait_ge(gsig, g - 3)
                tok = slice(tt * P, (tt + 1) * P)
                w = c.w(B_GATE + nh, KT * 512, 512)
                for k in range(KT):
                    mm = pe.matmul(c.bank[g % 4][:], c.XT[:, k, tok], w[:, k], start=k == 0, stop=k == KT - 1)
                mm.then_inc(gg, 1)
                for k in range(PLE // P):
                    mm = pe.matmul(c.bank[4 + g % 4][:], pT[:, k, tok], ple[:, k, nh * 512:(nh + 1) * 512], start=k == 0, stop=k == PLE // P - 1)
                mm.then_inc(pg, 1)

        @block.scalar
        def _(act):
            act.wait_ge(out0, GR)
            norm_sums(act, c, MX, junk)
            gains_act(act, c, None, T_POST)
            for g in range(GR):
                act.wait_ge(gg, g + 1)
                if g >= 2:
                    act.wait_ge(xo, g - 1)
                act.activation(gt[:, g % 2], c.bank[g % 4][:], ACT.Sigmoid).then_inc(gsig, 1)

        @block.gpsimd
        def _(pool):
            norm_rsqrt(pool, c, N_POST)

        @block.vector
        def _(dve):
            for g in range(GR):
                nh, tt = divmod(g, TT)
                dve.wait_ge(grp, g + 1)
                dve.tensor_copy(MX[:, tt, nh * 512:(nh + 1) * 512], c.bank[g % 4][:]).then_inc(out0, 1)
            dve.wait_ge(c.rooted, N_POST + 1)
            dve.wait_ge(in1, 16)
            for tt in range(TT):
                dve.tensor_scalar(MX[:, tt], MX[:, tt], c.rn[:, tt:tt + 1], None, ALU.mult).then_inc(s1, 1)
            for tt in range(TT):
                dve.wait_ge(s1, tt + 1)
                dve.tensor_tensor(MX[:, tt], MX[:, tt], npost[:], ALU.mult).then_inc(s2, 1)
            for tt in range(TT):
                dve.wait_ge(s2, tt + 1)
                dve.tensor_tensor(c.X[:, tt], c.X[:, tt], MX[:, tt], ALU.add).then_inc(c.scaled, 1)
            gains_dve(dve, c, None, T_POST)
            for g in range(GR):
                nh, tt = divmod(g, TT)
                xs = c.X[:, tt, nh * 512:(nh + 1) * 512]
                dve.wait_ge(pg, g + 1)
                dve.wait_ge(gsig, g + 1)
                dve.tensor_tensor(gt[:, g % 2], c.bank[4 + g % 4][:], gt[:, g % 2], ALU.mult).then_inc(step, 1)
                dve.wait_ge(step, g + 1)
                dve.tensor_tensor(xs, xs, gt[:, g % 2], ALU.add).then_inc(xo, 1)


class Attention:
    def __init__(self, c, ctx):
        sb = lambda name, shape: ctx.enter_context(c.nc.sbuf_tensor(name, shape, F32))
        self.y = sb("y", [P, TT, 2 * ATT_W])
        self.qz = sb("qz", [P, HEADS, SEQ])
        self.kT = sb("kT", [P, HEADS // 2, SEQ])
        self.qzb = sb("qzb", [P, HEADS, SEQ])
        self.va = c.ur[:].rearrange("p r (a w) -> p (r a) w", w=ATT_W)
        self.kTb = c.ar[:, 0]
        self.vb = c.ar[:, 1].rearrange("p (t w) -> p t w", t=TT)


def build(nc, t, upto=99):
    with ExitStack() as ctx:
        c = Core(nc, ctx, t)
        with ExitStack() as tmp:
            ijg = tmp.enter_context(nc.sbuf_tensor("ijg", [P, 3, SEQ], F32))
            early = Early(c, tmp)
            with ExitStack() as half:
                c.ring(half, "W1")
                with ExitStack() as att:
                    a = Attention(c, att)
                    phase_project(c, a)
                    if upto >= 2:
                        phase_attend(c, a)
                    if upto >= 3:
                        phase_merge(c, a)
                if upto >= 4:
                    phase_choose(c, ijg, early)
            if upto >= 5:
                phase_gates(c, ijg, early)
        if upto >= 6:
            phase_experts(c)
        c.ring(ctx, "W2")
        if upto >= 7:
            phase_between(c)
        if upto >= 8:
            with ExitStack() as mix:
                m_ = Mixer(nc, mix)
                phase_mixer_in(c, m_)
                if upto >= 9:
                    phase_scan(c, m_)
                if upto >= 10:
                    phase_mixer_out(c, m_)
        if upto < 10:
            dumped = ctx.enter_context(nc.semaphore("dumped"))
            with nc.Block() as block:
                @block.sync
                def _(sp):
                    sp.dma_start(t["out"].rearrange("(t p) d -> p t d", p=P), c.X[:] if upto != 1 else c.XT[:].rearrange("p a b -> p (a b)").rearrange("p (t d) -> p t d", t=TT)).then_inc(dumped, 16)
                    sp.wait_ge(dumped, 16)



def _rows(w, cols, k=None):
    w = w[:, cols]
    return w.reshape(w.shape[0] // P, P, w.shape[1]).transpose(1, 0, 2)


def _tables():
    tab = np.zeros((P, NTAB), np.float32)
    tab[:, T_ID:T_ID + P] = np.eye(P)
    tab[:, T_TRI:T_TRI + P] = np.triu(np.ones((P, P)))
    tab[:, T_IOTA:T_IOTA + P] = np.arange(P)
    nf = DH // 4
    inv = (np.float32(ROPE_THETA) ** (-np.arange(nf, dtype=np.float32) / np.float32(nf))).astype(np.float32)
    tok = np.arange(SEQ)
    for s, pos in enumerate((tok // GRID_W, tok % GRID_W)):
        ang = pos.astype(np.float32)[:, None] * inv[None, :]
        co, si = np.cos(ang).astype(np.float32), np.sin(ang).astype(np.float32)
        for f in range(2):
            at = s * 2 * nf + f * nf
            for tt in range(TT):
                rows = slice(tt * P, (tt + 1) * P)
                tab[:, T_COS + tt * DH + at:T_COS + tt * DH + at + nf] = co[rows]
                tab[:, T_SIN + tt * DH + at:T_SIN + tt * DH + at + nf] = si[rows] * (1 if f else -1)
    return tab


def _bias(rpb):
    q = np.arange(GRID_W)
    start = np.clip(q - WIN_W // 2, 0, GRID_W - WIN_W)
    k = np.arange(GRID_W)
    inside = (k[None] >= start[:, None]) & (k[None] < start[:, None] + WIN_W)
    dc = np.clip(k[None] - q[:, None], -(WIN_W - 1), WIN_W - 1) + WIN_W - 1
    out = np.full((HEADS, 2, GRID_W, BIAS_ROWS, GRID_W), NEG, np.float32)
    for par in range(2):
        for j in range(BIAS_ROWS):
            dr = j - par
            if 0 <= dr < 2 * WIN_H - 1:
                out[:, par, :, j, :] = np.where(inside[None], rpb[:, dr][:, dc], np.float32(NEG))
    return out.reshape(HEADS, P, BIAS_ROWS * GRID_W)


def pack(x, norm1_g, w_in, na_rpb, gqa_q_norm_g, gqa_k_norm_g, w_proj_a, w_proj_b, w_out, norm2_g,
         peer_w_q, peer_sub_keys, peer_u, peer_v, norm_f_g, p_2, norm_pre_2, norm_post_2, w_in_2,
         ssd_conv_w_2, ssd_conv_b_2, dt_bias_2, a_log_2, d_skip_2, ssd_norm_2, sc_conv_w_2, w_out_2,
         w_ple_gate_2, w_ple_proj_2):
    w_in, w2 = w_in[0], w_in_2[0]
    blocks = np.zeros((NB, P, WBLK), np.float32)

    def put(b, *parts):
        at = 0
        for w in parts:
            n = w.shape[1] * w.shape[2]
            blocks[b, :, at:at + n] = w.reshape(P, n)
            at += n

    cut = lambda a, n: slice(a, a + n)
    for b in range(4):
        put(b, _rows(w_in, cut(512 * b, 512)))
    put(B_KVB, _rows(w_in, cut(2048, 256)))
    for m in range(KT):
        put(B_MERGE + m, _rows(w_in, cut(2304 + P * m, P)), _rows(w_in, cut(3328 + P * m, P)),
            _rows(w_proj_a[0], cut(P * m, P)), _rows(w_proj_b[0], cut(P * m, P)))
        s0 = (D + 2 * SG * NS) + SH + D
        put(B_SC + m, *[_rows(w2, cut(s0 + D * j + P * m, P)) for j in (2, 0, 1, 3)])
    for b in range(2):
        put(B_OUT + b, _rows(w_out[0], cut(512 * b, 512)))
        put(B_Z + b, _rows(w2, cut(D + 2 * SG * NS + SH + 512 * b, 512)))
        put(B_GATE + b, _rows(w_ple_gate_2[0], cut(512 * b, 512)))
        for k in range(2):
            put(B_MIX + 2 * b + k, _rows(w_out_2[0][D * k:D * (k + 1)], cut(512 * b, 512)))
    for b in range(4):
        put(B_PQ + b, _rows(peer_w_q[0], cut(512 * b, 512)))
    put(B_KEYS, peer_sub_keys[0].reshape(2 * PH, PK, P).transpose(2, 0, 1))
    for b in range(3):
        put(B_XBC + b, _rows(w2, cut(512 * b, min(512, XBC_TILES * P - 512 * b))))
    put(B_DT, _rows(w2, cut(D + 2 * SG * NS, SH)))
    put(B_PLE, _rows(w_ple_proj_2[0], cut(0, D)))

    col = lambda v: v.reshape(-1, P).T
    cols = np.zeros((P, NCOL), np.float32)
    for at, v in ((C_G1, norm1_g[0]), (C_G2, norm2_g[0]), (C_GPRE, norm_pre_2[0]), (C_CB, ssd_conv_b_2[0])):
        cols[:, at:at + v.size // P] = col(v)
    cols[:, C_CW:C_CB] = ssd_conv_w_2[0].reshape(CONV_W, XBC_TILES, P).transpose(2, 1, 0).reshape(P, -1)
    cols[:, C_SW:NCOL] = sc_conv_w_2[0].reshape(SC_W, KT, P).transpose(2, 1, 0).reshape(P, -1)
    row = np.concatenate([np.tile(gqa_q_norm_g[0], HEADS), np.tile(gqa_k_norm_g[0], KV_HEADS), dt_bias_2[0], a_log_2[0], d_skip_2[0]])
    wide = lambda v: np.ascontiguousarray(np.broadcast_to(v.reshape(1, -1), (P, v.size)))
    return {
        "x": x[0], "tab": _tables(), "cols": cols, "rows": wide(row), "bias": _bias(na_rpb[0]),
        "w_stream": blocks,
        "u": peer_u[0].reshape(PK, P, KT, P).transpose(0, 3, 2, 1),
        "v": peer_v[0].reshape(PK, P, D),
        "norm_f": wide(norm_f_g), "norm_post": wide(norm_post_2[0]), "ssd_norm": wide(ssd_norm_2[0]),
        "pT": p_2[0, 0].T.reshape(PLE // P, P, SEQ).transpose(1, 0, 2),
    }


def kernel(**inputs):
    import concourse.bacc as bacc
    from concourse.bass_utils import run_bass_kernel_spmd

    nc = bacc.Bacc("TRN2", target_bir_lowering=False, num_devices=1)
    arrays, tensors = {}, {}
    for name, a in pack(**{k: np.asarray(v) for k, v in inputs.items()}).items():
        a = np.ascontiguousarray(a)
        arrays[f"in_{name}"] = a
        tensors[name] = nc.dram_tensor(f"in_{name}", a.shape, mybir.dt.from_np(a.dtype), kind="ExternalInput").ap()
    tensors["early"] = nc.dram_tensor("early", (EARLY, P, SEQ), F32).ap()
    tensors["gates"] = nc.dram_tensor("gates", (PK, PK, SEQ), F32).ap()
    tensors["out"] = nc.dram_tensor("out_x", (SEQ, D), F32, kind="ExternalOutput").ap()
    build(nc, tensors)
    r = run_bass_kernel_spmd(nc, [arrays], core_ids=[0])
    return r.results[0]["out_x"].reshape(1, SEQ, D)
```

```python
from contextlib import ExitStack

import numpy as np

import concourse.bass as bass
from concourse import mybir

F32 = mybir.dt.float32
F32R = mybir.dt.float32r
U32 = mybir.dt.uint32
ALU = mybir.AluOpType
ACT = mybir.ActivationFunctionType
AX = mybir.AxisListType.X

P = 128
SEQ = 512
TT = SEQ // P
D = 1024
KT = D // P
EPS = 1e-6
GRID_W = 64
DH = 64
HEADS = 8
WIN_H, WIN_W = 8, 16
ATT_W = HEADS * DH
KV_HEADS = 2
BIAS_ROWS = 2 * WIN_H
ROPE_THETA = 10000.0

PK = 128
PH = 8
TOPK = 16
EXPERTS = PK * PK
SLOTS = PH * TOPK
EG = 4
NG = PK // EG
E_CHOOSE, E_GATES, E_STORE = PK // 4, PK // 4, 8
EARLY = E_CHOOSE + E_GATES + E_STORE

SH = 16
SP_ = 64
SG = 2
HG = SH // SG
NS = 64
CONV_W, SC_W = 4, 3
XBC_TILES = (D + 2 * SG * NS) // P
PLE = 256

NEG = -1.0e30
LOWEST = -3.4028235e38

WBLK = 4096
RING = 3
B_QB, B_KVB, B_QA, B_KA, B_VA = range(5)
B_MERGE = 5
B_OUT = B_MERGE + KT
B_PQ = B_OUT + 2
B_KEYS = B_PQ + 4
B_MIX = B_KEYS + 1
B_PLE = B_MIX + 4
B_GATE = B_PLE + 1
NB = B_GATE + 2

WIN = 2048
RAW = 4
ZC = 256
I_XBC = 0
I_DT = XBC_TILES // 2
I_Z = I_DT + 1
I_SC = I_Z + D // ZC
NI = I_SC + 2 * KT

C_G1, C_G2, C_GPRE = 0, KT, 2 * KT
C_CW = 3 * KT
C_CB = C_CW + XBC_TILES * CONV_W
C_SW = C_CB + XBC_TILES
NCOL = C_SW + KT * SC_W
T_ID, T_TRI, T_IOTA, T_COS = 0, P, 2 * P, 3 * P
T_SIN = T_COS + TT * DH
NTAB = T_SIN + TT * DH
R_GQK = 0
R_DTB = R_GQK + ATT_W + KV_HEADS * DH
R_ALOG = R_DTB + SH
R_DSK = R_ALOG + SH
NROW = R_DSK + SH


def bc(ap, n):
    return ap.unsqueeze(len(ap.shape)).broadcast_to(list(ap.shape) + [n])


def mid(ap, n):
    return ap.unsqueeze(1).broadcast_to([ap.shape[0], n, ap.shape[1]])


class Core:

    def __init__(self, nc, ctx, t):
        self.nc, self.t = nc, t
        sb = lambda name, shape, dt=F32: ctx.enter_context(nc.sbuf_tensor(name, shape, dt))
        self.X = sb("x_res", [P, TT, D])
        self.XT = sb("XT", [P, KT, SEQ])
        self.tab = sb("tab_sb", [P, NTAB])
        self.cols = sb("cols_sb", [P, NCOL])
        self.rows = sb("rows_sb", [P, NROW])
        self.ss = sb("ss", [P, TT])
        self.ms = sb("ms", [P, TT])
        self.rn = sb("rn", [P, TT])
        self.half = sb("half", [P, 48])
        self.bank = [ctx.enter_context(nc.psum_tensor(f"bank{i}", [P, 512], F32)) for i in range(8)]
        self.w_loaded = [ctx.enter_context(nc.semaphore(f"w_loaded{i}")) for i in range(RING)]
        self.ur = sb("ur", [P, 2, KT * P])
        self.ar = sb("ar", [P, 2, SEQ])
        self.squared, self.meaned, self.rooted, self.scaled, self.turned, self.out_a, self.out_d = signals(
            nc, ctx, "squared meaned rooted scaled turned out_a out_d")
        self.xhi, self.xlo, self.whi, self.wlo = signals(nc, ctx, "x_hi x_lo w_hi w_lo")
        self.ident = self.tab[:, T_ID:T_ID + P]
        self.tri = self.tab[:, T_TRI:T_TRI + P]
        self.iota = self.tab[:, T_IOTA:T_IOTA + P]

    def ring(self, ctx, name):
        self.W = ctx.enter_context(self.nc.sbuf_tensor(name, [P, RING, WBLK], F32))

    def w(self, b, n, cols=P):
        return self.W[:, b % RING, 0:n].rearrange("p (k c) -> p k c", c=cols)

    def load_w(self, sp, b):
        sp.dma_start(self.W[:, b % RING, :], self.t["w_stream"][b]).then_inc(self.w_loaded[b % RING], 16)

    def wait_w(self, pe, b):
        pe.wait_ge(self.w_loaded[b % RING], 16 * (b // RING + 1))


def signals(nc, ctx, names):
    return [ctx.enter_context(nc.semaphore(n)) for n in names.split()]



N_FIRST, N_EXPERTS, N_FINAL, N_PRE, N_POST = range(5)


def norm_sums(act, c, src, junk, made=None, at=0):
    for tt in range(TT):
        if made is not None:
            act.wait_ge(made, at + tt + 1)
        act.activation(junk[:, tt], src[:, tt], ACT.Square, accum_out=c.ss[:, tt:tt + 1]).then_inc(c.squared, 1)


def norm_rsqrt(pool, c, n):
    pool.wait_ge(c.squared, (n + 1) * TT)
    pool.tensor_scalar(c.ms[:], c.ss[:], 1.0 / D, EPS, ALU.mult, ALU.add).then_inc(c.meaned, 1)
    pool.wait_ge(c.meaned, n + 1)
    pool.tensor_tensor(c.rn[:], c.ms[:], c.half[:, 0:TT], ALU.pow).then_inc(c.rooted, 1)


S_FIRST, S_MERGED, S_QUERY, S_EXPERTS, S_PRE = (KT * i for i in range(5))
W_MERGE, W_QUERY, W_PRE = 0, 2 * KT + 2 * 4, 2 * KT + 2 * 4 + 2 * PH
T_FIRST, T_EXPERTS, T_PRE, T_POST = range(4)


def transposes_pe(pe, c, src, n):
    pe.wait_ge(c.scaled, (n + 1) * TT)
    for kt in range(KT):
        if kt >= 4:
            pe.wait_ge(c.out_d if kt % 2 else c.out_a, n * KT // 2 + kt // 2 - 1)
        for tt in range(TT):
            mm = pe.transpose(c.bank[kt % 4][:, tt * P:(tt + 1) * P], src[:, tt, kt * P:(kt + 1) * P], c.ident)
        mm.then_inc(c.turned, 1)


def transposed_pe(pe, c, n):
    pe.wait_ge(c.out_a, (n + 1) * KT // 2)
    pe.wait_ge(c.out_d, (n + 1) * KT // 2)


def gains_act(act, c, col, n):
    for kt in range(0, KT, 2):
        act.wait_ge(c.turned, n * KT + kt + 1)
        act.activation(c.XT[:, kt], c.bank[kt % 4][:], ACT.Copy, scale=1.0 if col is None else c.cols[:, col + kt:col + kt + 1]).then_inc(c.out_a, 1)


def gains_dve(dve, c, col, n):
    for kt in range(1, KT, 2):
        dve.wait_ge(c.turned, n * KT + kt + 1)
        gain = 1.0 if col is None else c.cols[:, col + kt:col + kt + 1]
        dve.tensor_scalar(c.XT[:, kt], c.bank[kt % 4][:], gain, None, ALU.mult).then_inc(c.out_d, 1)


def phase_project(c, a):
    nc, t = c.nc, c.t
    with ExitStack() as ctx:
        HN = ctx.enter_context(nc.sbuf_tensor("HN", [P, TT, D], F32))
        QK = ctx.enter_context(nc.sbuf_tensor("QK", [P, TT, ATT_W + P], F32))
        S1 = ctx.enter_context(nc.sbuf_tensor("S1", [P, TT, ATT_W + P], F32))
        S2 = ctx.enter_context(nc.sbuf_tensor("S2", [P, TT, ATT_W + P], F32))
        KR = a.y[:, :, 0:P]
        hs = ctx.enter_context(nc.sbuf_tensor("hs", [P, 3, 40], F32))
        (x0, x1, x2, x3, const_in, grp, grp_a, grp_d,
         set0, step, hsum, hroot, roped, rturn, rout, rout_d) = signals(
            nc, ctx, "x_in0 x_in1 x_in2 x_in3 const_in grp grp_a grp_d "
            "set0 step hsum hroot roped rturn rout rout_d")
        x_in = (x0, x1, x2, x3)
        qpad = HN[:].rearrange("p t (h w) -> p t h w", w=P)
        block = ctx.enter_context(nc.Block())
        GROUPS, SHARED = 5 * TT, 2 * TT
        HR = HEADS + KV_HEADS

        def project_out(g, copy, sem):
            src = c.bank[4 + g % 4]
            i = g % 4
            if g < 4:
                copy(QK[:, i, 0:ATT_W], src[:], 1.0).then_inc(sem, 1)
            elif g < 8:
                copy(QK[:, i, ATT_W:], src[:, 0:P], 1.0)
                copy(a.vb[:, i], src[:, P:2 * P], 1.0).then_inc(sem, 1)
            elif g < 12:
                copy(a.qz[0:64, 2 * i], src[0:64, :], DH ** -0.5)
                copy(a.qz[64:128, 2 * i + 1], src[64:128, :], DH ** -0.5).then_inc(sem, 1)
            elif g < 16:
                copy(a.kT[:, i], src[:], 1.0).then_inc(sem, 1)
            else:
                copy(a.va[:, i], src[:], 1.0).then_inc(sem, 1)

        @block.sync
        def _(sp):
            for tt in range(TT):
                sp.dma_start(c.X[:, tt], t["x"][tt * P:(tt + 1) * P, :]).then_inc(x_in[tt], 16)
            for to, name in ((c.tab, "tab"), (c.cols, "cols"), (c.rows, "rows")):
                sp.dma_start(to[:], t[name]).then_inc(const_in, 16)
            for b in range(RING):
                c.load_w(sp, b)
            for b in range(5):
                sp.wait_ge(grp, 4 * (b + 1))
                c.load_w(sp, b + RING)

        @block.scalar
        def _(act):
            for tt in range(TT):
                act.wait_ge(x_in[tt], 16)
                act.activation(HN[:, tt], c.X[:, tt], ACT.Square, accum_out=c.ss[:, tt:tt + 1]).then_inc(c.squared, 1)
            act.wait_ge(const_in, 48)
            gains_act(act, c, C_G1, T_FIRST)
            for g in [*range(0, SHARED, 2), *range(SHARED, GROUPS)]:
                act.wait_ge(grp, g + 1)
                if g == SHARED:
                    act.wait_ge(set0, 2)
                project_out(g, lambda o, i, s: act.activation(o, i, ACT.Copy, scale=s), grp_a)
            for h in range(0, HEADS, 2):
                act.wait_ge(rturn, h + 1)
                act.activation(a.qzb[:, h], c.bank[h % 4][:], ACT.Copy, scale=DH ** -0.5).then_inc(rout, 1)
            act.wait_ge(rturn, HEADS + 1)
            act.activation(a.kTb, c.bank[HEADS % 4][:], ACT.Copy).then_inc(rout, 1)

        @block.gpsimd
        def _(pool):
            pool.memset(c.half[:], -0.5).then_inc(set0, 1)
            pool.memset(a.qz[:], 0.0).then_inc(set0, 1)
            pool.wait_ge(set0, 2)
            norm_rsqrt(pool, c, N_FIRST)
            pool.wait_ge(c.turned, KT)
            pool.memset(HN[:], 0.0).then_inc(set0, 1)
            pool.wait_ge(hsum, 1)
            pool.tensor_scalar(hs[:, 1], hs[:, 0], 1.0 / DH, EPS, ALU.mult, ALU.add).then_inc(set0, 1)
            pool.wait_ge(set0, 4)
            pool.tensor_tensor(hs[:, 2], hs[:, 1], c.half[:, 0:40], ALU.pow).then_inc(hroot, 1)

        @block.vector
        def _(dve):
            dve.wait_ge(c.rooted, N_FIRST + 1)
            for tt in range(TT):
                dve.wait_ge(x_in[tt], 16)
                dve.tensor_scalar(HN[:, tt], c.X[:, tt], c.rn[:, tt:tt + 1], None, ALU.mult).then_inc(c.scaled, 1)
            dve.wait_ge(const_in, 48)
            gains_dve(dve, c, C_G1, T_FIRST)
            for g in range(1, SHARED, 2):
                dve.wait_ge(grp, g + 1)
                project_out(g, lambda o, i, s: dve.tensor_scalar(o, i, s, None, ALU.mult), grp_d)
            n = [0]

            def link(ins):
                n[0] += 1
                ins.then_inc(step, 1)
                dve.wait_ge(step, n[0])

            dve.wait_ge(grp_a, SHARED // 2)
            dve.wait_ge(grp_d, SHARED // 2)
            flat = lambda x: x[:].rearrange("p t w -> p (t w)")
            heads = lambda x: x[:].rearrange("p t (h w) -> p (t h) w", w=DH)
            link(dve.tensor_tensor(flat(S1), flat(QK), flat(QK), ALU.mult))
            dve.tensor_reduce(hs[:, 0], heads(S1), AX, ALU.add).then_inc(hsum, 1)
            dve.wait_ge(hroot, 1)
            link(dve.tensor_tensor(heads(S1), heads(QK), bc(hs[:, 2], DH), ALU.mult))
            link(dve.tensor_tensor(QK[:], S1[:], mid(c.rows[:, R_GQK:R_GQK + ATT_W + P], TT), ALU.mult))
            for tt in range(TT):
                cos = mid(c.tab[:, T_COS + tt * DH:T_COS + (tt + 1) * DH], HR)
                dve.tensor_tensor(S1[:, tt].rearrange("p (h w) -> p h w", w=DH), QK[:, tt].rearrange("p (h w) -> p h w", w=DH), cos, ALU.mult)
                halves = lambda x: x.rearrange("p (h s f w) -> p h s f w", s=2, f=2, w=DH // 4)
                sin = c.tab[:, T_SIN + tt * DH:T_SIN + (tt + 1) * DH].rearrange("p (s f w) -> p s f w", s=2, f=2)
                for f in range(2):
                    s_f = sin[:, :, f].unsqueeze(1).broadcast_to([P, HR, 2, DH // 4])
                    last = dve.tensor_tensor(halves(S2[:, tt])[:, :, :, f], halves(QK[:, tt])[:, :, :, 1 - f], s_f, ALU.mult)
            link(last)
            dve.wait_ge(set0, 3)
            for tt in range(TT):
                for n0 in range(KV_HEADS):
                    o = qpad[:, tt, 4 * n0:4 * n0 + 4, 64 * n0:64 * n0 + 64]
                    cut = slice(256 * n0, 256 * n0 + 256)
                    dve.tensor_tensor(o, S1[:, tt, cut].rearrange("p (h w) -> p h w", w=DH),
                                      S2[:, tt, cut].rearrange("p (h w) -> p h w", w=DH), ALU.add)
                last = dve.tensor_tensor(KR[:, tt], S1[:, tt, ATT_W:], S2[:, tt, ATT_W:], ALU.add)
            last.then_inc(roped, 1)
            for h in range(1, HEADS, 2):
                dve.wait_ge(rturn, h + 1)
                dve.tensor_scalar(a.qzb[:, h], c.bank[h % 4][:], DH ** -0.5, None, ALU.mult).then_inc(rout_d, 1)

        @block.tensor
        def _(pe):
            pe.wait_ge(const_in, 48)
            transposes_pe(pe, c, HN, T_FIRST)
            transposed_pe(pe, c, T_FIRST)
            for g in range(GROUPS):
                ps = c.bank[4 + g % 4]
                if g % 4 == 0:
                    c.wait_w(pe, g // 4)
                if g >= 4 + SHARED:
                    pe.wait_ge(grp_a, g - 3 - SHARED // 2)
                elif g >= 4:
                    pe.wait_ge(grp_d if g % 2 else grp_a, g // 2 - 1)
                if 8 <= g < 16:
                    w = c.w(g // 4, KT * 512, 512)
                    for k in range(KT):
                        mm = pe.matmul(ps[:], w[:, k, (g % 4) * P:(g % 4 + 1) * P], c.XT[:, k], start=k == 0, stop=k == KT - 1)
                else:
                    width = 256 if 4 <= g < 8 else 512
                    w, tt = c.w(g // 4, KT * width, width), g % 4
                    for k in range(KT):
                        mm = pe.matmul(ps[:, 0:width], c.XT[:, k, tt * P:(tt + 1) * P], w[:, k], start=k == 0, stop=k == KT - 1)
                mm.then_inc(grp, 1)
            pe.wait_ge(roped, 1)
            for h in range(HEADS + 1):
                if h >= 4:
                    pe.wait_ge(rout_d if h % 2 else rout, h // 2 - 1)
                for tt in range(TT):
                    src = qpad[:, tt, h] if h < HEADS else KR[:, tt]
                    mm = pe.transpose(c.bank[h % 4][:, tt * P:(tt + 1) * P], src, c.ident)
                mm.then_inc(rturn, 1)


def phase_attend(c, a):
    nc, t = c.nc, c.t
    UNITS = 2 * HEADS * TT
    PR = 4
    with ExitStack() as ctx:
        Pr = ctx.enter_context(nc.sbuf_tensor("Pr", [P, PR, SEQ], F32))
        PT = ctx.enter_context(nc.sbuf_tensor("PT", [P, PR, TT, P], F32))
        bias = ctx.enter_context(nc.sbuf_tensor("bias_sb", [P, 2, BIAS_ROWS * GRID_W], F32))
        mx = ctx.enter_context(nc.sbuf_tensor("mx", [P, UNITS], F32))
        nm = ctx.enter_context(nc.sbuf_tensor("nm", [P, UNITS], F32))
        rs = ctx.enter_context(nc.sbuf_tensor("rs", [P, UNITS], F32))
        ri = ctx.enter_context(nc.sbuf_tensor("ri", [P, UNITS], F32))
        scored, maxed, negated, expd, turned, pt_a, pt_d, weighed, inverted, y_out, b0, b1 = signals(
            nc, ctx, "scored maxed negated expd turned2 pt_a pt_d weighed inverted y_out bias_in0 bias_in1")
        bias_in = (b0, b1)
        block = ctx.enter_context(nc.Block())
        psS, psT, psY = c.bank[0:3], c.bank[3:6], c.bank[6:8]

        @block.sync
        def _(sp):
            for h in range(HEADS):
                if h >= 2:
                    sp.wait_ge(negated, TT * (h - 1))
                sp.dma_start(bias[:, h % 2], t["bias"][h]).then_inc(bias_in[h % 2], 16)

        def pt_copied(eng, u):
            eng.wait_ge(pt_d if u % 2 else pt_a, u // 2 + 1)

        @block.tensor
        def _(pe):
            for i in range(UNITS + 3):
                if i < UNITS:
                    h, q = divmod(i, TT)
                    if i >= 3:
                        pe.wait_ge(expd, i - 2)
                    if h < HEADS:
                        qT, kT = a.qz[:, h], a.kT[:, h // 2]
                    else:
                        qT, kT = a.qzb[:, h - HEADS], a.kTb[:]
                    pe.matmul(psS[i % 3][:], qT[:, q * P:(q + 1) * P], kT, start=True, stop=True).then_inc(scored, 1)
                u = i - 2
                if 0 <= u < UNITS:
                    pe.wait_ge(expd, u + 1)
                    if u >= 3:
                        pt_copied(pe, u - 3)
                    for kt in range(TT):
                        mm = pe.transpose(psT[u % 3][:, kt * P:(kt + 1) * P], Pr[:, u % PR, kt * P:(kt + 1) * P], c.ident)
                    mm.then_inc(turned, 1)
                u = i - 3
                if 0 <= u < UNITS:
                    h, q = divmod(u, TT)
                    pt_copied(pe, u)
                    if q == 0 and h >= 2:
                        pe.wait_ge(y_out, h - 1)
                    for kt in range(TT):
                        v = a.va[:, kt, h * DH:(h + 1) * DH] if h < HEADS else \
                            a.vb[:, kt, (h - HEADS) // 4 * DH:((h - HEADS) // 4 + 1) * DH]
                        mm = pe.matmul(psY[h % 2][:, q * DH:(q + 1) * DH], PT[:, u % PR, kt], v, start=kt == 0, stop=kt == TT - 1)
                    mm.then_inc(weighed, 1)

        @block.vector
        def _(dve):
            for i in range(UNITS + 4):
                u = i - 3
                if 0 <= u < UNITS and u % 2:
                    dve.wait_ge(turned, u + 1)
                    if u >= PR:
                        dve.wait_ge(weighed, u - PR + 1)
                    dve.tensor_copy(PT[:, u % PR].rearrange("p a b -> p (a b)"), psT[u % 3][:]).then_inc(pt_d, 1)
                if i < UNITS:
                    h, q = divmod(i, TT)
                    dve.wait_ge(scored, i + 1)
                    if h < HEADS:
                        if q == 0:
                            dve.wait_ge(bias_in[h % 2], 16 * (h // 2 + 1))
                        if i >= PR:
                            dve.wait_ge(turned, i - PR + 1)
                        r0 = (WIN_H - 1 - 2 * q) * GRID_W
                        dve.tensor_tensor_reduce(Pr[:, i % PR], psS[i % 3][:], bias[:, h % 2, r0:r0 + SEQ], 1.0, LOWEST,
                                                 ALU.add, ALU.max, mx[:, i:i + 1]).then_inc(maxed, 1)
                        dve.wait_ge(maxed, i + 1)
                        dve.tensor_scalar(nm[:, i:i + 1], mx[:, i:i + 1], -1.0, None, ALU.mult).then_inc(negated, 1)
                    else:
                        dve.tensor_reduce(nm[:, i:i + 1], psS[i % 3][:], AX, ALU.max, negate=True).then_inc(negated, 1)
                u = i - 4
                if u >= 0 and u % TT == TT - 1:
                    h = u // TT
                    dve.wait_ge(expd, TT * (h + 1))
                    dve.reciprocal(ri[:, TT * h:TT * (h + 1)], rs[:, TT * h:TT * (h + 1)]).then_inc(inverted, 1)
                    dve.wait_ge(inverted, h + 1)
                    dve.wait_ge(weighed, TT * (h + 1))
                    dve.tensor_tensor(a.y[:, :, h * DH:(h + 1) * DH], psY[h % 2][:, 0:TT * DH].rearrange("p (t w) -> p t w", w=DH),
                                      bc(ri[:, TT * h:TT * (h + 1)], DH), ALU.mult).then_inc(y_out, 1)

        @block.scalar
        def _(act):
            for i in range(UNITS + 3):
                u = i - 3
                if 0 <= u < UNITS and u % 2 == 0:
                    act.wait_ge(turned, u + 1)
                    if u >= PR:
                        act.wait_ge(weighed, u - PR + 1)
                    act.activation(PT[:, u % PR].rearrange("p a b -> p (a b)"), psT[u % 3][:], ACT.Copy).then_inc(pt_a, 1)
                if i < UNITS:
                    act.wait_ge(negated, i + 1)
                    if i >= PR and i >= HEADS * TT:
                        act.wait_ge(turned, i - PR + 1)
                    src = Pr[:, i % PR] if i < HEADS * TT else psS[i % 3][:]
                    act.activation(Pr[:, i % PR], src, ACT.Exp, bias=nm[:, i:i + 1], accum_out=rs[:, i:i + 1]).then_inc(expd, 1)


def phase_merge(c, a):
    nc = c.nc
    with ExitStack() as ctx:
        sb = lambda name, shape, dt=F32: ctx.enter_context(nc.sbuf_tensor(name, shape, dt))
        yT, mT = sb("yT", [P, KT, SEQ]), sb("mT", [P, KT, SEQ])
        sg = c.ur[:].rearrange("p r (j t) -> p r j t", j=2)
        Xh, Xl = sb("X1h", [P, KT, SEQ], F32R), sb("X1l", [P, KT, SEQ], F32R)
        PIECE = KT * P
        Wh = [sb(f"Ph{i}", [P, PIECE], F32R) for i in range(2)]
        Wl = [sb(f"Pl{i}", [P, PIECE], F32R) for i in range(2)]
        (turned, out_a, out_d, grp, gated, halfd, merged, xg, added) = signals(
            nc, ctx, "m_turned m_out_a m_out_d m_grp gated halved merged x_grp x_added")
        block = ctx.enter_context(nc.Block())
        GP = 2 * KT
        OP = 4
        OG = OP - 1 + TT

        yT_as_rows = yT[:].rearrange("p a b -> p (a b)").rearrange("p (t d) -> p t d", t=TT)
        junk = mT[:].rearrange("p a b -> p (a b)").rearrange("p (t d) -> p t d", t=TT)

        def piece(i):
            b, part = (B_MERGE + i // 2, i % 2) if i < GP else (B_OUT + (i - GP) // OP, (i - GP) % OP)
            return b, c.W[:, b % RING, part * PIECE:(part + 1) * PIECE]

        def hi(act, i):
            b, src = piece(i)
            c.wait_w(act, b)
            if 2 <= i < GP + 2:
                act.wait_ge(grp, 4 * ((i - 2) // 2) + i % 2 + 1)
            elif i >= GP + 2:
                nh, part = divmod(i - 2 - GP, OP)
                act.wait_ge(xg, nh * OG + (OG if part == OP - 1 else part + 1))
            act.activation(Wh[i % 2][:], src, ACT.Copy).then_inc(c.whi, 1)

        def lo(dve, i):
            dve.wait_ge(c.whi, W_MERGE + i + 1)
            dve.tensor_tensor(Wl[i % 2][:], piece(i)[1], Wh[i % 2][:].bitcast(F32), ALU.subtract).then_inc(c.wlo, 1)

        @block.sync
        def _(sp):
            for b in range(5, B_PQ):
                if b < B_OUT:
                    sp.wait_ge(grp, 4 * (b - B_MERGE + 1))
                else:
                    sp.wait_ge(c.wlo, W_MERGE + GP + OP * (b - B_OUT + 1))
                c.load_w(sp, b + RING)

        @block.tensor
        def _(pe):
            for kt in range(KT):
                if kt >= 4:
                    pe.wait_ge(out_d if kt % 2 else out_a, kt // 2 - 1)
                for tt in range(TT):
                    mm = pe.transpose(c.bank[kt % 4][:, tt * P:(tt + 1) * P], a.y[:, tt, kt * P:(kt + 1) * P], c.ident)
                mm.then_inc(turned, 1)
            pe.wait_ge(out_a, KT // 2)
            pe.wait_ge(out_d, KT // 2)
            pe.wait_ge(c.xlo, S_FIRST + KT)
            for m in range(KT):
                bk = c.bank[4 * (m % 2):4 * (m % 2) + 4]
                w = c.w(B_MERGE + m, 24 * P)
                if m >= 2:
                    pe.wait_ge(gated, 2 * (m - 1))
                    pe.wait_ge(halfd, 2 * (m - 1))
                for j in range(2):
                    pe.wait_ge(c.wlo, W_MERGE + 2 * m + j + 1)
                    for k in range(KT):
                        cut = slice(k * P, (k + 1) * P)
                        pe.matmul(bk[j][:], Wh[j][:, cut], Xh[:, k], start=k == 0, stop=False)
                        pe.matmul(bk[j][:], Wh[j][:, cut], Xl[:, k], start=False, stop=False)
                        mm = pe.matmul(bk[j][:], Wl[j][:, cut], Xh[:, k], start=False, stop=k == KT - 1)
                    mm.then_inc(grp, 1)
                c.wait_w(pe, B_MERGE + m)
                for j in range(2):
                    for k in range(4):
                        mm = pe.matmul(bk[2 + j][:], w[:, 2 * KT + 4 * j + k], yT[:, 4 * j + k], start=k == 0, stop=k == 3)
                    mm.then_inc(grp, 1)
            pe.wait_ge(c.xlo, S_MERGED + KT)
            for nh in range(2):
                for part in range(OP):
                    i = GP + nh * OP + part
                    pe.wait_ge(c.wlo, W_MERGE + i + 1)
                    for tt in range(TT):
                        tok, ps = slice(tt * P, (tt + 1) * P), c.bank[4 * nh + tt][:]
                        for k2 in range(KT // OP):
                            k, cut = part * (KT // OP) + k2, slice(k2 * 512, (k2 + 1) * 512)
                            pe.matmul(ps, Xh[:, k, tok], Wh[i % 2][:, cut], start=k == 0, stop=False)
                            pe.matmul(ps, Xh[:, k, tok], Wl[i % 2][:, cut], start=False, stop=False)
                            mm = pe.matmul(ps, Xl[:, k, tok], Wh[i % 2][:, cut], start=False, stop=k == KT - 1)
                        if part == OP - 1 or tt == TT - 1:
                            mm.then_inc(xg, 1)
            pe.wait_ge(added, 2 * TT)
            transposes_pe(pe, c, yT_as_rows, T_EXPERTS)

        @block.scalar
        def _(act):
            for kt in range(KT):
                act.activation(Xh[:, kt], c.XT[:, kt], ACT.Copy).then_inc(c.xhi, 1)
                if kt % 2 == 0:
                    act.wait_ge(turned, kt + 1)
                    act.activation(yT[:, kt], c.bank[kt % 4][:], ACT.Copy).then_inc(out_a, 1)
            hi(act, 0)
            hi(act, 1)
            for m in range(KT):
                for j in range(2):
                    act.wait_ge(grp, 4 * m + j + 1)
                    if m >= 2:
                        act.wait_ge(merged, m - 1)
                    act.activation(sg[:, m % 2, j], c.bank[4 * (m % 2) + j][:], ACT.Sigmoid).then_inc(gated, 1)
                    hi(act, 2 * m + 2 + j)
            for k in range(KT):
                act.wait_ge(merged, k + 1)
                act.activation(Xh[:, k], mT[:, k], ACT.Copy).then_inc(c.xhi, 1)
            for i in range(GP + 2, GP + 2 * OP):
                hi(act, i)
            act.wait_ge(c.xlo, S_MERGED + KT)
            norm_sums(act, c, c.X, junk, added, TT)
            gains_act(act, c, C_G2, T_EXPERTS)

        @block.gpsimd
        def _(pool):
            norm_rsqrt(pool, c, N_EXPERTS)

        @block.vector
        def _(dve):
            for kt in range(KT):
                dve.wait_ge(c.xhi, S_FIRST + kt + 1)
                dve.tensor_tensor(Xl[:, kt], c.XT[:, kt], Xh[:, kt].bitcast(F32), ALU.subtract).then_inc(c.xlo, 1)
                if kt % 2:
                    dve.wait_ge(turned, kt + 1)
                    dve.tensor_copy(yT[:, kt], c.bank[kt % 4][:]).then_inc(out_d, 1)

            def lo_merged(k):
                dve.wait_ge(c.xhi, S_MERGED + k + 1)
                dve.tensor_tensor(Xl[:, k], mT[:, k], Xh[:, k].bitcast(F32), ALU.subtract).then_inc(c.xlo, 1)

            lo(dve, 0)
            lo(dve, 1)
            for m in range(KT):
                lo(dve, 2 * m + 2)
                lo(dve, 2 * m + 3)
                if m == KT - 1:
                    for k in range(m):
                        lo_merged(k)
                for j in range(2):
                    dve.wait_ge(grp, 4 * m + 3 + j)
                    dve.wait_ge(gated, 2 * m + j + 1)
                    dve.tensor_tensor(sg[:, m % 2, j], c.bank[4 * (m % 2) + 2 + j][:], sg[:, m % 2, j], ALU.mult).then_inc(halfd, 1)
                dve.wait_ge(halfd, 2 * (m + 1))
                dve.tensor_tensor(mT[:, m], sg[:, m % 2, 0], sg[:, m % 2, 1], ALU.add).then_inc(merged, 1)
            lo_merged(KT - 1)
            for nh in range(2):
                for i in range(GP + 2, GP + OP + 2) if nh == 0 else range(GP + OP + 2, GP + 2 * OP):
                    lo(dve, i)
                for tt in range(TT):
                    dve.wait_ge(xg, nh * OG + OP + tt)
                    xs = c.X[:, tt, nh * 512:(nh + 1) * 512]
                    dve.tensor_tensor(xs, c.bank[4 * nh + tt][:], xs, ALU.add).then_inc(added, 1)
            dve.wait_ge(c.rooted, N_EXPERTS + 1)
            for tt in range(TT):
                dve.tensor_scalar(yT_as_rows[:, tt], c.X[:, tt], c.rn[:, tt:tt + 1], None, ALU.mult).then_inc(c.scaled, 1)
            gains_dve(dve, c, C_G2, T_EXPERTS)


class Early:

    def __init__(self, c, ctx):
        self.c = c
        i0, i1, self.done, self.gelud, k0, k1 = signals(c.nc, ctx, "ue_in0 ue_in1 ue_done ue_gelud ue_kept0 ue_kept1")
        self.u_in, self.kept = (i0, i1), (k0, k1)

    def load(self, sp, it, n):
        one = bass.ds(it * 2 + n, 1)
        sp.dma_start(self.c.ur[:, n % 2], self.c.t["u"][one].rearrange("g p k e -> (g p) (k e)")).then_inc(self.u_in[n % 2], 16)

    def keep(self, sp, it, n):
        sp.wait_ge(self.gelud, it * 2 + (n + 1))
        one = bass.ds(it * 2 + n, 1)
        sp.dma_start(self.c.t["early"][one].rearrange("g p t -> (g p) t"), self.c.ar[:, n % 2]).then_inc(self.kept[n % 2], 16)

    def next_load(self, sp, it, n):
        sp.wait_ge(self.done, it * 2 + (n + 1))
        self.load(sp, it, n + 2)

    def products(self, pe, it, n, bank, first, part=None):
        c, r = self.c, n % 2
        if part in (None, 0):
            pe.wait_ge(self.u_in[r], it * 16 + 16 * (n // 2 + 1))
            if not first:
                pe.wait_ge(self.gelud, it * 2 + (n - 1))
        ks = range(KT) if part is None else range(part * KT // 2, (part + 1) * KT // 2)
        for k in ks:
            mm = pe.matmul(c.bank[bank + r][:], c.ur[:, r, k * P:(k + 1) * P], c.XT[:, k], start=k == 0, stop=k == KT - 1)
        if part in (None, 1):
            mm.then_inc(self.done, 1)

    def gelu(self, act, it, n, bank, first):
        c, r = self.c, n % 2
        act.wait_ge(self.done, it * 2 + (n + 1))
        if not first:
            act.wait_ge(self.kept[r], it * 16 + 16 * (n // 2))
        act.activation(c.ar[:, r], c.bank[bank + r][:], ACT.Gelu).then_inc(self.gelud, 1)


def phase_query(c, qT):
    nc = c.nc
    NQ = 2 * PH
    with ExitStack() as ctx:
        sb = lambda name, shape, dt=F32: ctx.enter_context(nc.sbuf_tensor(name, shape, dt))
        Xh, Xl = sb("Xqh", [P, KT, SEQ], F32R), sb("Xql", [P, KT, SEQ], F32R)
        Wh = [sb(f"Qh{i}", [P, KT, P], F32R) for i in range(2)]
        Wl = [sb(f"Ql{i}", [P, KT, P], F32R) for i in range(2)]
        qg, qa, qd = signals(nc, ctx, "q_grp q_out_a q_out_d")
        block = ctx.enter_context(nc.Block())

        def piece(g):
            return c.w(B_PQ + g // 4, KT * 512, 512)[:, :, g % 4 * P:(g % 4 + 1) * P]

        @block.sync
        def _(sp):
            for b in range(B_PQ, B_KEYS + 1 - RING):
                sp.wait_ge(c.wlo, W_QUERY + 4 * (b - B_PQ + 1))
                c.load_w(sp, b + RING)

        @block.tensor
        def _(pe):
            for g in range(NQ):
                pe.wait_ge(c.wlo, W_QUERY + g + 1)
                if g >= 4:
                    pe.wait_ge(qd if g % 2 else qa, g // 2 - 1)
                h, l, ps = Wh[g % 2], Wl[g % 2], c.bank[g % 4][:]
                for k in range(KT):
                    if g == 0:
                        pe.wait_ge(c.xlo, S_QUERY + k + 1)
                    pe.matmul(ps, h[:, k], Xh[:, k], start=k == 0, stop=False)
                    pe.matmul(ps, h[:, k], Xl[:, k], start=False, stop=False)
                    mm = pe.matmul(ps, l[:, k], Xh[:, k], start=False, stop=k == KT - 1)
                mm.then_inc(qg, 1)

        @block.scalar
        def _(act):
            def hi(g):
                if g < NQ:
                    c.wait_w(act, B_PQ + g // 4)
                    if g >= 2:
                        act.wait_ge(qg, g - 1)
                    act.activation(Wh[g % 2][:], piece(g), ACT.Copy).then_inc(c.whi, 1)

            hi(0)
            for k in range(KT):
                act.activation(Xh[:, k], c.XT[:, k], ACT.Copy).then_inc(c.xhi, 1)
            hi(1)
            for g in range(NQ):
                hi(g + 2)
                if g % 2 == 0:
                    act.wait_ge(qg, g + 1)
                    act.activation(qT[:, g], c.bank[g % 4][:], ACT.Copy).then_inc(qa, 1)

        @block.vector
        def _(dve):
            def lo(g):
                if g < NQ:
                    dve.wait_ge(c.whi, W_QUERY + g + 1)
                    dve.tensor_tensor(Wl[g % 2][:], piece(g), Wh[g % 2][:].bitcast(F32), ALU.subtract).then_inc(c.wlo, 1)

            lo(0)
            for k in range(KT):
                dve.wait_ge(c.xhi, S_QUERY + k + 1)
                dve.tensor_tensor(Xl[:, k], c.XT[:, k], Xh[:, k].bitcast(F32), ALU.subtract).then_inc(c.xlo, 1)
            lo(1)
            for g in range(NQ):
                lo(g + 2)
                if g % 2:
                    dve.wait_ge(qg, g + 1)
                    dve.tensor_copy(qT[:, g], c.bank[g % 4][:]).then_inc(qd, 1)


def phase_choose(c, ijg, early, qT):
    nc = c.nc
    NQ = 2 * PH
    with ExitStack() as ctx:
        sb = lambda name, shape, dt=F32: ctx.enter_context(nc.sbuf_tensor(name, shape, dt))
        SC = sb("SC", [P, 2, NQ, PK])
        S2 = sb("SC2", [P, NQ * PK])
        cand = sb("cand", [P, PH, TOPK * TOPK])
        t16 = sb("t16", [P, NQ, TOPK])
        i16 = sb("i16", [P, NQ, TOPK], U32)
        i16f = sb("i16f", [P, NQ, TOPK])
        b16 = sb("b16", [P, PH, TOPK])
        pos = sb("pos", [P, PH, TOPK], U32)
        ab = sb("ab", [P, 2, SLOTS], U32)
        abf = sb("abf", [P, 2, SLOTS])
        eq = sb("eq", [P, SLOTS, TOPK])
        out3 = sb("out3", [P, 3, SLOTS])
        gs = sb("gs", [P, 2, PH])
        sg, so, step, gexp, gdiff, chosen, t3, t3o = signals(
            nc, ctx, "s_grp s_out c_step g_exp g_diff chosen t3_turned t3_out")
        block = ctx.enter_context(nc.Block())

        PER = E_CHOOSE // TT
        EB = 1

        @block.sync
        def _(sp):
            early.load(sp, 0, 0)
            early.load(sp, 0, 1)
            with sp.Fori(0, E_CHOOSE // 2) as it:
                for r in range(2):
                    early.next_load(sp, it, r)
                    early.keep(sp, it, r)

        @block.tensor
        def _(pe):
            c.wait_w(pe, B_KEYS)
            keys = c.w(B_KEYS, NQ * PK)

            def scores(tt):
                for j in range(4):
                    if tt >= 1:
                        pe.wait_ge(so, 4 * (tt - 1) + j + 1)
                    for i in range(4):
                        mm = pe.matmul(c.bank[4 + j][:, i * PK:(i + 1) * PK], qT[:, 4 * j + i, tt * P:(tt + 1) * P], keys[:, 4 * j + i],
                                       start=True, stop=True)
                    mm.then_inc(sg, 1)

            scores(0)
            for tt in range(TT):
                if tt + 1 < TT:
                    scores(tt + 1)
                if tt == 0:
                    for n in range(2):
                        early.products(pe, 0, n, EB, True)
                with pe.Fori(int(tt == 0), PER // 2) as it:
                    for r in range(2):
                        early.products(pe, it, tt * PER + r, EB, False)
                pe.wait_ge(chosen, tt + 1)
                if tt >= 1:
                    pe.wait_ge(t3o, tt)
                for i in range(3):
                    mm = pe.transpose(c.bank[0][:, i * P:(i + 1) * P], out3[:, i], c.ident)
                mm.then_inc(t3, 1)

        @block.scalar
        def _(act):
            def scores_out(tt):
                for j in range(4):
                    act.wait_ge(sg, 4 * tt + j + 1)
                    if tt >= 2:
                        act.wait_ge(chosen, tt - 1)
                    act.activation(SC[:, tt % 2, 4 * j:4 * j + 4].rearrange("p a b -> p (a b)"), c.bank[4 + j][:], ACT.Copy).then_inc(so, 1)

            scores_out(0)
            for tt in range(TT):
                if tt + 1 < TT:
                    scores_out(tt + 1)
                if tt == 0:
                    for n in range(2):
                        early.gelu(act, 0, n, EB, True)
                with act.Fori(int(tt == 0), PER // 2 - 1) as it:
                    for r in range(2):
                        early.gelu(act, it, tt * PER + r, EB, False)
                act.wait_ge(gdiff, tt + 1)
                act.activation(b16[:], b16[:], ACT.Exp).then_inc(gexp, 1)
                for r in range(2):
                    early.gelu(act, 0, (tt + 1) * PER - 2 + r, EB, False)
                act.wait_ge(t3, tt + 1)
                act.activation(ijg[:, :, tt * P:(tt + 1) * P], c.bank[0][:, 0:3 * P].rearrange("p (a b) -> p a b", b=P), ACT.Copy).then_inc(t3o, 1)

        @block.vector
        def _(dve):
            n = [0]

            def link(ins):
                n[0] += 1
                ins.then_inc(step, 1)
                dve.wait_ge(step, n[0])

            sc2 = S2[:].rearrange("p (a b) -> p a b", b=PK)
            cand2 = S2[:].rearrange("p (a b) -> p a b", b=TOPK * TOPK)
            for tt in range(TT):
                sc = SC[:, tt % 2]
                dve.wait_ge(so, 4 * (tt + 1))
                for j in range(NQ):
                    last = dve.max(t16[:, j, 0:8], sc[:, j])
                link(last)
                for j in range(NQ):
                    dve.max_index(i16[:, j, 0:8], t16[:, j, 0:8], sc[:, j])
                    last = dve.match_replace(sc2[:, j], t16[:, j, 0:8], sc[:, j], LOWEST)
                link(last)
                for j in range(NQ):
                    last = dve.max(t16[:, j, 8:16], sc2[:, j])
                link(last)
                for j in range(NQ):
                    last = dve.max_index(i16[:, j, 8:16], t16[:, j, 8:16], sc2[:, j])
                link(last)
                link(dve.tensor_copy(i16f[:], i16[:]))
                for h in range(PH):
                    last = dve.tensor_tensor(cand[:, h].rearrange("p (a b) -> p a b", b=TOPK), bc(t16[:, 2 * h], TOPK),
                                             mid(t16[:, 2 * h + 1], TOPK), ALU.add)
                link(last)
                if tt >= 1:
                    dve.wait_ge(t3, tt)
                for h in range(PH):
                    last = dve.max(b16[:, h, 0:8], cand[:, h])
                link(last)
                for h in range(PH):
                    dve.max_index(pos[:, h, 0:8], b16[:, h, 0:8], cand[:, h])
                    last = dve.match_replace(cand2[:, h], b16[:, h, 0:8], cand[:, h], LOWEST)
                link(last)
                for h in range(PH):
                    last = dve.max(b16[:, h, 8:16], cand2[:, h])
                link(last)
                for h in range(PH):
                    last = dve.max_index(pos[:, h, 8:16], b16[:, h, 8:16], cand2[:, h])
                link(last)
                link(dve.tensor_copy(gs[:, 0], b16[:, :, 0]))
                dve.tensor_tensor(b16[:], b16[:], bc(gs[:, 0], TOPK), ALU.subtract).then_inc(gdiff, 1)
                posf = pos[:].rearrange("p h k -> p (h k)")
                dve.tensor_scalar(ab[:, 0], posf, 4, None, ALU.logical_shift_right)
                link(dve.tensor_scalar(ab[:, 1], posf, TOPK - 1, None, ALU.bitwise_and))
                link(dve.tensor_copy(abf[:], ab[:]))
                for half in range(2):
                    link(dve.tensor_tensor(eq[:], bc(abf[:, half], TOPK), mid(c.iota[:, 0:TOPK], SLOTS), ALU.is_equal))
                    eqh = eq[:].rearrange("p (h k) a -> p h k a", h=PH)
                    key = i16f[:].rearrange("p (h f) a -> p h f a", f=2)[:, :, half].unsqueeze(2).broadcast_to([P, PH, TOPK, TOPK])
                    link(dve.tensor_tensor(eqh, eqh, key, ALU.mult))
                    link(dve.tensor_reduce(out3[:, half], eq[:], AX, ALU.add))
                dve.wait_ge(gexp, tt + 1)
                link(dve.tensor_reduce(gs[:, 0], b16[:], AX, ALU.add))
                link(dve.reciprocal(gs[:, 1], gs[:, 0]))
                dve.tensor_tensor(out3[:, 2].rearrange("p (h k) -> p h k", h=PH), b16[:], bc(gs[:, 1], TOPK), ALU.mult).then_inc(chosen, 1)
                dve.wait_ge(chosen, tt + 1)


def phase_gates(c, ijg, early):
    nc, t = c.nc, c.t
    Q = 4
    S = 2 * Q
    NSL = P // S
    B = 4
    ON_ACT = 6
    EB = 4
    CUTS = 16
    E0 = E_CHOOSE
    with ExitStack() as ctx:
        hot = [[ctx.enter_context(nc.sbuf_tensor(f"hot{half}{i}", [P, S, P], F32)) for i in range(2)] for half in range(2)]
        stage = [ctx.enter_context(nc.sbuf_tensor(f"stage{i}", [P, PK, P], F32)) for i in range(2)]
        hot_made, weighed_a, weighed_d, built, copied, st0, st1 = signals(
            nc, ctx, "hot_made weighed_a weighed_d built copied stored0 stored1")
        stored = (st0, st1)
        block = ctx.enter_context(nc.Block())
        dest = t["gates"].rearrange("i j t -> j i t")

        @block.vector
        def _(dve):
            for tt in range(TT):
                with dve.Fori(0, NSL // B) as it:
                    for s in range(B):
                        j, r = tt * NSL + s, s % 2
                        dve.wait_ge(built, it * (2 * B) + (2 * j + 2))
                        tok = it * (B * S) + j * S
                        for half in (1, 0):
                            dve.tensor_tensor(hot[half][r][:], mid(c.iota, S), bc(ijg[:, half, bass.ds(tok, S)], P),
                                              ALU.is_equal).then_inc(hot_made, 1)
                        dve.wait_ge(hot_made, it * (2 * B) + (2 * j + 2))
                        part = hot[0][r][:, ON_ACT:]
                        dve.tensor_tensor(part, part, bc(ijg[:, 2, bass.ds(tok + ON_ACT, S - ON_ACT)], P), ALU.mult).then_inc(weighed_d, 1)

        @block.tensor
        def _(pe):
            pe.sem_inc(built, 4)
            for tt in range(TT):
                with pe.Fori(0, NSL // B) as it:
                    for s in range(B):
                        j, r = tt * NSL + s, s % 2
                        pe.wait_ge(weighed_a, it * B + (j + 1))
                        pe.wait_ge(weighed_d, it * B + (j + 1))
                        for q in range(2):
                            pe.wait_ge(copied, it * (2 * B) + (2 * j + q + 1))
                            for k in range(Q):
                                mm = pe.matmul(c.bank[2 * r + q][:, k * P:(k + 1) * P], hot[1][r][:, Q * q + k], hot[0][r][:, Q * q + k],
                                               start=True, stop=True)
                            mm.then_inc(built, 1)
                        early.products(pe, it, E0 + j // B * 2 + s // 2, EB, False, part=s % 2)
            with pe.Fori(0, E_STORE // 2) as it:
                for r in range(2):
                    early.products(pe, it, E0 + E_GATES + r, EB, False)

        @block.scalar
        def _(act):
            act.sem_inc(copied, 4)

            def weigh(it, j):
                act.wait_ge(hot_made, it * (2 * B) + (2 * j + 2))
                for k in range(ON_ACT):
                    one = hot[0][j % 2][:, k]
                    last = act.activation(one, one, ACT.Copy, scale=ijg[:, 2, bass.ds(it * (B * S) + (j * S + k), 1)])
                last.then_inc(weighed_a, 1)

            def turn(it, tt, last):
                for s in range(B):
                    j = tt * NSL + s
                    if not (last and s == B - 1):
                        weigh(it, j + 1)
                    for q in range(2):
                        act.wait_ge(built, it * (2 * B) + (2 * j + q + 5))
                        o = stage[tt % 2][:, :, bass.ds(it * (B * S) + (2 * s + q) * Q, Q)]
                        act.activation(o, c.bank[2 * (s % 2) + q][:].rearrange("p (k i) -> p i k", k=Q), ACT.Copy).then_inc(copied, 1)
                    if s % 2:
                        early.gelu(act, it, E0 + j // B * 2 + s // 2, EB, False)

            weigh(0, 0)
            for tt in range(TT):
                if tt >= 2:
                    act.wait_ge(stored[tt % 2], 16 * CUTS)
                whole = NSL // B - (tt == TT - 1)
                with act.Fori(0, whole) as it:
                    turn(it, tt, False)
            turn(NSL // B - 1, TT - 1, True)
            with act.Fori(0, E_STORE // 2) as it:
                for r in range(2):
                    early.gelu(act, it, E0 + E_GATES + r, EB, False)

        @block.sync
        def _(sp):
            with sp.Fori(E0 // 2, EARLY // 2 - 1) as it:
                for r in range(2):
                    early.next_load(sp, it, r)
                    early.keep(sp, it, r)
            for r in range(2):
                early.keep(sp, EARLY // 2 - 1, r)
            for s in early.kept:
                sp.wait_ge(s, 16 * EARLY // 2)

        @block.gpsimd
        def _(pool):
            for tt in range(TT):
                pool.wait_ge(copied, 2 * NSL * (tt + 1) + 4)
                for j in range(CUTS):
                    if tt < TT - 1:
                        pool.wait_ge(copied, 2 * NSL * (tt + 1) + 4 + j * 2 * NSL // CUTS)
                    else:
                        pool.wait_ge(early.done, E0 + E_GATES + j * (E_STORE - 2) // CUTS)
                    i = slice(j * PK // CUTS, (j + 1) * PK // CUTS)
                    pool.dma_start(dest[:, i, tt * P:(tt + 1) * P], stage[tt % 2][:, i]).then_inc(stored[tt % 2], 16)
            for s in stored:
                pool.wait_ge(s, 16 * CUTS * TT // 2)


def phase_experts(c):
    nc, t = c.nc, c.t
    with ExitStack() as ctx:
        sb = lambda name, shape, dt=F32: ctx.enter_context(nc.sbuf_tensor(name, shape, dt))
        Xh, Xl = sb("Xh", [P, KT, SEQ], F32R), sb("Xl", [P, KT, SEQ], F32R)
        Ur = [c.ur[:, i].rearrange("p (k e) -> p k e", e=P) for i in range(2)]
        Uh = [sb(f"Uh{i}", [P, KT, P], F32R) for i in range(2)]
        Ul = [sb(f"Ul{i}", [P, KT, P], F32R) for i in range(2)]
        Vr = [sb(f"Vr{i}", [P, D]) for i in range(2)]
        Vh = [sb(f"Vh{i}", [P, EG, D], F32R) for i in range(2)]
        Vl = [sb(f"Vl{i}", [P, EG, D], F32R) for i in range(2)]
        Gr = [sb(f"Gr{i}", [P, SEQ]) for i in range(2)]
        A = [c.ar[:, i] for i in range(2)]
        Hh = [sb(f"Hh{i}", [P, EG, SEQ], F32R) for i in range(2)]
        Hl = [sb(f"Hl{i}", [P, EG, SEQ], F32R) for i in range(2)]
        (u0, u1, a0, a1, v0, v1, g0, g1, u_hi, u_lo, v_hi, v_lo, acted, gelud, gated, h_hi, h_lo, summed, added) = signals(
            nc, ctx, "u_in0 u_in1 a_in0 a_in1 v_in0 v_in1 g_in0 g_in1 u_hi u_lo v_hi v_lo acted gelud e_gated h_hi h_lo summed added2")
        u_in, a_in, v_in, g_in = (u0, u1), (a0, a1), (v0, v1), (g0, g1)
        block = ctx.enter_context(nc.Block())
        VG = 2 * TT
        A0 = 2
        S0 = 16
        L0 = 2
        G0 = 2
        B0 = 8

        LATE, TURNS = EARLY // (2 * EG), NG // 2

        def load_u(sp, it, m):
            one = bass.ds(it * 8 + (EARLY + m), 1)
            sp.dma_start(Ur[m % 2], t["u"][one].rearrange("g p k e -> (g p) k e")).then_inc(u_in[m % 2], 16)

        def load_gv(sp, it, n):
            one, r = bass.ds(it * 8 + n, 1), n % 2
            sp.wait_ge(gated, it * 8 + (n - 1 + G0))
            sp.dma_start(Gr[r][:], t["gates"][one].rearrange("i j t -> (i j) t")).then_inc(g_in[r], 16)
            sp.wait_ge(v_lo, it * 8 + (n - 1 + L0))
            sp.dma_start(Vr[r][:], t["v"][one].rearrange("g e d -> (g e) d")).then_inc(v_in[r], 16)

        @block.sync
        def _(sp):
            load_u(sp, 0, 0)
            load_u(sp, 0, 1)

            def kept(it, n):
                sp.wait_ge(h_lo, it * 8 + (n - 1 + G0))
                sp.dma_start(A[n % 2], t["early"][bass.ds(it * 8 + n, 1)].rearrange("g p t -> (g p) t")).then_inc(a_in[n % 2], 16)
                load_gv(sp, it, n)

            def next_u(it, m):
                sp.wait_ge(u_lo, (it - LATE) * 8 + (m - 1 + L0))
                load_u(sp, it - LATE, m)

            for n in range(8):
                kept(0, n)
                if n < 4:
                    next_u(LATE, n + 2)
            with sp.Fori(1, LATE) as it:
                for n in range(8):
                    kept(it, n)
            for n in range(4):
                load_gv(sp, LATE, n)
            with sp.Fori(LATE, TURNS - 1) as it:
                for n in range(4, 12):
                    next_u(it, n + 2)
                    load_gv(sp, it, n)
            for n in range(4, 8):
                if n < 6:
                    next_u(TURNS - 1, n + 2)
                load_gv(sp, TURNS - 1, n)

        def up(pe, turn, s):
            it = turn - LATE
            for e in range(EG):
                n, r = 4 * s + e, e % 2
                pe.wait_ge(u_lo, it * 8 + (n + 1 + L0))
                pe.wait_ge(gelud, it * 8 + (n + 1 - 4 + B0))
                for k in range(KT):
                    pe.matmul(c.bank[e][:], Uh[r][:, k], Xh[:, k], start=k == 0, stop=False)
                    pe.matmul(c.bank[e][:], Uh[r][:, k], Xl[:, k], start=False, stop=False)
                    mm = pe.matmul(c.bank[e][:], Ul[r][:, k], Xh[:, k], start=False, stop=k == KT - 1)
                mm.then_inc(acted, 1)

        def down(pe, it, s):
            pe.wait_ge(h_lo, it * 8 + (4 * s + 4 + G0))
            pe.wait_ge(v_lo, it * 8 + (4 * s + 4 + L0))
            for p in range(VG):
                tt, nh = divmod(p, 2)
                tok, cut, ps = slice(tt * P, (tt + 1) * P), slice(nh * 512, (nh + 1) * 512), c.bank[4 + p % 4]
                pe.wait_ge(added, it * 16 + (8 * s + p + 1 - 4 + B0))
                for e in range(EG):
                    pe.matmul(ps[:], Hh[s][:, e, tok], Vh[s][:, e, cut], start=e == 0, stop=False)
                    pe.matmul(ps[:], Hh[s][:, e, tok], Vl[s][:, e, cut], start=False, stop=False)
                    mm = pe.matmul(ps[:], Hl[s][:, e, tok], Vh[s][:, e, cut], start=False, stop=e == EG - 1)
                mm.then_inc(summed, 1)

        @block.tensor
        def _(pe):
            pe.sem_inc(acted, A0)
            pe.sem_inc(summed, S0)
            pe.wait_ge(c.xlo, S_EXPERTS + KT)
            up(pe, LATE, 0)
            with pe.Fori(0, LATE) as it:
                down(pe, it, 0)
                down(pe, it, 1)
            with pe.Fori(LATE, TURNS - 1) as it:
                up(pe, it, 1)
                down(pe, it, 0)
                up(pe, it + 1, 0)
                down(pe, it, 1)
            up(pe, TURNS - 1, 1)
            down(pe, TURNS - 1, 0)
            down(pe, TURNS - 1, 1)

        def hi_u(act, it, n):
            act.wait_ge(u_in[n % 2], it * 64 + 16 * (n // 2 + 1))
            act.wait_ge(acted, it * 8 + (n - 1 + A0))
            act.activation(Uh[n % 2][:], Ur[n % 2], ACT.Copy).then_inc(u_hi, 1)

        def tile_act(act, it, s, e, late, ahead=True):
            n, r = 4 * s + e, e % 2
            if late:
                act.wait_ge(acted, (it - LATE) * 8 + (n + 1 + A0))
                act.wait_ge(h_lo, it * 8 + (n - 1 + G0))
                act.activation(A[r], c.bank[e][:], ACT.Gelu).then_inc(gelud, 1)
                if ahead:
                    hi_u(act, it - LATE, n + 2)
            act.wait_ge(v_in[r], it * 64 + 16 * (n // 2 + 1))
            act.wait_ge(summed, it * 16 + (8 * s - 8 + S0))
            act.activation(Vh[s][:, e], Vr[r][:], ACT.Copy).then_inc(v_hi, 1)
            act.wait_ge(gated, it * 8 + (n + 1 + G0))
            act.activation(Hh[s][:, e], A[r], ACT.Copy).then_inc(h_hi, 1)

        def lo_u(dve, it, n):
            dve.wait_ge(u_hi, it * 8 + n + 1)
            dve.tensor_tensor(Ul[n % 2][:], Ur[n % 2], Uh[n % 2][:].bitcast(F32), ALU.subtract).then_inc(u_lo, 1)

        def tile_dve(dve, it, s, e, late, ahead=True):
            n, r = 4 * s + e, e % 2
            dve.wait_ge(g_in[r], it * 64 + 16 * (n // 2 + 1))
            if late:
                dve.wait_ge(gelud, (it - LATE) * 8 + (n + 1 + B0))
            else:
                dve.wait_ge(a_in[r], it * 64 + 16 * (n // 2 + 1))
            dve.tensor_tensor(A[r], A[r], Gr[r][:], ALU.mult).then_inc(gated, 1)
            if late and ahead:
                lo_u(dve, it - LATE, n + 2)
            dve.wait_ge(v_hi, it * 8 + (n + 1))
            dve.tensor_tensor(Vl[s][:, e], Vr[r][:], Vh[s][:, e].bitcast(F32), ALU.subtract).then_inc(v_lo, 1)
            dve.wait_ge(h_hi, it * 8 + (n + 1))
            dve.tensor_tensor(Hl[s][:, e], A[r], Hh[s][:, e].bitcast(F32), ALU.subtract).then_inc(h_lo, 1)

        @block.scalar
        def _(act):
            act.sem_inc(gelud, B0)
            for k in range(KT):
                act.activation(Xh[:, k], c.XT[:, k], ACT.Copy).then_inc(c.xhi, 1)
            hi_u(act, 0, 0)
            hi_u(act, 0, 1)
            for e in range(EG):
                tile_act(act, 0, 0, e, False)
                hi_u(act, 0, e + 2)
            with act.Fori(0, LATE - 1) as it:
                for e in range(EG):
                    tile_act(act, it, 1, e, False)
                for e in range(EG):
                    tile_act(act, it + 1, 0, e, False)
            for e in range(EG):
                tile_act(act, LATE - 1, 1, e, False)
            for e in range(EG):
                tile_act(act, LATE, 0, e, True, False)
            with act.Fori(LATE, TURNS - 1) as it:
                for e in range(EG):
                    tile_act(act, it, 1, e, True)
                for e in range(EG):
                    tile_act(act, it + 1, 0, e, True)
            for e in range(EG):
                tile_act(act, TURNS - 1, 1, e, True, e < 2)

        def add(dve, it, s, pieces=range(VG)):
            for p in pieces:
                tt, nh = divmod(p, 2)
                dve.wait_ge(summed, it * 16 + (8 * s + p + 1 + S0))
                dve.wait_ge(added, it * 16 + (8 * s + p + 1 - 8 + B0))
                xs = c.X[:, tt, nh * 512:(nh + 1) * 512]
                dve.tensor_tensor(xs, c.bank[4 + p % 4][:], xs, ALU.add).then_inc(added, 1)

        @block.vector
        def _(dve):
            dve.sem_inc(u_lo, L0)
            dve.sem_inc(v_lo, L0)
            dve.sem_inc(gated, G0)
            dve.sem_inc(h_lo, G0)
            dve.sem_inc(added, B0)
            for k in range(KT):
                dve.wait_ge(c.xhi, S_EXPERTS + k + 1)
                dve.tensor_tensor(Xl[:, k], c.XT[:, k], Xh[:, k].bitcast(F32), ALU.subtract).then_inc(c.xlo, 1)
            lo_u(dve, 0, 0)
            lo_u(dve, 0, 1)
            for e in range(EG):
                tile_dve(dve, 0, 0, e, False)
                lo_u(dve, 0, e + 2)
            with dve.Fori(0, LATE - 1) as it:
                for e in range(EG):
                    tile_dve(dve, it, 1, e, False)
                    add(dve, it, 0, (2 * e, 2 * e + 1))
                for e in range(EG):
                    tile_dve(dve, it + 1, 0, e, False)
                    add(dve, it, 1, (2 * e, 2 * e + 1))
            for e in range(EG):
                tile_dve(dve, LATE - 1, 1, e, False)
                add(dve, LATE - 1, 0, (2 * e, 2 * e + 1))
            for e in range(EG):
                tile_dve(dve, LATE, 0, e, True, False)
                add(dve, LATE - 1, 1, (2 * e, 2 * e + 1))
            with dve.Fori(LATE, TURNS - 1) as it:
                for e in range(EG):
                    tile_dve(dve, it, 1, e, True)
                add(dve, it, 0)
                for e in range(EG):
                    tile_dve(dve, it + 1, 0, e, True)
                add(dve, it, 1)
            for e in range(EG):
                tile_dve(dve, TURNS - 1, 1, e, True, e < 2)
            add(dve, TURNS - 1, 0)
            add(dve, TURNS - 1, 1)


class Raw:

    def __init__(self, c, ctx):
        own = ctx.enter_context(c.nc.sbuf_tensor("w_raw", [P, 2, WIN], F32))
        xt = c.XT[:].rearrange("p a b -> p (a b)")
        self.c = c
        self.slot = [own[:, 0], own[:, 1], xt[:, 0:WIN], xt[:, WIN:2 * WIN]]
        self.loaded = signals(c.nc, ctx, "raw_in0 raw_in1 raw_in2 raw_in3")

    def load(self, sp, b):
        sp.dma_start(self.slot[b % RAW], self.c.t["w_mixer"][b]).then_inc(self.loaded[b % RAW], 16)


def phase_between(c, raw):
    nc, t = c.nc, c.t
    with ExitStack() as ctx:
        HN = ctx.enter_context(nc.sbuf_tensor("HN2", [P, TT, D], F32))
        nf = ctx.enter_context(nc.sbuf_tensor("nf", [P, D], F32))
        nf_in, xnorm, xready = signals(
            nc, ctx, "nf_in b_xnorm b_xready")
        block = ctx.enter_context(nc.Block())

        @block.sync
        def _(sp):
            sp.dma_start(nf[:], t["norm_f"]).then_inc(nf_in, 16)
            for b in range(2):
                raw.load(sp, b)

        @block.scalar
        def _(act):
            norm_sums(act, c, c.X, HN)
            act.wait_ge(c.squared, (N_FINAL + 1) * TT)
            norm_sums(act, c, c.X, HN, xready)
            gains_act(act, c, C_GPRE, T_PRE)

        @block.gpsimd
        def _(pool):
            norm_rsqrt(pool, c, N_FINAL)
            pool.wait_ge(xnorm, TT)
            norm_rsqrt(pool, c, N_PRE)

        @block.vector
        def _(dve):
            dve.wait_ge(c.rooted, N_FINAL + 1)
            for tt in range(TT):
                dve.tensor_scalar(c.X[:, tt], c.X[:, tt], c.rn[:, tt:tt + 1], None, ALU.mult).then_inc(xnorm, 1)
            dve.wait_ge(nf_in, 16)
            for tt in range(TT):
                dve.wait_ge(xnorm, tt + 1)
                dve.tensor_tensor(c.X[:, tt], c.X[:, tt], nf[:], ALU.mult).then_inc(xready, 1)
            dve.wait_ge(c.rooted, N_PRE + 1)
            dve.wait_ge(xready, TT)
            for tt in range(TT):
                dve.tensor_scalar(HN[:, tt], c.X[:, tt], c.rn[:, tt:tt + 1], None, ALU.mult).then_inc(c.scaled, 1)
            gains_dve(dve, c, C_GPRE, T_PRE)

        @block.tensor
        def _(pe):
            transposes_pe(pe, c, HN, T_PRE)


class Mixer:
    def __init__(self, nc, ctx):
        sb = lambda name, shape: ctx.enter_context(nc.sbuf_tensor(name, shape, F32))
        self.yscT = sb("yscT", [P, KT, SEQ])
        self.xs = sb("xs", [P, TT, D])
        self.zs = sb("zs", [P, TT, D])
        self.xbcT = sb("xbcT", [P, XBC_TILES, SEQ])
        self.dt = sb("dt", [P, TT, SH])
        self.adt = sb("adt", [P, TT, SH])


def phase_mixer_in(c, m_, raw):
    nc = c.nc
    with ExitStack() as ctx:
        sb = lambda name, shape, dt=F32: ctx.enter_context(nc.sbuf_tensor(name, shape, dt))
        Xh, Xl = sb("X2h", [P, KT, SEQ], F32R), sb("X2l", [P, KT, SEQ], F32R)
        Wh = [sb(f"Wh{i}", [P, WIN], F32R) for i in range(2)]
        Wl = [sb(f"Wl{i}", [P, WIN], F32R) for i in range(2)]
        pad = sb("pad", [P, 2, CONV_W - 1 + SEQ])
        pad2 = sb("pad2", [P, 2, SC_W - 1 + SEQ])
        cv = c.ur[:, 0].rearrange("p (r t) -> p r t", r=2)
        cs = c.ur[:, 1].rearrange("p (r t) -> p r t", r=2)
        sp_ = cv[:, 0, 0:6 * TT * SH].rearrange("p (a t h) -> p a t h", a=6, t=TT)
        aneg = cv[:, 1, 0:SH]
        zz = c.ar
        zero, grp, padded, convd, silud, dto, c_out, z_out, step, vdone, aexp, sexp, sln, sstep = signals(
            nc, ctx, "n_zero n_grp n_padded n_convd n_silud n_dt_out n_c_out n_z_out n_step n_done n_aexp n_sexp n_sln n_sstep")
        block = ctx.enter_context(nc.Block())
        NX, NZ = XBC_TILES, D // ZC * TT
        G_DT, G_Z, G_SC = NX, NX + 1, NX + 1 + NZ

        def done(b):
            if b < I_DT:
                return 2 * (b + 1)
            if b < I_SC:
                return G_Z + TT * (b - I_DT)
            return G_SC + 2 * (b - I_SC + 1)

        @block.sync
        def _(sp):
            for b in range(2, NI):
                if b < RAW:
                    sp.wait_ge(c.xlo, S_PRE + KT)
                else:
                    sp.wait_ge(c.wlo, W_PRE + b - RAW + 1)
                raw.load(sp, b)

        @block.gpsimd
        def _(pool):
            pool.memset(pad[:], 0.0).then_inc(zero, 1)
            pool.memset(pad2[:], 0.0).then_inc(zero, 1)

        @block.tensor
        def _(pe):
            def group(ps, left, right, first=False):
                for k in range(KT):
                    if first:
                        pe.wait_ge(c.xlo, S_PRE + k + 1)
                    (lh, ll), (rh, rl) = left(k), right(k)
                    pe.matmul(ps, lh, rh, start=k == 0, stop=False)
                    pe.matmul(ps, lh, rl, start=False, stop=False)
                    mm = pe.matmul(ps, ll, rh, start=False, stop=k == KT - 1)
                return mm

            x_all = lambda k: (Xh[:, k], Xl[:, k])
            x_tok = lambda tt: lambda k: (Xh[:, k, tt * P:(tt + 1) * P], Xl[:, k, tt * P:(tt + 1) * P])

            def w(b, stride, at, n):
                return lambda k: tuple(x[b % 2][:, k * stride + at:k * stride + at + n] for x in (Wh, Wl))

            for n in range(NX):
                pe.wait_ge(c.wlo, W_PRE + n // 2 + 1)
                if n >= 4:
                    pe.wait_ge(padded, n - 3)
                group(c.bank[n % 4][:], w(n // 2, 2 * P, n % 2 * P, P), x_all, n == 0).then_inc(grp, 1)
            pe.wait_ge(c.wlo, W_PRE + I_DT + 1)
            for tt in range(TT):
                mm = group(c.bank[7][:, tt * SH:(tt + 1) * SH], x_tok(tt), w(I_DT, SH, 0, SH))
            mm.then_inc(grp, 1)
            for n in range(NZ):
                b, tt = I_Z + n // TT, n % TT
                pe.wait_ge(c.wlo, W_PRE + b + 1)
                if n >= 3:
                    pe.wait_ge(z_out, n - 2)
                group(c.bank[4 + n % 3][:, 0:ZC], x_tok(tt), w(b, ZC, 0, ZC)).then_inc(grp, 1)
            pe.wait_ge(padded, NX)
            for m in range(KT):
                if m == 1:
                    pe.wait_ge(z_out, NZ)
                    pe.wait_ge(dto, 1)
                if m >= 2:
                    pe.wait_ge(vdone, m - 1)
                    pe.wait_ge(z_out, NZ + m - 1)
                for j in range(4):
                    b = I_SC + 2 * m + j // 2
                    pe.wait_ge(c.wlo, W_PRE + b + 1)
                    group(c.bank[4 * (m % 2) + j][:], w(b, P, j % 2 * KT * P, P), x_all).then_inc(grp, 1)

        @block.scalar
        def _(act):
            def hi(b):
                if b < NI:
                    act.wait_ge(raw.loaded[b % RAW], 16 * (b // RAW + 1))
                    if b >= 2:
                        act.wait_ge(grp, done(b - 2))
                    act.activation(Wh[b % 2][:], raw.slot[b % RAW], ACT.Copy).then_inc(c.whi, 1)

            def silu(n):
                act.wait_ge(convd, n + 1)
                act.activation(m_.xbcT[:, n], cv[:, n % 2], ACT.Silu, bias=c.cols[:, C_CB + n:C_CB + n + 1]).then_inc(silud, 1)

            hi(0)
            for k in range(KT):
                act.activation(Xh[:, k], c.XT[:, k], ACT.Copy).then_inc(c.xhi, 1)
            act.wait_ge(zero, 2)
            for n in range(NX):
                if n % 2 == 0:
                    hi(n // 2 + 1)
                act.wait_ge(grp, n + 1)
                if n >= 2:
                    act.wait_ge(convd, n - 1)
                act.activation(pad[:, n % 2, CONV_W - 1:], c.bank[n % 4][:], ACT.Copy).then_inc(padded, 1)
                if n >= 1:
                    silu(n - 1)
            silu(NX - 1)
            hi(I_Z)
            act.wait_ge(sstep, 1)
            act.activation(aneg, c.rows[:, R_ALOG:R_ALOG + SH], ACT.Exp).then_inc(aexp, 1)
            act.activation(sp_[:, 1], sp_[:, 0], ACT.Exp).then_inc(sexp, 1)
            act.wait_ge(sstep, 2)
            act.activation(sp_[:, 3], sp_[:, 2], ACT.Ln).then_inc(sln, 1)
            for n in range(NZ):
                b, tt = I_Z + n // TT, n % TT
                if tt == 0:
                    hi(b + 1)
                act.wait_ge(grp, G_Z + n + 1)
                act.activation(m_.zs[:, tt, (n // TT) * ZC:(n // TT + 1) * ZC], c.bank[4 + n % 3][:, 0:ZC], ACT.Silu).then_inc(z_out, 1)
            for m in range(KT):
                bk = c.bank[4 * (m % 2):4 * (m % 2) + 4]
                hi(I_SC + 2 * m + 1)
                act.wait_ge(grp, G_SC + 4 * m + 1)
                if m >= 2:
                    act.wait_ge(vdone, m - 1)
                act.activation(cs[:, m % 2], bk[0][:], ACT.Copy).then_inc(c_out, 1)
                hi(I_SC + 2 * m + 2)
                act.wait_ge(grp, G_SC + 4 * m + 4)
                act.activation(zz[:, m % 2], bk[3][:], ACT.Silu).then_inc(z_out, 1)

        @block.vector
        def _(dve):
            n_ = [0]

            def link(ins):
                n_[0] += 1
                ins.then_inc(step, 1)
                dve.wait_ge(step, n_[0])

            def lo(b):
                if b < NI:
                    dve.wait_ge(c.whi, W_PRE + b + 1)
                    dve.tensor_tensor(Wl[b % 2][:], raw.slot[b % RAW], Wh[b % 2][:].bitcast(F32), ALU.subtract).then_inc(c.wlo, 1)

            lo(0)
            for k in range(KT):
                dve.wait_ge(c.xhi, S_PRE + k + 1)
                dve.tensor_tensor(Xl[:, k], c.XT[:, k], Xh[:, k].bitcast(F32), ALU.subtract).then_inc(c.xlo, 1)
            for n in range(NX):
                if n % 2 == 0:
                    lo(n // 2 + 1)
                dve.wait_ge(padded, n + 1)
                if n >= 2:
                    dve.wait_ge(silud, n - 1)
                tap = lambda k: c.cols[:, C_CW + n * CONV_W + k:C_CW + n * CONV_W + k + 1]
                o = cv[:, n % 2]
                link(dve.tensor_scalar(o, pad[:, n % 2, 0:SEQ], tap(0), None, ALU.mult))
                for k in range(1, CONV_W):
                    ins = dve.scalar_tensor_tensor(out=o, in0=pad[:, n % 2, k:k + SEQ], scalar=tap(k), in1=o, op0=ALU.mult, op1=ALU.add)
                    if k < CONV_W - 1:
                        link(ins)
                ins.then_inc(convd, 1)
            lo(I_Z)
            dve.wait_ge(grp, G_DT + 1)
            dve.tensor_tensor(m_.dt[:], c.bank[7][:, 0:TT * SH].rearrange("p (t h) -> p t h", h=SH), mid(c.rows[:, R_DTB:R_DTB + SH], TT),
                              ALU.add).then_inc(dto, 1)
            dve.wait_ge(dto, 1)
            dve.wait_ge(silud, NX)
            ns = [0]

            def slink(ins):
                ns[0] += 1
                ins.then_inc(sstep, 1)
                dve.wait_ge(sstep, ns[0])

            slink(dve.scalar_tensor_tensor(out=sp_[:, 0], in0=m_.dt[:], scalar=-1.0, in1=m_.dt[:], op0=ALU.mult, op1=ALU.min))
            dve.wait_ge(sexp, 1)
            slink(dve.tensor_scalar(sp_[:, 2], sp_[:, 1], 1.0, None, ALU.add))
            slink(dve.tensor_scalar(sp_[:, 4], sp_[:, 2], -1.0, None, ALU.add))
            slink(dve.tensor_scalar(sp_[:, 5], sp_[:, 4], 0.0, None, ALU.is_equal))
            slink(dve.tensor_tensor(sp_[:, 4], sp_[:, 4], sp_[:, 5], ALU.add))
            slink(dve.reciprocal(sp_[:, 4], sp_[:, 4]))
            dve.wait_ge(sln, 1)
            slink(dve.tensor_tensor(sp_[:, 3], sp_[:, 3], sp_[:, 5], ALU.add))
            slink(dve.tensor_tensor(sp_[:, 3], sp_[:, 3], sp_[:, 1], ALU.mult))
            slink(dve.tensor_tensor(sp_[:, 3], sp_[:, 3], sp_[:, 4], ALU.mult))
            slink(dve.scalar_tensor_tensor(out=m_.dt[:], in0=m_.dt[:], scalar=0.0, in1=sp_[:, 3], op0=ALU.max, op1=ALU.add))
            dve.wait_ge(aexp, 1)
            slink(dve.tensor_scalar(sp_[:, 0], m_.dt[:], -1.0, None, ALU.mult))
            slink(dve.tensor_tensor(m_.adt[:], sp_[:, 0], mid(aneg, TT), ALU.mult))
            for b in range(I_Z + 1, I_SC + 1):
                lo(b)
            for m in range(KT):
                bk = c.bank[4 * (m % 2):4 * (m % 2) + 4]
                lo(I_SC + 2 * m + 1)
                dve.wait_ge(grp, G_SC + 4 * m + 2)
                dve.wait_ge(c_out, m + 1)
                link(dve.tensor_tensor(pad2[:, m % 2, SC_W - 1:], bk[1][:], cs[:, m % 2], ALU.mult))
                tap = lambda k: c.cols[:, C_SW + m * SC_W + k:C_SW + m * SC_W + k + 1]
                o = m_.yscT[:, m]
                link(dve.tensor_scalar(o, pad2[:, m % 2, 0:SEQ], tap(0), None, ALU.mult))
                for k in range(1, SC_W):
                    link(dve.scalar_tensor_tensor(out=o, in0=pad2[:, m % 2, k:k + SEQ], scalar=tap(k), in1=o, op0=ALU.mult, op1=ALU.add))
                lo(I_SC + 2 * m + 2)
                dve.wait_ge(grp, G_SC + 4 * m + 3)
                link(dve.tensor_tensor(o, bk[2][:], o, ALU.mult))
                dve.wait_ge(z_out, NZ + m + 1)
                dve.tensor_tensor(o, o, zz[:, m % 2], ALU.mult).then_inc(vdone, 1)


def phase_scan(c, m_):
    nc, t = c.nc, c.t
    GW = HG * SP_
    UN = TT * SG
    with ExitStack() as ctx:
        sb = lambda name, shape: ctx.enter_context(nc.sbuf_tensor(name, shape, F32))
        bt = sb("bt", [P, TT, P])
        ones = sb("ones", [P, P])
        acs = sb("acs", [P, 2, TT, SH])
        eacs = sb("eacs", [P, TT, SH])
        dst = sb("dst", [P, TT, SH])
        etot = sb("etot", [P, TT, SH])
        dec = sb("dec", [P, TT, HG])
        xd = c.ur
        xdd = sb("xdd", [P, 2, D])
        E = sb("E", [P, 2, HG, P])
        cbm = sb("cbm", [P, 2, P])
        st = sb("st", [P, GW])
        tmp = sb("tmp", [P, GW])
        sg = sb("sgn", [P, 3, UN])
        nrm = sb("nrm", [P, D])
        y = c.XT[:].rearrange("p a b -> p (a b)").rearrange("p (t d) -> p t d", t=TT)
        (nrm_in, pooled, turned, x_out, x_outd, step, cums, cum_out, decs, e2, unit, masked, mexp, mt, xdok,
         diag, offd, stg, yv, stv, ydsk, yz, ysq, yroot, yn, yt, ya, yd) = signals(
            nc, ctx, "nrm_in s_pooled s_turned s_x_out s_x_outd s_step s_cums s_cum_out s_decs s_e2 s_unit s_masked "
            "s_mexp s_mt s_xd s_diag s_off s_states s_yv s_stv s_ydsk s_yz s_ysq s_yroot s_yn s_yt s_ya s_yd")
        block = ctx.enter_context(nc.Block())
        BT, CT = m_.xbcT[:, KT], m_.xbcT[:, KT + 1]
        yT = lambda kt: m_.xs[:].rearrange("p t d -> p (t d)")[:, kt * SEQ:(kt + 1) * SEQ]
        adt = m_.adt
        heads = lambda x: x.rearrange("p (h w) -> p h w", w=SP_)
        tmp2 = lambda v: m_.xs[:, v // SG, v % SG * GW:(v % SG + 1) * GW]

        @block.sync
        def _(sp):
            sp.dma_start(nrm[:], t["ssd_norm"]).then_inc(nrm_in, 16)
            for b in range(B_MIX, B_MIX + RING):
                c.load_w(sp, b)

        @block.gpsimd
        def _(pool):
            pool.memset(ones[:], 1.0).then_inc(pooled, 1)

            def chunk(cc):
                pool.wait_ge(x_out, 2 * cc + 2)
                pool.wait_ge(x_outd, cc + 1)
                for g in range(SG):
                    cut = slice(g * GW, (g + 1) * GW)
                    pool.tensor_tensor(heads(y[:, cc, cut]), heads(m_.xs[:, cc, cut]), bc(c.rows[:, R_DSK + g * HG:R_DSK + (g + 1) * HG], SP_),
                                       ALU.mult).then_inc(ydsk, 1)
                if cc >= 2:
                    pool.wait_ge(diag, 2 * (cc - 1))
                    pool.wait_ge(stg, 2 * (cc - 1))
                pool.tensor_tensor(heads(xd[:, cc % 2]), heads(m_.xs[:, cc]), bc(m_.dt[:, cc], SP_), ALU.mult).then_inc(xdok, 1)
                pool.wait_ge(xdok, 2 * cc + 1)
                pool.wait_ge(e2, 1)
                pool.tensor_tensor(heads(xdd[:, cc % 2]), heads(xd[:, cc % 2]), bc(dst[:, cc], SP_), ALU.mult).then_inc(xdok, 1)

            chunk(0)
            chunk(1)
            for v in range(UN):
                cc, g = divmod(v, SG)
                yo = y[:, cc, g * GW:(g + 1) * GW]
                pool.wait_ge(yv, v + 1)
                pool.tensor_tensor(yo, yo, m_.zs[:, cc, g * GW:(g + 1) * GW], ALU.mult).then_inc(yz, 1)
                if g == SG - 1 and cc + 2 < TT:
                    chunk(cc + 2)
            pool.wait_ge(ysq, UN)
            pool.tensor_scalar(sg[:, 1], sg[:, 0], 1.0 / GW, EPS, ALU.mult, ALU.add).then_inc(pooled, 1)
            pool.wait_ge(pooled, 2)
            pool.tensor_tensor(sg[:, 2], sg[:, 1], c.half[:, 0:UN], ALU.pow).then_inc(yroot, 1)

        @block.tensor
        def _(pe):
            pe.wait_ge(pooled, 1)
            for cc in range(TT):
                pe.matmul(c.bank[3][:, cc * SH:(cc + 1) * SH], c.tri, adt[:, cc], start=True, stop=True)
                mm = pe.matmul(c.bank[3][:, (TT + cc) * SH:(TT + cc + 1) * SH], ones[:], adt[:, cc], start=True, stop=True)
            mm.then_inc(cums, 1)
            for cc in range(TT):
                if cc >= 1:
                    pe.wait_ge(x_out, 2 * cc)
                    pe.wait_ge(x_outd, cc)
                for j in range(KT + 1):
                    mm = pe.transpose(c.bank[j // 4][:, (j % 4) * P:(j % 4 + 1) * P], m_.xbcT[:, j, cc * P:(cc + 1) * P], c.ident)
                mm.then_inc(turned, 1)
            pe.wait_ge(x_out, 2 * TT)
            pe.wait_ge(x_outd, TT)
            pe.wait_ge(cum_out, 1)

            def decays(v):
                cc, g = divmod(v, SG)
                rows, tok = slice(64 * g, 64 * g + 64), slice(cc * P, (cc + 1) * P)
                if v >= 1:
                    pe.wait_ge(masked, v)
                if v >= 2:
                    pe.wait_ge(unit, v - 1)
                pe.matmul(c.bank[4][:, 0:P], BT[rows, tok], CT[rows, tok], start=True, stop=True)
                for h in range(HG):
                    a1 = adt[:, cc, g * HG + h:g * HG + h + 1].broadcast_to([P, P])
                    mm = pe.matmul(c.bank[2 * (v % 2) + h // 4][:, (h % 4) * P:(h % 4 + 1) * P], a1, c.tri, start=True, stop=True)
                mm.then_inc(cums, 1)

            decays(0)
            decays(1)
            for v in range(UN):
                cc, g = divmod(v, SG)
                rows, tok = slice(64 * g, 64 * g + 64), slice(cc * P, (cc + 1) * P)
                if v + 2 < UN:
                    decays(v + 2)
                if v >= 1:
                    pe.wait_ge(yv, v)
                if cc >= 1:
                    pe.wait_ge(stv, cc)
                    pe.matmul(c.bank[6][:], CT[rows, tok], st[rows, :], start=True, stop=True).then_inc(offd, 1)
                pe.wait_ge(mt, v + 1)
                pe.wait_ge(xdok, 2 * cc + 2)
                for h in range(HG):
                    mm = pe.matmul(c.bank[5][:, h * SP_:(h + 1) * SP_], E[:, v % 2, h],
                                   xd[:, cc % 2, g * GW + h * SP_:g * GW + (h + 1) * SP_], start=True, stop=True)
                mm.then_inc(diag, 1)
                if cc + 1 < TT:
                    pe.matmul(c.bank[7][rows, :], bt[:, cc, rows], xdd[:, cc % 2, g * GW:(g + 1) * GW], start=True, stop=True).then_inc(stg, 1)
            for kt in range(KT):
                if kt == 0:
                    pe.wait_ge(yn, TT)
                if kt >= 4:
                    pe.wait_ge(yd if kt % 2 else ya, kt // 2 - 1)
                for tt in range(TT):
                    mm = pe.transpose(c.bank[kt % 4][:, tt * P:(tt + 1) * P], y[:, tt, kt * P:(kt + 1) * P], c.ident)
                mm.then_inc(yt, 1)

        @block.scalar
        def _(act):
            act.wait_ge(decs, 1)
            act.activation(eacs[:], acs[:, 0], ACT.Exp)
            act.activation(etot[:], acs[:, 1], ACT.Exp)
            act.activation(dst[:], dst[:], ACT.Exp).then_inc(e2, 1)
            for cc in range(TT):
                act.wait_ge(turned, cc + 1)
                act.activation(m_.xs[:, cc, 0:512], c.bank[0][:], ACT.Copy).then_inc(x_out, 1)
                act.activation(bt[:, cc], c.bank[2][:, 0:P], ACT.Copy).then_inc(x_out, 1)
            for i in range(UN + 2):
                if i < UN:
                    act.wait_ge(unit, i + 1)
                    act.activation(E[:, i % 2], E[:, i % 2], ACT.Exp).then_inc(mexp, 1)
                v = i - 2
                if v >= 0:
                    cc, g = divmod(v, SG)
                    act.wait_ge(yz, v + 1)
                    act.activation(tmp2(v), y[:, cc, g * GW:(g + 1) * GW], ACT.Square, accum_out=sg[:, 0, v:v + 1]).then_inc(ysq, 1)
            for kt in range(0, KT, 2):
                act.wait_ge(yt, kt + 1)
                act.activation(yT(kt), c.bank[kt % 4][:], ACT.Copy).then_inc(ya, 1)

        @block.vector
        def _(dve):
            n = [0]

            def link(ins):
                n[0] += 1
                ins.then_inc(step, 1)
                dve.wait_ge(step, n[0])

            dve.wait_ge(cums, 1)
            dve.tensor_copy(acs[:].rearrange("p a t h -> p (a t h)"), c.bank[3][:, 0:2 * TT * SH]).then_inc(cum_out, 1)
            dve.wait_ge(cum_out, 1)
            dve.tensor_tensor(dst[:], acs[:, 1], acs[:, 0], ALU.subtract).then_inc(decs, 1)
            for cc in range(TT):
                dve.wait_ge(turned, cc + 1)
                dve.tensor_copy(m_.xs[:, cc, 512:], c.bank[1][:]).then_inc(x_outd, 1)
            dve.wait_ge(e2, 1)
            for g in range(SG):
                last = dve.tensor_copy(dec[64 * g:64 * g + 64], etot[64 * g:64 * g + 64, :, g * HG:(g + 1) * HG])
            link(last)

            def decays(v):
                cc, g = divmod(v, SG)
                dve.wait_ge(cums, v + 2)
                if v >= 2:
                    dve.wait_ge(diag, v - 1)
                dve.tensor_tensor(cbm[:, v % 2], c.bank[4][:, 0:P], c.tri, ALU.mult).then_inc(masked, 1)
                for h in range(HG):
                    last = dve.tensor_scalar(E[:, v % 2, h], c.bank[2 * (v % 2) + h // 4][:, (h % 4) * P:(h % 4 + 1) * P],
                                             acs[:, 0, cc, g * HG + h:g * HG + h + 1], 0.0, ALU.subtract, ALU.min)
                last.then_inc(unit, 1)

            decays(0)
            for v in range(UN):
                cc, g = divmod(v, SG)
                if v + 1 < UN:
                    decays(v + 1)
                dve.wait_ge(mexp, v + 1)
                dve.tensor_tensor(E[:, v % 2], E[:, v % 2], mid(cbm[:, v % 2], HG), ALU.mult).then_inc(mt, 1)
                yo = y[:, cc, g * GW:(g + 1) * GW]
                dve.wait_ge(ydsk, v + 1)
                if cc >= 1:
                    dve.wait_ge(offd, 2 * (cc - 1) + g + 1)
                    link(dve.tensor_tensor(heads(tmp[:]), heads(c.bank[6][:]), bc(eacs[:, cc, g * HG:(g + 1) * HG], SP_), ALU.mult))
                    link(dve.tensor_tensor(yo, yo, tmp[:], ALU.add))
                dve.wait_ge(diag, v + 1)
                dve.tensor_tensor(yo, c.bank[5][:], yo, ALU.add).then_inc(yv, 1)
                if g == SG - 1 and cc + 1 < TT:
                    dve.wait_ge(stg, 2 * cc + 2)
                    if cc == 0:
                        dve.tensor_copy(st[:], c.bank[7][:]).then_inc(stv, 1)
                    else:
                        st3 = st[:].rearrange("p (h w) -> p h w", w=SP_)
                        dve.wait_ge(offd, 2 * cc)
                        dve.wait_ge(stv, cc)
                        link(dve.tensor_tensor(st3, st3, bc(dec[:, cc], SP_), ALU.mult))
                        dve.tensor_tensor(st[:], c.bank[7][:], st[:], ALU.add).then_inc(stv, 1)
            dve.wait_ge(yroot, 1)
            dve.wait_ge(nrm_in, 16)
            for v in range(UN):
                cc, g = divmod(v, SG)
                cut = slice(g * GW, (g + 1) * GW)
                last = dve.scalar_tensor_tensor(out=y[:, cc, cut], in0=y[:, cc, cut], scalar=sg[:, 2, v:v + 1], in1=nrm[:, cut],
                                                op0=ALU.mult, op1=ALU.mult)
                if g == SG - 1:
                    last.then_inc(yn, 1)
            for kt in range(1, KT, 2):
                dve.wait_ge(yt, kt + 1)
                dve.tensor_copy(yT(kt), c.bank[kt % 4][:]).then_inc(yd, 1)


def phase_mixer_out(c, m_):
    nc, t = c.nc, c.t
    with ExitStack() as ctx:
        pT = ctx.enter_context(nc.sbuf_tensor("pT_sb", [P, PLE // P, SEQ], F32))
        npost = ctx.enter_context(nc.sbuf_tensor("npost", [P, D], F32))
        gt = ctx.enter_context(nc.sbuf_tensor("gt", [P, 2, 512], F32))
        (in0, in1, grp, out0, s1, s2, pg, gg, gsig, xo, stored, step) = signals(
            nc, ctx, "o_in0 o_in1 o_grp o_out o_s1 o_s2 o_pg o_gg o_gsig o_xo o_stored o_step")
        block = ctx.enter_context(nc.Block())
        yssdT = m_.xs[:].rearrange("p t d -> p (t d)").rearrange("p (k s) -> p k s", k=KT)
        MX = m_.zs
        junk = m_.xbcT[:, 0:KT].rearrange("p a b -> p (a b)").rearrange("p (t d) -> p t d", t=TT)
        GR = 2 * TT

        @block.sync
        def _(sp):
            sp.dma_start(pT[:], t["pT"]).then_inc(in0, 16)
            sp.dma_start(npost[:], t["norm_post"]).then_inc(in1, 16)
            for b in range(B_MIX, NB - RING):
                nh, kb = divmod(b - B_MIX, 2)
                sp.wait_ge(grp, nh * (TT + 1) + (TT + 1 if kb else 1))
                c.load_w(sp, b + RING)
            out = t["out"].rearrange("(t p) d -> p t d", p=P)
            for g in range(GR):
                nh, tt = divmod(g, TT)
                sp.wait_ge(xo, g + 1)
                sp.dma_start(out[:, tt, nh * 512:(nh + 1) * 512], c.X[:, tt, nh * 512:(nh + 1) * 512]).then_inc(stored, 16)
            sp.wait_ge(stored, 16 * GR)

        @block.tensor
        def _(pe):
            for nh in range(2):
                for kb in range(2):
                    c.wait_w(pe, B_MIX + 2 * nh + kb)
                    w, src = c.w(B_MIX + 2 * nh + kb, KT * 512, 512), (yssdT, m_.yscT)[kb]
                    for tt in range(TT):
                        for k in range(KT):
                            mm = pe.matmul(c.bank[4 * nh + tt][:], src[:, k, tt * P:(tt + 1) * P], w[:, k],
                                           start=kb == 0 and k == 0, stop=kb == 1 and k == KT - 1)
                        if kb or tt == TT - 1:
                            mm.then_inc(grp, 1)
            pe.wait_ge(out0, GR)
            pe.wait_ge(in0, 16)
            c.wait_w(pe, B_PLE)
            ple = c.w(B_PLE, PLE // P * D, D)

            def embed(g):
                nh, tt = divmod(g, TT)
                for k in range(PLE // P):
                    mm = pe.matmul(c.bank[4 + g % 4][:], pT[:, k, tt * P:(tt + 1) * P], ple[:, k, nh * 512:(nh + 1) * 512],
                                   start=k == 0, stop=k == PLE // P - 1)
                mm.then_inc(pg, 1)

            for g in range(4):
                embed(g)
            transposes_pe(pe, c, c.X, T_POST)
            transposed_pe(pe, c, T_POST)
            for g in range(GR):
                nh, tt = divmod(g, TT)
                if tt == 0:
                    c.wait_w(pe, B_GATE + nh)
                if g >= 4:
                    pe.wait_ge(xo, g - 3)
                    pe.wait_ge(gsig, g - 3)
                tok = slice(tt * P, (tt + 1) * P)
                w = c.w(B_GATE + nh, KT * 512, 512)
                for k in range(KT):
                    mm = pe.matmul(c.bank[g % 4][:], c.XT[:, k, tok], w[:, k], start=k == 0, stop=k == KT - 1)
                mm.then_inc(gg, 1)
                if g >= 4:
                    embed(g)

        @block.scalar
        def _(act):
            norm_sums(act, c, MX, junk, out0, TT)
            gains_act(act, c, None, T_POST)
            for g in range(GR):
                act.wait_ge(gg, g + 1)
                if g >= 2:
                    act.wait_ge(xo, g - 1)
                act.activation(gt[:, g % 2], c.bank[g % 4][:], ACT.Sigmoid).then_inc(gsig, 1)

        @block.gpsimd
        def _(pool):
            norm_rsqrt(pool, c, N_POST)

        @block.vector
        def _(dve):
            for g in range(GR):
                nh, tt = divmod(g, TT)
                dve.wait_ge(grp, nh * (TT + 1) + tt + 2)
                dve.tensor_copy(MX[:, tt, nh * 512:(nh + 1) * 512], c.bank[g][:]).then_inc(out0, 1)
            dve.wait_ge(c.rooted, N_POST + 1)
            dve.wait_ge(in1, 16)
            for tt in range(TT):
                dve.tensor_scalar(MX[:, tt], MX[:, tt], c.rn[:, tt:tt + 1], None, ALU.mult).then_inc(s1, 1)
            for tt in range(TT):
                dve.wait_ge(s1, tt + 1)
                dve.tensor_tensor(MX[:, tt], MX[:, tt], npost[:], ALU.mult).then_inc(s2, 1)
            for tt in range(TT):
                dve.wait_ge(s2, tt + 1)
                dve.tensor_tensor(c.X[:, tt], c.X[:, tt], MX[:, tt], ALU.add).then_inc(c.scaled, 1)
            gains_dve(dve, c, None, T_POST)
            for g in range(GR):
                nh, tt = divmod(g, TT)
                xs = c.X[:, tt, nh * 512:(nh + 1) * 512]
                dve.wait_ge(pg, g + 1)
                dve.wait_ge(gsig, g + 1)
                dve.tensor_tensor(gt[:, g % 2], c.bank[4 + g % 4][:], gt[:, g % 2], ALU.mult).then_inc(step, 1)
                dve.wait_ge(step, g + 1)
                dve.tensor_tensor(xs, xs, gt[:, g % 2], ALU.add).then_inc(xo, 1)


class Attention:
    def __init__(self, c, ctx):
        self.y = ctx.enter_context(c.nc.sbuf_tensor("y", [P, TT, 2 * ATT_W], F32))

    def inputs(self, c, ctx):
        sb = lambda name, shape: ctx.enter_context(c.nc.sbuf_tensor(name, shape, F32))
        self.qz = sb("qz", [P, HEADS, SEQ])
        self.kT = sb("kT", [P, HEADS // 2, SEQ])
        self.qzb = sb("qzb", [P, HEADS, SEQ])
        self.va = c.ur[:].rearrange("p r (a w) -> p (r a) w", w=ATT_W)
        self.kTb = c.ar[:, 0]
        self.vb = c.ar[:, 1].rearrange("p (t w) -> p t w", t=TT)


def build(nc, t, upto=99):
    with ExitStack() as ctx:
        c = Core(nc, ctx, t)
        with ExitStack() as tmp:
            ijg = tmp.enter_context(nc.sbuf_tensor("ijg", [P, 3, SEQ], F32))
            early = Early(c, tmp)
            with ExitStack() as half:
                c.ring(half, "W1")
                with ExitStack() as att:
                    a = Attention(c, att)
                    with ExitStack() as inputs:
                        a.inputs(c, inputs)
                        phase_project(c, a)
                        if upto >= 2:
                            phase_attend(c, a)
                    if upto >= 3:
                        phase_merge(c, a)
                if upto >= 4:
                    qT = half.enter_context(nc.sbuf_tensor("qT", [P, 2 * PH, SEQ], F32))
                    phase_query(c, qT)
                    phase_choose(c, ijg, early, qT)
            if upto >= 5:
                phase_gates(c, ijg, early)
        if upto >= 6:
            phase_experts(c)
        with ExitStack() as mix:
            m_ = Mixer(nc, mix)
            with ExitStack() as first:
                raw = Raw(c, first)
                if upto >= 7:
                    phase_between(c, raw)
                if upto >= 8:
                    phase_mixer_in(c, m_, raw)
            if upto >= 9:
                c.ring(mix, "W2")
                if upto >= 9:
                    phase_scan(c, m_)
                if upto >= 10:
                    phase_mixer_out(c, m_)
        if upto < 10:
            dumped = ctx.enter_context(nc.semaphore("dumped"))
            with nc.Block() as block:
                @block.sync
                def _(sp):
                    sp.dma_start(t["out"].rearrange("(t p) d -> p t d", p=P), c.X[:] if upto != 1 else c.XT[:].rearrange("p a b -> p (a b)").rearrange("p (t d) -> p t d", t=TT)).then_inc(dumped, 16)
                    sp.wait_ge(dumped, 16)



def _rows(w, cols, k=None):
    w = w[:, cols]
    return w.reshape(w.shape[0] // P, P, w.shape[1]).transpose(1, 0, 2)


def _tables():
    tab = np.zeros((P, NTAB), np.float32)
    tab[:, T_ID:T_ID + P] = np.eye(P)
    tab[:, T_TRI:T_TRI + P] = np.triu(np.ones((P, P)))
    tab[:, T_IOTA:T_IOTA + P] = np.arange(P)
    nf = DH // 4
    inv = (np.float32(ROPE_THETA) ** (-np.arange(nf, dtype=np.float32) / np.float32(nf))).astype(np.float32)
    tok = np.arange(SEQ)
    for s, pos in enumerate((tok // GRID_W, tok % GRID_W)):
        ang = pos.astype(np.float32)[:, None] * inv[None, :]
        co, si = np.cos(ang).astype(np.float32), np.sin(ang).astype(np.float32)
        for f in range(2):
            at = s * 2 * nf + f * nf
            for tt in range(TT):
                rows = slice(tt * P, (tt + 1) * P)
                tab[:, T_COS + tt * DH + at:T_COS + tt * DH + at + nf] = co[rows]
                tab[:, T_SIN + tt * DH + at:T_SIN + tt * DH + at + nf] = si[rows] * (1 if f else -1)
    return tab


def _bias(rpb):
    q = np.arange(GRID_W)
    start = np.clip(q - WIN_W // 2, 0, GRID_W - WIN_W)
    k = np.arange(GRID_W)
    inside = (k[None] >= start[:, None]) & (k[None] < start[:, None] + WIN_W)
    dc = np.clip(k[None] - q[:, None], -(WIN_W - 1), WIN_W - 1) + WIN_W - 1
    out = np.full((HEADS, 2, GRID_W, BIAS_ROWS, GRID_W), NEG, np.float32)
    for par in range(2):
        for j in range(BIAS_ROWS):
            dr = j - par
            if 0 <= dr < 2 * WIN_H - 1:
                out[:, par, :, j, :] = np.where(inside[None], rpb[:, dr][:, dc], np.float32(NEG))
    return out.reshape(HEADS, P, BIAS_ROWS * GRID_W)


def pack(x, norm1_g, w_in, na_rpb, gqa_q_norm_g, gqa_k_norm_g, w_proj_a, w_proj_b, w_out, norm2_g,
         peer_w_q, peer_sub_keys, peer_u, peer_v, norm_f_g, p_2, norm_pre_2, norm_post_2, w_in_2,
         ssd_conv_w_2, ssd_conv_b_2, dt_bias_2, a_log_2, d_skip_2, ssd_norm_2, sc_conv_w_2, w_out_2,
         w_ple_gate_2, w_ple_proj_2):
    w_in, w2 = w_in[0], w_in_2[0]
    blocks = np.zeros((NB, P, WBLK), np.float32)

    blocks_in = np.zeros((NI, P, WIN), np.float32)

    def put(b, *parts, to=blocks):
        at = 0
        for w in parts:
            n = w.shape[1] * w.shape[2]
            to[b, :, at:at + n] = w.reshape(P, n)
            at += n

    put_in = lambda b, *parts: put(b, *parts, to=blocks_in)

    cut = lambda a, n: slice(a, a + n)
    for i, b in enumerate((B_QA, B_KA, B_VA, B_QB)):
        put(b, _rows(w_in, cut(512 * i, 512)))
    put(B_KVB, _rows(w_in, cut(2048, 256)))
    for m in range(KT):
        put(B_MERGE + m, _rows(w_in, cut(2304 + P * m, P)), _rows(w_in, cut(3328 + P * m, P)),
            _rows(w_proj_a[0], cut(P * m, P)), _rows(w_proj_b[0], cut(P * m, P)))
        s0 = (D + 2 * SG * NS) + SH + D
        for i, js in enumerate(((2, 0), (1, 3))):
            put_in(I_SC + 2 * m + i, *[_rows(w2, cut(s0 + D * j + P * m, P)) for j in js])
    for b in range(2):
        put(B_OUT + b, _rows(w_out[0], cut(512 * b, 512)))
        put(B_GATE + b, _rows(w_ple_gate_2[0], cut(512 * b, 512)))
        for k in range(2):
            put(B_MIX + 2 * b + k, _rows(w_out_2[0][D * k:D * (k + 1)], cut(512 * b, 512)))
    for b in range(4):
        put(B_PQ + b, _rows(peer_w_q[0], cut(512 * b, 512)))
    put(B_KEYS, peer_sub_keys[0].reshape(2 * PH, PK, P).transpose(2, 0, 1))
    for b in range(I_DT):
        put_in(I_XBC + b, _rows(w2, cut(2 * P * b, 2 * P)))
    put_in(I_DT, _rows(w2, cut(D + 2 * SG * NS, SH)))
    for b in range(D // ZC):
        put_in(I_Z + b, _rows(w2, cut(D + 2 * SG * NS + SH + ZC * b, ZC)))
    put(B_PLE, _rows(w_ple_proj_2[0], cut(0, D)))

    col = lambda v: v.reshape(-1, P).T
    cols = np.zeros((P, NCOL), np.float32)
    for at, v in ((C_G1, norm1_g[0]), (C_G2, norm2_g[0]), (C_GPRE, norm_pre_2[0]), (C_CB, ssd_conv_b_2[0])):
        cols[:, at:at + v.size // P] = col(v)
    cols[:, C_CW:C_CB] = ssd_conv_w_2[0].reshape(CONV_W, XBC_TILES, P).transpose(2, 1, 0).reshape(P, -1)
    cols[:, C_SW:NCOL] = sc_conv_w_2[0].reshape(SC_W, KT, P).transpose(2, 1, 0).reshape(P, -1)
    row = np.concatenate([np.tile(gqa_q_norm_g[0], HEADS), np.tile(gqa_k_norm_g[0], KV_HEADS), dt_bias_2[0], a_log_2[0], d_skip_2[0]])
    wide = lambda v: np.ascontiguousarray(np.broadcast_to(v.reshape(1, -1), (P, v.size)))
    return {
        "x": x[0], "tab": _tables(), "cols": cols, "rows": wide(row), "bias": _bias(na_rpb[0]),
        "w_stream": blocks, "w_mixer": blocks_in,
        "u": peer_u[0].reshape(PK, P, KT, P).transpose(0, 3, 2, 1),
        "v": peer_v[0].reshape(PK, P, D),
        "norm_f": wide(norm_f_g), "norm_post": wide(norm_post_2[0]), "ssd_norm": wide(ssd_norm_2[0]),
        "pT": p_2[0, 0].T.reshape(PLE // P, P, SEQ).transpose(1, 0, 2),
    }


def kernel(**inputs):
    import concourse.bacc as bacc
    from concourse.bass_utils import run_bass_kernel_spmd

    nc = bacc.Bacc("TRN2", target_bir_lowering=False, num_devices=1)
    arrays, tensors = {}, {}
    for name, a in pack(**{k: np.asarray(v) for k, v in inputs.items()}).items():
        a = np.ascontiguousarray(a)
        arrays[f"in_{name}"] = a
        tensors[name] = nc.dram_tensor(f"in_{name}", a.shape, mybir.dt.from_np(a.dtype), kind="ExternalInput").ap()
    tensors["early"] = nc.dram_tensor("early", (EARLY, P, SEQ), F32).ap()
    tensors["gates"] = nc.dram_tensor("gates", (PK, PK, SEQ), F32).ap()
    tensors["out"] = nc.dram_tensor("out_x", (SEQ, D), F32, kind="ExternalOutput").ap()
    build(nc, tensors)
    r = run_bass_kernel_spmd(nc, [arrays], core_ids=[0])
    return r.results[0]["out_x"].reshape(1, SEQ, D)
```
